# Optimizing a Trainium2 kernel written in Bass

```python
import math
import jax, jax.numpy as jnp
from jax import lax
import numpy as np

D_MODEL = 1024
BATCH = 1
SEQ = 1024
DEPTH = 1
DEC_BATCH = 8
DEC_SEQ = 1
PAST_LEN = 1024
PAGE_SIZE = 128

DA_HEADS = 4
DA_QK_DIM = 64
DA_V_DIM = 2 * DA_QK_DIM
FX_HEADS = 8
FX_DIM = 64
DA_Q_COLS = DA_HEADS * 2 * DA_QK_DIM
DA_K_COLS = DA_HEADS * 2 * DA_QK_DIM
DA_V_COLS = DA_HEADS * DA_V_DIM
FX_COLS = FX_HEADS * FX_DIM
D_IN = DA_Q_COLS + DA_K_COLS + DA_V_COLS + 3 * FX_COLS + FX_HEADS
MIX_WIDTH = DA_HEADS * DA_V_DIM + FX_HEADS * FX_DIM
D_FF = 2816
CONV_W = 3
ROPE_THETA = 10000.0
Q_BLOCK = 128
NORM_EPS = 1e-6

kernel_name = "hymba_diff_fox_convffn_step"

def _rmsnorm(x, g):
    x32 = x.astype(jnp.float32)
    y = x32 * lax.rsqrt(jnp.mean(x32 * x32, axis=-1, keepdims=True) + NORM_EPS)
    return (y * g.astype(jnp.float32)).astype(x.dtype)

def _rope(x, pos):
    half = x.shape[-1] // 2
    inv = ROPE_THETA ** (-jnp.arange(half, dtype=jnp.float32) / half)
    ang = pos.astype(jnp.float32)[:, None] * inv[None, :]
    cos = jnp.cos(ang)[:, None, :]
    sin = jnp.sin(ang)[:, None, :]
    x32 = x.astype(jnp.float32)
    x1, x2 = x32[..., :half], x32[..., half:]
    return jnp.concatenate([x1 * cos - x2 * sin, x2 * cos + x1 * sin], axis=-1).astype(x.dtype)

def _project(h, w_in, b_f, pos):
    B, S, _ = h.shape
    z = h @ w_in
    o = 0
    qa = z[..., o:o + DA_Q_COLS].reshape(B, S, DA_HEADS, 2, DA_QK_DIM); o += DA_Q_COLS
    ka = z[..., o:o + DA_K_COLS].reshape(B, S, DA_HEADS, 2, DA_QK_DIM); o += DA_K_COLS
    va = z[..., o:o + DA_V_COLS].reshape(B, S, DA_HEADS, DA_V_DIM); o += DA_V_COLS
    qf = z[..., o:o + FX_COLS].reshape(B, S, FX_HEADS, FX_DIM); o += FX_COLS
    kf = z[..., o:o + FX_COLS].reshape(B, S, FX_HEADS, FX_DIM); o += FX_COLS
    vf = z[..., o:o + FX_COLS].reshape(B, S, FX_HEADS, FX_DIM); o += FX_COLS
    f_logit = z[..., o:o + FX_HEADS]
    q1 = _rope(qa[..., 0, :], pos)
    q2 = _rope(qa[..., 1, :], pos)
    ka_rot = jnp.concatenate([_rope(ka[..., 0, :], pos), _rope(ka[..., 1, :], pos)], axis=-1)
    logf = jax.nn.log_sigmoid(f_logit.astype(jnp.float32) + b_f.astype(jnp.float32))
    return q1, q2, ka_rot, va, qf, kf, vf, logf

def _causal_mask(qpos, kpos):
    return kpos[None, :] <= qpos[:, None]

def _diff_attend(q1, q2, k1, k2, v, qpos, kpos, lam):
    scale = DA_QK_DIM ** -0.5
    mask = _causal_mask(qpos, kpos)

    def probs(q, k):
        s = jnp.einsum('bqhd,bkhd->bhqk', q, k, preferred_element_type=jnp.float32) * scale
        s = jnp.where(mask, s, jnp.finfo(jnp.float32).min)
        return jax.nn.softmax(s, axis=-1)

    a = probs(q1, k1) - lam * probs(q2, k2)
    return jnp.einsum('bhqk,bkhe->bqhe', a.astype(v.dtype), v)

def _fox_attend(q, k, v, cq, ck, qpos, kpos):
    scale = FX_DIM ** -0.5
    mask = _causal_mask(qpos, kpos)
    s = jnp.einsum('bqhd,bkhd->bhqk', q, k, preferred_element_type=jnp.float32) * scale
    bias = jnp.transpose(cq, (0, 2, 1))[..., :, None] - jnp.transpose(ck, (0, 2, 1))[..., None, :]
    s = jnp.where(mask, s + bias, jnp.finfo(jnp.float32).min)
    p = jax.nn.softmax(s, axis=-1)
    return jnp.einsum('bhqk,bkhe->bqhe', p.astype(v.dtype), v)

def _prompt_attention(q1, q2, ka, va, qf, kf, vf, cf, lam):
    B, S = q1.shape[0], q1.shape[1]
    n_blocks = S // Q_BLOCK
    kpos = jnp.arange(S)
    k1, k2 = ka[..., :DA_QK_DIM], ka[..., DA_QK_DIM:]

    def block(i):
        s0 = i * Q_BLOCK
        sl = lambda a: lax.dynamic_slice_in_dim(a, s0, Q_BLOCK, axis=1)
        qpos = s0 + jnp.arange(Q_BLOCK)
        oa = _diff_attend(sl(q1), sl(q2), k1, k2, va, qpos, kpos, lam)
        of = _fox_attend(sl(qf), kf, vf, sl(cf), cf, qpos, kpos)
        return oa, of

    oa, of = lax.map(block, jnp.arange(n_blocks))
    unblock = lambda o: jnp.moveaxis(o, 0, 1).reshape(B, S, o.shape[3], o.shape[4])
    return unblock(oa), unblock(of)

def _merge(oa, of, subln_g, lam_init, w_o):
    B, S = oa.shape[0], oa.shape[1]
    oa = _rmsnorm(oa, subln_g) * (1.0 - lam_init)
    o = jnp.concatenate([oa.reshape(B, S, -1), of.reshape(B, S, -1)], axis=-1)
    return o @ w_o

def _conv_ffn(x, prev, pre_g, w_gate, w_up, conv_w, conv_b, w_down, post_g):
    h = _rmsnorm(x, pre_g)
    g = h @ w_gate
    u = h @ w_up
    S = g.shape[1]
    gp = jnp.concatenate([prev.astype(g.dtype), g], axis=1)
    c = conv_b
    for j in range(CONV_W):
        c = c + conv_w[j] * gp[:, j:j + S]
    a = jax.nn.gelu(c, approximate=True) * u
    out = a @ w_down
    return x + _rmsnorm(out, post_g), gp[:, -(CONV_W - 1):]

def setup_inputs(seed: int = 0) -> dict:
    key = jax.random.key(seed)
    ks = iter(jax.random.split(key, 40))
    f32 = jnp.float32
    nrm = lambda shape, s=1.0: jax.random.normal(next(ks), shape, f32) * s
    n_pages = PAST_LEN // PAGE_SIZE
    n_pool = (DEC_BATCH * n_pages * 5) // 4
    perm = jax.random.permutation(next(ks), n_pool)[:DEC_BATCH * n_pages]
    page_table = perm.reshape(DEC_BATCH, n_pages).astype(jnp.int32)
    return {
        "x_prompt": nrm((BATCH, SEQ, D_MODEL)),
        "x_sample": nrm((DEC_BATCH, DEC_SEQ, D_MODEL)),
        "cache_diff_k": nrm((DEPTH, n_pool, PAGE_SIZE, DA_HEADS, 2 * DA_QK_DIM)),
        "cache_diff_v": nrm((DEPTH, n_pool, PAGE_SIZE, DA_HEADS, DA_V_DIM)),
        "cache_fox_k": nrm((DEPTH, n_pool, PAGE_SIZE, FX_HEADS, FX_DIM)),
        "cache_fox_v": nrm((DEPTH, n_pool, PAGE_SIZE, FX_HEADS, FX_DIM)),
        "cache_fox_logf": jax.nn.log_sigmoid(3.0 + nrm((DEPTH, n_pool, PAGE_SIZE, FX_HEADS))),
        "state_ffn_conv": nrm((DEPTH, DEC_BATCH, CONV_W - 1, D_FF)),
        "page_table": page_table,
        "attn_pre_g": 1.0 + nrm((DEPTH, D_MODEL), 0.02),
        "w_in": nrm((DEPTH, D_MODEL, D_IN), D_MODEL ** -0.5),
        "b_f": 3.0 + nrm((DEPTH, FX_HEADS), 0.1),
        "lam_q1": nrm((DEPTH, DA_QK_DIM), 0.1),
        "lam_k1": nrm((DEPTH, DA_QK_DIM), 0.1),
        "lam_q2": nrm((DEPTH, DA_QK_DIM), 0.1),
        "lam_k2": nrm((DEPTH, DA_QK_DIM), 0.1),
        "subln_g": 1.0 + nrm((DEPTH, DA_V_DIM), 0.02),
        "w_o": nrm((DEPTH, MIX_WIDTH, D_MODEL), MIX_WIDTH ** -0.5),
        "attn_post_g": 1.0 + nrm((DEPTH, D_MODEL), 0.02),
        "ffn_pre_g": 1.0 + nrm((DEPTH, D_MODEL), 0.02),
        "w_gate": nrm((DEPTH, D_MODEL, D_FF), D_MODEL ** -0.5),
        "w_up": nrm((DEPTH, D_MODEL, D_FF), D_MODEL ** -0.5),
        "conv_w": nrm((DEPTH, CONV_W, D_FF), CONV_W ** -0.5),
        "conv_b": nrm((DEPTH, D_FF), 0.02),
        "w_down": nrm((DEPTH, D_FF, D_MODEL), D_FF ** -0.5),
        "ffn_post_g": 1.0 + nrm((DEPTH, D_MODEL), 0.02),
    }

def reference(x_prompt, x_sample, cache_diff_k, cache_diff_v, cache_fox_k, cache_fox_v,
              cache_fox_logf, state_ffn_conv, page_table, attn_pre_g, w_in, b_f,
              lam_q1, lam_k1, lam_q2, lam_k2, subln_g, w_o, attn_post_g, ffn_pre_g,
              w_gate, w_up, conv_w, conv_b, w_down, ffn_post_g):
    f32 = jnp.float32
    B, S = x_prompt.shape[0], x_prompt.shape[1]
    DB, DS = x_sample.shape[0], x_sample.shape[1]
    past_len = page_table.shape[1] * PAGE_SIZE
    pos_p = jnp.arange(S)
    pos_s = past_len + jnp.arange(DS)
    kpos_s = jnp.arange(past_len + DS)

    xp, xs = x_prompt, x_sample
    pk_a, pv_a, pk_f, pv_f, plf, pconv = [], [], [], [], [], []
    sk_a, sv_a, sk_f, sv_f, slf, sconv = [], [], [], [], [], []

    for l in range(DEPTH):
        lam_init = 0.8 - 0.6 * math.exp(-0.3 * l)
        lam = (jnp.exp(jnp.sum(lam_q1[l].astype(f32) * lam_k1[l].astype(f32)))
               - jnp.exp(jnp.sum(lam_q2[l].astype(f32) * lam_k2[l].astype(f32))) + lam_init)

        h = _rmsnorm(xp, attn_pre_g[l])
        q1, q2, ka, va, qf, kf, vf, logf = _project(h, w_in[l], b_f[l], pos_p)
        cf = jnp.cumsum(logf, axis=1)
        oa, of = _prompt_attention(q1, q2, ka, va, qf, kf, vf, cf, lam)
        xp = xp + _rmsnorm(_merge(oa, of, subln_g[l], lam_init, w_o[l]), attn_post_g[l])
        prev0 = jnp.zeros((B, CONV_W - 1, D_FF), xp.dtype)
        xp, conv_p = _conv_ffn(xp, prev0, ffn_pre_g[l], w_gate[l], w_up[l], conv_w[l],
                               conv_b[l], w_down[l], ffn_post_g[l])
        pk_a.append(ka); pv_a.append(va); pk_f.append(kf); pv_f.append(vf)
        plf.append(logf); pconv.append(conv_p)

        h = _rmsnorm(xs, attn_pre_g[l])
        q1s, q2s, kas, vas, qfs, kfs, vfs, logfs = _project(h, w_in[l], b_f[l], pos_s)
        gather = lambda c: c[l][page_table].reshape((DB, past_len) + c.shape[3:])
        ka_all = jnp.concatenate([gather(cache_diff_k).astype(kas.dtype), kas], axis=1)
        va_all = jnp.concatenate([gather(cache_diff_v).astype(vas.dtype), vas], axis=1)
        kf_all = jnp.concatenate([gather(cache_fox_k).astype(kfs.dtype), kfs], axis=1)
        vf_all = jnp.concatenate([gather(cache_fox_v).astype(vfs.dtype), vfs], axis=1)
        lf_all = jnp.concatenate([gather(cache_fox_logf).astype(f32), logfs], axis=1)
        cf_all = jnp.cumsum(lf_all, axis=1)
        oa_s = _diff_attend(q1s, q2s, ka_all[..., :DA_QK_DIM], ka_all[..., DA_QK_DIM:],
                            va_all, pos_s, kpos_s, lam)
        of_s = _fox_attend(qfs, kf_all, vf_all, cf_all[:, past_len:], cf_all, pos_s, kpos_s)
        xs = xs + _rmsnorm(_merge(oa_s, of_s, subln_g[l], lam_init, w_o[l]), attn_post_g[l])
        xs, conv_s = _conv_ffn(xs, state_ffn_conv[l], ffn_pre_g[l], w_gate[l], w_up[l],
                               conv_w[l], conv_b[l], w_down[l], ffn_post_g[l])
        sk_a.append(kas); sv_a.append(vas); sk_f.append(kfs); sv_f.append(vfs)
        slf.append(logfs); sconv.append(conv_s)

    return (xp, xs,
            jnp.stack(pk_a), jnp.stack(pv_a), jnp.stack(pk_f), jnp.stack(pv_f),
            jnp.stack(plf), jnp.stack(pconv),
            jnp.stack(sk_a), jnp.stack(sv_a), jnp.stack(sk_f), jnp.stack(sv_f),
            jnp.stack(slf), jnp.stack(sconv))


_drawn_inputs = setup_inputs


def setup_inputs(seed=0):
    import zlib

    import numpy as np

    out = dict(_drawn_inputs(seed))
    spreads = {}
    factors = {'lam_q2': 8.0,
     'subln_g': 3.59,
     'attn_post_g': 3.51,
     'ffn_pre_g': 2.781,
     'conv_b': 5.025,
     'ffn_post_g': 16.997,
     'cache_fox_logf': 2.99}
    for name, (base, spread) in spreads.items():
        noise = np.random.default_rng([zlib.crc32(name.encode()), seed]).standard_normal(out[name].shape)
        drawn = base * np.exp(spread * noise) if base else spread * noise
        out[name] = __import__('jax').numpy.asarray(drawn.astype(out[name].dtype))
    for name, factor in factors.items():
        out[name] = (out[name] * factor).astype(out[name].dtype)
    return out
```

```python
import math
from contextlib import ExitStack

import numpy as np
import concourse.bass as bass
from concourse import mybir

F32 = mybir.dt.float32
F32R = mybir.dt.float32r
BF16 = mybir.dt.bfloat16
I32 = mybir.dt.int32
ALU = mybir.AluOpType
ACT = mybir.ActivationFunctionType
AX = mybir.AxisListType.X

P = 128
D = 1024
KC = D // P
SEQ = 1024
NT = SEQ // P
DB = 8
TOK = SEQ + DB
THIRD = TOK // 3
PAGES = 8
PAST = PAGES * P
NPOOL = DB * PAGES * 5 // 4
MAPS = 8
HD = 64
GRP = MAPS * HD
FF = 2816
FC = FF // P
EPS = 1e-6
LAM_INIT = 0.8 - 0.6 * math.exp(0.0)
SCALE = HD ** -0.5
NEG = -1e37
THETA = 10000.0
LO_ROW = 32

QA, KA, QF, KF, VA, VF = range(6)
BLOCK_COL = {QA: 0, KA: 512, VA: 1024, QF: 1536, KF: 2048, VF: 2560}
ORDER = [QA, KA, QF, KF, VA, VF]
F_COL = 3072

C_ID, C_MASK, C_SUFFIX, C_ONES, C_HM, C_SELB, C_SIGN, C_ROPE, C_SELH = (
    0, 128, 256, 384, 512, 1024, 1032, 1040, 1040 + 9 * P)
C_END = C_SELH + MAPS * P


def shape_constants():
    c = np.zeros((P, C_END), np.float32)
    i = np.arange(P)
    c[:, C_ID:C_ID + P] = np.eye(P)
    c[:, C_MASK:C_MASK + P] = np.where(i[None, :] <= i[:, None], 0.0, NEG)
    c[:, C_SUFFIX:C_SUFFIX + P] = i[:, None] > i[None, :]
    c[:, C_ONES:C_ONES + P] = 1.0
    col = np.arange(GRP)
    m = i % MAPS
    diff = i < HD
    c[:, C_HM:C_HM + GRP] = np.where(diff[:, None], (col[None, :] // P) == (m[:, None] // 2),
                                     (col[None, :] // HD) == m[:, None])
    c[:, C_SIGN] = ~diff | (m % 2 == 0)
    c[:, C_SIGN + 1] = diff & (m % 2 == 1)
    c[:, C_SELB:C_SELB + DB] = (i[:, None] % HD // MAPS) == np.arange(DB)[None, :]
    half = HD // 2
    inv = np.float32(THETA) ** (-np.arange(half, dtype=np.float32) / np.float32(half))
    for t in range(NT + 1):
        pos = (t * P + i if t < NT else np.full(P, PAST)).astype(np.float32)
        ang = (pos[:, None] * inv[None, :]).astype(np.float32).astype(np.float64)
        at = C_ROPE + t * P
        c[:, at:at + half] = c[:, at + half:at + HD] = np.cos(ang)
        c[:, at + HD:at + HD + half] = -np.sin(ang)
        c[:, at + HD + half:at + 2 * HD] = np.sin(ang)
    for h in range(MAPS):
        c[h, C_SELH + h * P:C_SELH + (h + 1) * P] = 1.0
        c[LO_ROW + h, C_SELH + h * P:C_SELH + (h + 1) * P] = 1.0
    return c


class Place:

    def __init__(self, nc, base):
        self.nc, self.base, self.n, self.made = nc, base, 0, {}

    def at(self, off, name, cols, dt=F32):
        assert off + (2 if dt == BF16 else 4) * cols <= 212800, (name, off + 4 * cols)
        key = (off, name, cols, dt)
        if key not in self.made:
            self.made[key] = self._make(off, name, cols, dt)
        return self.made[key]

    def _make(self, off, name, cols, dt):
        self.n += 1
        return self.nc.alloc_sbuf_tensor_at(f"{name}_{self.n}", [P, cols], dt, offset=self.base + off)


def view(tensor, **dims):
    names = list(dims)
    return tensor[:, :].rearrange("p (%s) -> p %s" % (" ".join(names), " ".join(names)),
                             **{n: dims[n] for n in names[:-1]})


HT_BYTES = 4 * KC * TOK
R_HI, R_LO = 0, HT_BYTES
R_ID = 2 * HT_BYTES + 512
R_SMALL = R_ID + 512
R_F = R_SMALL + 256
R_PT = R_F + 864
R_OS = R_SMALL + 1408
R_FREE = R_OS + 4 * D
R_LF = R_OS + 1024
R_OT = 4 * (12 * SEQ + 4 * SEQ)
R_ZS = R_FREE + 4 * (4 * KC * GRP + 6 * GRP + 6 * GRP + (NT + 1) * P + KC * P)
R_SCORES = R_ZS + 4 * (6 * GRP + 8 * GRP)


def project(nc, io, place):
    ht_hi = view(place.at(R_HI, "ht_hi", KC * TOK, F32R), k=KC, t=TOK)
    ht_lo = view(place.at(R_LO, "ht_lo", KC * TOK, F32R), k=KC, t=TOK)
    ht_hi_f = ht_hi.bitcast(F32)
    ident = place.at(R_ID, "ident", P)
    o = R_FREE
    w_hi = view(place.at(o, "w_hi", 2 * KC * GRP, F32R), s=2, k=KC, n=GRP); o += 8 * KC * GRP
    w_lo = view(place.at(o, "w_lo", 2 * KC * GRP, F32R), s=2, k=KC, n=GRP); o += 8 * KC * GRP
    RAW = 3
    raw = view(place.at(o, "w_raw", RAW * 2 * GRP), s=RAW, k=2, n=GRP); o += 4 * RAW * 2 * GRP
    zst = view(place.at(o, "z_stage", 2 * GRP), s=2, n=GRP); o += 8 * GRP
    zraw = view(place.at(o, "z_raw", 2 * GRP), s=2, n=GRP); o += 8 * GRP
    tmp = view(place.at(o, "rope_tmp", 2 * GRP), s=2, n=GRP); o += 8 * GRP
    rope = view(place.at(o, "rope", (NT + 1) * P), t=NT + 1, n=P); o += 4 * (NT + 1) * P
    hsp = view(place.at(o, "h_sample", KC * P, F32R), k=KC, m=P); o += 4 * KC * P
    assert o == R_ZS
    zs = view(place.at(o, "z_sample", 6 * GRP), g=6, n=GRP); o += 4 * 6 * GRP
    KP = 4
    kpage = view(place.at(o, "k_page", KP * 2 * GRP), s=KP, n=2 * GRP)
    x_sb = view(place.at(o, "x", 2 * D), s=2, n=D)
    xn = place.at(o + 8 * D, "xn", D)
    g_bc = place.at(o + 12 * D, "g_bc", D); o += 4 * KP * 2 * GRP
    assert o == R_SCORES
    scores = place.at(o, "scores", DB * PAGES * 16); o += 4 * DB * PAGES * 16
    qbc = view(place.at(o, "q_bc", 2 * 2 * GRP), s=2, n=2 * GRP); o += 16 * GRP
    small = place.at(R_SMALL, "small", 64)
    ssq, ms, rstd, expo, b_f = (small[:, 9 * n:9 * n + 9] for n in range(5))
    b_f = b_f[:, 0:MAPS]
    f_sb = place.at(R_F, "f_tmp", 3 * (NT + 1) * MAPS)
    junk = scores
    ptab = io["pt_sb"]

    HALF = GRP // 2
    w_v = io["w_in"].rearrange("(k p) n -> p k n", p=P)

    sem = lambda n: io["ctx"].enter_context(nc.semaphore("a_" + n))
    consts_in, ssq_done, ms_done, rstd_done = map(sem, ["consts_in", "ssq_done", "ms_done", "rstd_done"])
    x_in = [sem("x_in0"), sem("x_in1")]
    xn_done, tr_done, hi_done, lo_done = map(sem, ["xn_done", "tr_done", "hi_done", "lo_done"])
    raw_in = [sem(f"raw_in{s}") for s in range(RAW)]
    w_hi_done, w_lo_done, proj_done, evac, rope_step = map(sem, ["w_hi_done", "w_lo_done", "proj_done", "evac", "rope_step"])
    z_done, z_copy = map(sem, ["z_done", "z_copy"])
    stored = [sem("stored0"), sem("stored1")]
    zs_stored, qs_stored = map(sem, ["zs_stored", "qs_stored"])
    qbc_in = [sem("qbc_in0"), sem("qbc_in1")]
    kp_in = [sem(f"kp_in{s}") for s in range(KP)]
    mult_done, red_done, zeroed = map(sem, ["mult_done", "red_done", "zeroed"])
    lf_in = sem("lf_in")
    lf = view(place.at(R_LF, "lf_pages", DB * PAGES * MAPS), g=DB * PAGES, h=MAPS)
    f_in, wf_done, f_done, f_step, f_stored = map(sem, ["f_in", "wf_done", "f_done", "f_step", "f_stored"])
    PS = io["PS"]
    wf_hi = w_hi[:, 1, 0, 0:KC * MAPS].rearrange("p (k n) -> p k n", n=MAPS)
    wf_lo = w_lo[:, 1, 0, 0:KC * MAPS].rearrange("p (k n) -> p k n", n=MAPS)
    wf_raw = tmp[:, 0, 0:KC * MAPS].rearrange("p (k n) -> p k n", n=MAPS)

    NS = NT + 1
    steps = [(i, t) for i in range(6) for t in range(NS)]
    is_rope = lambda i, t: ORDER[i] in (QA, KA)
    uses_zraw = lambda i, t: is_rope(i, t) or t == NT
    zr_count = [0]
    for i, t in steps:
        zr_count.append(zr_count[-1] + uses_zraw(i, t))
    out_of = {KA: io["o_dk"], VA: io["o_dv"], KF: io["o_fk"], VF: io["o_fv"]}
    outs_of = {KA: io["o_sdk"], VA: io["o_sdv"], KF: io["o_sfk"], VF: io["o_sfv"]}
    PG0 = 3
    pages_at = {}
    per = (DB * PAGES + 3 * NS - 1) // (3 * NS)
    for n in range(DB * PAGES):
        pages_at.setdefault((PG0 + n // per // NS, n // per % NS), []).append(n)

    with nc.Block() as block:

        @block.sync
        def _(sp):
            sp.dma_start(ident[:, :], io["consts"][:, C_ID:C_ID + P]).then_inc(consts_in, 16)
            sp.dma_start(rope[:, :, :], io["consts"][:, C_ROPE:C_SELH].rearrange("p (t n) -> p t n", n=P)).then_inc(consts_in, 16)
            sp.dma_start(g_bc[:, :], io["attn_pre_g"].to_broadcast([P, D])).then_inc(consts_in, 16)
            sp.dma_start(wf_raw, w_v[:, :, F_COL:F_COL + MAPS]).then_inc(f_in, 16)
            sp.dma_start(b_f, io["b_f"].to_broadcast([P, MAPS])).then_inc(f_in, 16)
            sp.dma_start(ptab[0:1, :], io["page_table"]).then_inc(consts_in, 16)

            def load_x(t):
                if t >= 2:
                    sp.wait_ge(xn_done, t - 1)
                n = P if t < NT else DB
                src = io["x"][t * P:t * P + P, :] if t < NT else io["xs"]
                sp.dma_start(x_sb[0:n, t % 2, :], src).then_inc(x_in[t % 2], 16)

            def load_w(q):
                i, pair = divmod(q, 4)
                if q >= RAW:
                    sp.wait_ge(w_lo_done, q - RAW + 1)
                c = BLOCK_COL[ORDER[i]]
                sp.dma_start(raw[:, q % RAW, :, :], w_v[:, 2 * pair:2 * pair + 2, c:c + GRP]).then_inc(raw_in[q % RAW], 16)

            load_x(0)
            load_x(1)
            for q in range(RAW):
                load_w(q)
            for t in range(2, NS):
                load_x(t)
            for q in range(RAW, 16):
                load_w(q)
            sp.wait_ge(z_done, zr_count[3 * NS])
            for n, g in enumerate((QA, QF)):
                sp.dma_start(io["qs_dram"][:, n * GRP:n * GRP + GRP], zs[0:DB, g, :]).then_inc(qs_stored, 16)
            sp.wait_ge(qs_stored, 32)
            def load_page(g):
                b, n = divmod(g, PAGES)
                if n == 0:
                    if b >= 2:
                        sp.wait_ge(mult_done, (b - 1) * PAGES)
                    sp.dma_start(qbc[:, b % 2, :], io["qs_dram"][b:b + 1, :].to_broadcast([P, 2 * GRP])).then_inc(qbc_in[b % 2], 16)
                if g >= KP:
                    sp.wait_ge(red_done, g - KP + 1)
                page = sp.value_load(ptab[0:1, g:g + 1], min_val=0, max_val=NPOOL - 1)
                for kind, cache in enumerate((io["c_dk"], io["c_fk"])):
                    sp.dma_start(kpage[:, g % KP, kind * GRP:(kind + 1) * GRP],
                                 cache[bass.ds(page * P, P), :]).then_inc(kp_in[g % KP], 16)

            sp.wait_ge(consts_in, 64)
            q = 16
            for i, t in steps[PG0 * NS:]:
                while q < 24 and ((q - RAW) // 4 - 1, (q - RAW) % 4) < (i, t):
                    load_w(q)
                    q += 1
                for g in pages_at.get((i, t), []):
                    load_page(g)
            sp.wait_ge(lf_in, 16 * DB * PAGES)
            sp.wait_ge(f_stored, 32)
            sp.wait_ge(zs_stored, 16 * 4)

        @block.gpsimd
        def _(pool):
            pool.memset(expo, -0.5).then_inc(zeroed, 1)
            pool.memset(hsp.bitcast(F32), 0.0).then_inc(zeroed, 1)
            pool.wait_ge(zeroed, 2)
            for t in range(NS):
                n = P if t < NT else DB
                pool.wait_ge(ssq_done, t + 1)
                pool.tensor_scalar(ms[0:n, t:t + 1], ssq[0:n, t:t + 1], 1.0 / D, EPS, ALU.mult, ALU.add).then_inc(ms_done, 1)
                pool.wait_ge(ms_done, t + 1)
                pool.tensor_tensor(rstd[0:n, t:t + 1], ms[0:n, t:t + 1], expo[0:n, t:t + 1], ALU.pow).then_inc(rstd_done, 1)
            pool.wait_ge(consts_in, 64)
            with pool.Fori(0, DB * PAGES) as g:
                page = pool.value_load(ptab[0:1, bass.ds(g, 1)], min_val=0, max_val=NPOOL - 1)
                pool.dma_start(lf[:, bass.ds(g, 1), :], io["c_lf"][bass.ds(page * P, P), :].rearrange("p (a h) -> p a h", a=1)).then_inc(lf_in, 16)
            for g in range(DB * PAGES):
                b = g // PAGES
                if g % PAGES == 0:
                    pool.wait_ge(qbc_in[b % 2], 16 * (b // 2 + 1))
                pool.wait_ge(kp_in[g % KP], 32 * (g // KP + 1))
                pool.tensor_tensor(kpage[:, g % KP, :], kpage[:, g % KP, :], qbc[:, b % 2, :], ALU.mult).then_inc(mult_done, 1)

        @block.scalar
        def _(act):
            def square(t):
                n = P if t < NT else DB
                act.wait_ge(x_in[t % 2], 16 * (t // 2 + 1))
                if t:
                    act.wait_ge(ssq_done, t)
                act.activation(junk[0:n, :], x_sb[0:n, t % 2, :], ACT.Square, accum_out=ssq[0:n, t:t + 1]).then_inc(ssq_done, 1)

            def hi_part(t):
                n = P if t < NT else DB
                for half in range(2):
                    act.wait_ge(tr_done, 2 * t + half + 1)
                    src = PS[:, 4 + 2 * (t % 2) + half, 0:4 * n].rearrange("p (k n) -> p k n", n=n)
                    dst = (ht_hi[:, 4 * half:4 * half + 4, t * P:t * P + n] if t < NT else
                           hsp[:, 4 * half:4 * half + 4, 0:n])
                    if t == NT:
                        act.wait_ge(zeroed, 2)
                    act.activation(dst, src, ACT.Copy).then_inc(hi_done, 1)

            def w_split(q):
                i, pair = divmod(q, 4)
                act.wait_ge(raw_in[q % RAW], 16 * (q // RAW + 1))
                if i >= 2:
                    act.wait_ge(proj_done, NS * (i - 1))
                if i == 1:
                    act.wait_ge(f_done, 1)
                act.activation(w_hi[:, i % 2, 2 * pair:2 * pair + 2, :], raw[:, q % RAW, :, :], ACT.Copy).then_inc(w_hi_done, 1)

            act.wait_ge(f_in, 32)
            act.activation(wf_hi, wf_raw, ACT.Copy).then_inc(wf_done, 1)
            square(0)
            for t in range(1, NS):
                square(t)
                hi_part(t - 1)
            hi_part(NT)
            for q in range(4):
                w_split(q)

            pending = None
            for j, (i, t) in enumerate(steps):
                blk = ORDER[i]
                act.wait_ge(proj_done, j + 1)
                bank = PS[:, j % 4, :]
                slot = (i * NT + t) % 2
                if uses_zraw(i, t) and zr_count[j - 1] and j >= 2:
                    act.wait_ge(z_done, zr_count[j - 1])
                if t == NT:
                    act.activation(zraw[0:DB, j % 2, :], bank[LO_ROW:LO_ROW + DB, :], ACT.Copy).then_inc(evac, 1)
                elif is_rope(i, t):
                    act.activation(zraw[:, j % 2, :], bank, ACT.Copy).then_inc(evac, 1)
                else:
                    act.wait_ge(stored[slot], 16 * ((i * NT + t) // 2))
                    act.activation(zst[:, slot, :], bank, ACT.Copy).then_inc(evac, 1)
                if pending is not None:
                    pending()
                    pending = None
                if t < NT:
                    def pending(i=i, t=t, j=j, slot=slot, blk=blk):
                        if is_rope(i, t):
                            act.wait_ge(z_done, zr_count[j + 1])
                        else:
                            act.wait_ge(evac, j + 1)
                        dst = (io["q_dram"][t * P:(t + 1) * P, (blk == QF) * GRP:(blk == QF) * GRP + GRP]
                               if blk in (QA, QF) else out_of[blk][t * P:(t + 1) * P, :])
                        act.dma_start(dst, zst[:, slot, :]).then_inc(stored[slot], 16)
                elif blk in outs_of:
                    def pending(i=i, blk=blk):
                        act.wait_ge(z_done, zr_count[(i + 1) * NS])
                        act.dma_start(outs_of[blk], zs[0:DB, blk, :]).then_inc(zs_stored, 16)
                if i < 5 and t < 4:
                    w_split(4 * (i + 1) + t)
                if (i, t) == (5, 1):
                    act.wait_ge(f_step, 3)
                    act.activation(f_sb[:, 72:144], f_sb[:, 72:144], ACT.Exp).then_inc(f_step, 1)
                    act.wait_ge(f_step, 4)
                    act.activation(f_sb[:, 144:216], f_sb[:, 72:144], ACT.Ln, bias=1.0).then_inc(f_step, 1)
                if (i, t) == (5, 3):
                    act.wait_ge(f_step, 6)
                    act.dma_start(io["o_flf"].rearrange("(t p) h -> p t h", p=P),
                                  f_sb[:, 0:64].rearrange("p (t h) -> p t h", h=MAPS)).then_inc(f_stored, 16)
                    act.dma_start(io["o_sflf"], f_sb[0:DB, 64:72]).then_inc(f_stored, 16)
            pending()
            for s in range(2):
                act.wait_ge(stored[s], 16 * 6 * NT // 2)

        @block.vector
        def _(dve):
            dve.wait_ge(consts_in, 64)
            dve.wait_ge(f_in, 32)
            dve.wait_ge(wf_done, 1)
            dve.tensor_tensor(wf_lo, wf_raw, wf_hi.bitcast(F32), ALU.subtract).then_inc(wf_done, 1)

            def lo_part(t):
                n = P if t < NT else DB
                for half in range(2):
                    dve.wait_ge(hi_done, 2 * t + half + 1)
                    src = PS[:, 4 + 2 * (t % 2) + half, 0:4 * n].rearrange("p (k n) -> p k n", n=n)
                    sl = slice(4 * half, 4 * half + 4)
                    if t < NT:
                        hi, dst = ht_hi_f[:, sl, t * P:t * P + n], ht_lo[:, sl, t * P:t * P + n]
                    else:
                        hi, dst = hsp[:, sl, 0:n].bitcast(F32), hsp[:, sl, LO_ROW:LO_ROW + n]
                    dve.tensor_tensor(dst, src, hi, ALU.subtract).then_inc(lo_done, 1)

            def norm(t):
                n = P if t < NT else DB
                dve.wait_ge(rstd_done, t + 1)
                if t:
                    dve.wait_ge(tr_done, 2 * t)
                dve.scalar_tensor_tensor(xn[0:n, :], x_sb[0:n, t % 2, :], rstd[0:n, t:t + 1], g_bc[0:n, :],
                                         ALU.mult, ALU.mult).then_inc(xn_done, 1)

            norm(0)
            for t in range(1, NS):
                norm(t)
                lo_part(t - 1)
            lo_part(NT)

            def w_split(q):
                i, pair = divmod(q, 4)
                dve.wait_ge(w_hi_done, q + 1)
                sl = (slice(None), i % 2, slice(2 * pair, 2 * pair + 2), slice(None))
                dve.tensor_tensor(w_lo[sl], raw[:, q % RAW, :, :], w_hi[sl].bitcast(F32), ALU.subtract).then_inc(w_lo_done, 1)

            for q in range(4):
                w_split(q)

            rs = 0
            fs = 0
            for j, (i, t) in enumerate(steps):
                blk = ORDER[i]
                n = P if t < NT else DB
                if i < 5 and t < 4:
                    w_split(4 * (i + 1) + t)
                if uses_zraw(i, t):
                    dve.wait_ge(evac, j + 1)
                    if zr_count[j]:
                        dve.wait_ge(z_done, zr_count[j])
                    src = zraw[0:n, j % 2, :]
                    if t == NT:
                        ins = dve.tensor_tensor(zs[0:DB, blk, :], PS[0:DB, j % 4, :], src, ALU.add)
                        if is_rope(i, t):
                            ins.then_inc(rope_step, 1)
                            rs += 1
                            dve.wait_ge(rope_step, rs)
                            src = zs[0:DB, blk, :]
                        else:
                            ins.then_inc(z_done, 1)
                    if is_rope(i, t):
                        xv = src.rearrange("p (m h c) -> p m h c", m=MAPS, h=2)
                        cos = rope[0:n, t:t + 1, 0:HD].to_broadcast([n, MAPS, HD])
                        sin = rope[0:n, t:t + 1, HD:2 * HD].to_broadcast([n, MAPS, HD])
                        t1 = tmp[0:n, 0, :].rearrange("p (m c) -> p m c", c=HD)
                        t2 = tmp[0:n, 1, :].rearrange("p (m h c) -> p m h c", m=MAPS, h=2)
                        dve.tensor_tensor(t1, src.rearrange("p (m c) -> p m c", c=HD), cos, ALU.mult).then_inc(rope_step, 1)
                        dve.tensor_tensor(t2[:, :, 0, :], xv[:, :, 1, :], sin[:, :, 0:HD // 2], ALU.mult).then_inc(rope_step, 1)
                        dve.tensor_tensor(t2[:, :, 1, :], xv[:, :, 0, :], sin[:, :, HD // 2:HD], ALU.mult).then_inc(rope_step, 1)
                        rs += 3
                        dve.wait_ge(rope_step, rs)
                        if t < NT:
                            slot = (i * NT + t) % 2
                            if i * NT + t >= 2:
                                dve.wait_ge(stored[slot], 16 * ((i * NT + t) // 2))
                            dst = zst[:, slot, :]
                        else:
                            dst = src
                        last = dve.tensor_tensor(dst, tmp[0:n, 0, :], tmp[0:n, 1, :], ALU.add)
                        last.then_inc(z_done, 1)
                if (i, t) == (0, NT):
                    dve.wait_ge(f_done, 1)
                    dve.tensor_copy(f_sb[:, 144:216], PS[:, 4, 0:72]).then_inc(f_step, 1)
                    dve.wait_ge(f_step, 1)
                    dve.tensor_tensor(f_sb[0:DB, 208:216], PS[LO_ROW:LO_ROW + DB, 4, 64:72],
                                      f_sb[0:DB, 208:216], ALU.add).then_inc(wf_done, 1)
                    dve.wait_ge(wf_done, 3)
                    dve.tensor_tensor(f_sb[:, 0:72].rearrange("p (t h) -> p t h", h=MAPS),
                                      f_sb[:, 144:216].rearrange("p (t h) -> p t h", h=MAPS),
                                      b_f.rearrange("p (a h) -> p a h", a=1).to_broadcast([P, NS, MAPS]),
                                      ALU.add).then_inc(f_step, 1)
                    dve.wait_ge(f_step, 2)
                    dve.scalar_tensor_tensor(f_sb[:, 72:144], f_sb[:, 0:72], -1.0, f_sb[:, 0:72], ALU.mult, ALU.min).then_inc(f_step, 1)
                if (i, t) == (5, 2):
                    dve.wait_ge(f_step, 5)
                    dve.scalar_tensor_tensor(f_sb[:, 0:72], f_sb[:, 0:72], 0.0, f_sb[:, 144:216], ALU.min, ALU.subtract).then_inc(f_step, 1)
                for g in pages_at.get((i, t), []):
                    dve.wait_ge(mult_done, g + 1)
                    dve.tensor_reduce(scores[:, :].rearrange("p (k g m) -> p k g m", k=2, m=MAPS)[:, :, g, :], kpage[:, g % KP, :].rearrange("p (k m c) -> p k m c", k=2, c=HD),
                                      AX, ALU.add).then_inc(red_done, 1)

        @block.tensor
        def _(pe):
            pe.wait_ge(consts_in, 64)
            for t in range(NS):
                n = P if t < NT else DB
                pe.wait_ge(xn_done, t + 1)
                for half in range(2):
                    if t >= 2:
                        pe.wait_ge(lo_done, 2 * (t - 2) + half + 1)
                    for k in range(4):
                        c = (4 * half + k) * P
                        ins = pe.transpose(PS[:, 4 + 2 * (t % 2) + half, k * n:k * n + n], xn[0:n, c:c + P], ident[0:n, 0:n])
                    ins.then_inc(tr_done, 1)
            pe.wait_ge(lo_done, 2 * NS)
            pe.wait_ge(wf_done, 2)
            for t in range(NS):
                parts = ([(ht_hi, wf_hi), (ht_hi, wf_lo), (ht_lo, wf_hi)] if t < NT else [(hsp, wf_hi), (hsp, wf_lo)])
                for n, (a, w) in enumerate(parts):
                    for k in range(KC):
                        at = a[:, k, t * P:(t + 1) * P] if t < NT else a[:, k, :]
                        ins = pe.matmul(PS[:, 4, t * MAPS:(t + 1) * MAPS], at, w[:, k, :], start=(n == 0 and k == 0),
                                        stop=(n == len(parts) - 1 and k == KC - 1))
            ins.then_inc(f_done, 1)
            for j, (i, t) in enumerate(steps):
                if t == 0:
                    pe.wait_ge(w_lo_done, 4 * (i + 1))
                if j >= 4:
                    pe.wait_ge(evac, j - 3)
                    if zr_count[j - 3]:
                        pe.wait_ge(z_done, zr_count[j - 3])
                parts = ([(ht_hi, w_hi), (ht_hi, w_lo), (ht_lo, w_hi)] if t < NT else [(hsp, w_hi), (hsp, w_lo)])
                for k in range(KC):
                    for n, (a, w) in enumerate(parts):
                        at = a[:, k, t * P:(t + 1) * P] if t < NT else a[:, k, :]
                        ins = pe.matmul(PS[:, j % 4, :], at, w[:, i % 2, k, :], start=(n == 0 and k == 0),
                                        stop=(n == len(parts) - 1 and k == KC - 1))
                ins.then_inc(proj_done, 1)


def decode(nc, io, place):
    ident = place.at(R_ID, "ident", P)
    zs = view(place.at(R_ZS, "z_sample", 6 * GRP), g=6, n=GRP)
    scores = place.at(R_SCORES, "scores", 2 * DB * PAGES * MAPS)
    sc5 = scores[:, :].rearrange("p (k b n m) -> p k b n m", k=2, b=DB, m=MAPS)
    sck = scores[:, :].rearrange("p (k c) -> p k c", k=2)
    f_sb = place.at(R_F, "f_tmp", 3 * (NT + 1) * MAPS)
    lf = view(place.at(R_LF, "lf_pages", DB * PAGES * MAPS), b=DB, n=PAGES * MAPS)
    small = place.at(R_SMALL, "small", 64)
    o = R_FREE
    epad = view(place.at(o, "e_pad", 2 * DB * PAGES * HD), k=2, g=DB * PAGES, c=HD); o += 8 * DB * PAGES * HD
    VP = 6
    vpage = view(place.at(o, "v_page", VP * 2 * GRP), s=VP, n=2 * GRP); o += 8 * VP * GRP
    consts = place.at(o, "consts", C_ROPE - C_SUFFIX); o += 4 * (C_ROPE - C_SUFFIX)
    suffix, ones = consts[:, 0:P], consts[:, P:2 * P]
    hm = consts[:, C_HM - C_SUFFIX:C_HM - C_SUFFIX + GRP]
    selb = consts[:, C_SELB - C_SUFFIX:C_SELB - C_SUFFIX + DB]
    sgn = consts[:, C_SIGN - C_SUFFIX:C_SIGN - C_SUFFIX + 2]
    lamv = view(place.at(o, "lam_vectors", 6 * HD), v=6, n=HD); o += 24 * HD
    prod = place.at(o, "prod", 2 * GRP); o += 8 * GRP
    snew = place.at(o, "s_new", 2 * MAPS); o += 8 * MAPS
    npad = place.at(o, "new_pad", P); o += 4 * P
    lfpad = place.at(o, "lf_pad", DB * MAPS); o += 4 * DB * MAPS
    m1 = place.at(o, "m1", P); o += 4 * P
    diag = place.at(o, "diag", P); o += 4 * P
    negm = place.at(o, "neg_max", P); o += 4 * P
    cols = place.at(o, "cols", 16); o += 64
    gated = place.at(o, "gated", GRP); o += 4 * GRP
    osamp = place.at(R_OS, "o_sample", 2 * GRP)
    assert o <= R_ZS
    PS = io["PS"]
    DOUT, FB, MT, MC, NM, LC, OD, OF = (PS[:, n, :] for n in (0, 1, 2, 3, 4, 5, 6, 7))
    mx, mxc, l_r, coef, lam = (cols[:, n:n + 1] for n in range(5))
    lsum = cols[:, 6:8]
    sem = lambda n: io["ctx"].enter_context(nc.semaphore("d_" + n))
    consts_in, zeroed, v_step, fb_done, mt_done, nm_done, e_done, lc_done = map(
        sem, ["consts_in", "zeroed", "v_step", "fb_done", "mt_done", "nm_done", "e_done", "lc_done"])
    pads_ready, padded, sel_done, lam_step = map(sem, ["pads_ready", "padded", "sel_done", "lam_step"])
    vp_in = [sem(f"vp_in{s}") for s in range(VP)]
    v_used = sem("v_used")
    diag8 = ident[0:DB, 0:DB].rearrange("p (k b m) -> p k b m", k=1, m=1).to_broadcast([DB, 2, DB, MAPS])

    with nc.Block() as block:

        @block.sync
        def _(sp):
            sp.dma_start(consts[:, :], io["consts"][:, C_SUFFIX:C_ROPE]).then_inc(consts_in, 16)
            for n, name in enumerate(("lam_q1", "lam_k1", "lam_q2", "lam_k2")):
                sp.dma_start(lamv[:, n, :], io[name].to_broadcast([P, HD])).then_inc(consts_in, 16)
            for g in range(DB * PAGES):
                if g >= VP:
                    sp.wait_ge(v_used, g - VP + 1)
                page = sp.value_load(io["pt_sb"][0:1, g:g + 1], min_val=0, max_val=NPOOL - 1)
                for kind, cache in enumerate((io["c_dv"], io["c_fv"])):
                    sp.dma_start(vpage[:, g % VP, kind * GRP:(kind + 1) * GRP],
                                 cache[bass.ds(page * P, P), :]).then_inc(vp_in[g % VP], 16)

        @block.gpsimd
        def _(pool):
            pool.memset(epad[:, :, :, :], 0.0).then_inc(zeroed, 1)

        @block.scalar
        def _(act):
            act.wait_ge(lam_step, 3)
            act.activation(lsum, lsum, ACT.Exp).then_inc(lam_step, 1)
            act.wait_ge(v_step, io["D_SUB"])
            act.activation(scores[:, :], scores[:, :], ACT.Exp).then_inc(e_done, 1)
            act.wait_ge(v_step, io["D_PN"])
            act.activation(npad[0:DB, :], npad[0:DB, :], ACT.Exp).then_inc(e_done, 1)
            act.wait_ge(zeroed, 1)
            act.wait_ge(e_done, 2)
            for b in range(DB):
                act.activation(epad[:, 1, b * PAGES:(b + 1) * PAGES, b * MAPS:(b + 1) * MAPS], sc5[:, 1, b, :, :], ACT.Copy).then_inc(padded, 1)

        @block.vector
        def _(dve):
            count = [0]

            def step(ins):
                ins.then_inc(v_step, 1)
                count[0] += 1
                dve.wait_ge(v_step, count[0])

            dve.wait_ge(consts_in, 80)
            step(dve.tensor_tensor(prod[0:DB, 0:GRP], zs[0:DB, QA, :], zs[0:DB, KA, :], ALU.mult))
            step(dve.tensor_tensor(prod[0:DB, GRP:], zs[0:DB, QF, :], zs[0:DB, KF, :], ALU.mult))
            step(dve.tensor_reduce(snew[0:DB, :], prod[0:DB, :].rearrange("p (m c) -> p m c", c=HD), AX, ALU.add))
            step(dve.scalar_tensor_tensor(npad[0:DB, :].rearrange("p (k b m) -> p k b m", k=2, b=DB)[:, 0],
                                          snew[0:DB, 0:MAPS].rearrange("p (b m) -> p b m", b=1).to_broadcast([DB, DB, MAPS]), SCALE,
                                          diag8[:, 0], ALU.mult, ALU.mult))
            step(dve.scalar_tensor_tensor(npad[0:DB, :].rearrange("p (k b m) -> p k b m", k=2, b=DB)[:, 1],
                                          snew[0:DB, MAPS:].rearrange("p (b m) -> p b m", b=1).to_broadcast([DB, DB, MAPS]), SCALE,
                                          diag8[:, 1], ALU.mult, ALU.mult))
            step(dve.tensor_tensor(lfpad[0:DB, :].rearrange("p (b m) -> p b m", b=DB),
                                   f_sb[0:DB, 64:72].rearrange("p (b m) -> p b m", b=1).to_broadcast([DB, DB, MAPS]),
                                   diag8[:, 0], ALU.mult))
            assert count[0] == io["D_PADS"]
            for n in range(2):
                dve.tensor_tensor(lamv[:, 4 + n, :], lamv[:, 2 * n, :], lamv[:, 2 * n + 1, :], ALU.mult).then_inc(lam_step, 1)
            dve.wait_ge(lam_step, 2)
            dve.tensor_reduce(lsum, lamv[:, 4:6, :], AX, ALU.add).then_inc(lam_step, 1)
            dve.wait_ge(lam_step, 4)
            step(dve.tensor_scalar(lam, lsum[:, 0:1], lsum[:, 1:2], LAM_INIT, ALU.subtract, ALU.add))
            step(dve.tensor_scalar(small[:, 50:51], lam, -1.0, None, ALU.mult))
            step(dve.tensor_scalar(sck[:, 0, :], sck[:, 0, :], SCALE, None, ALU.mult))
            dve.wait_ge(fb_done, 1)
            step(dve.scalar_tensor_tensor(sck[:, 1, :], sck[:, 1, :], SCALE, FB, ALU.mult, ALU.add))
            step(dve.tensor_reduce(m1[:, :].rearrange("p (k b m) -> p k b m", k=2, b=DB)[:, 0], sc5[:, 0].rearrange("p b n m -> p b m n"), AX, ALU.max))
            step(dve.tensor_reduce(m1[:, :].rearrange("p (k b m) -> p k b m", k=2, b=DB)[:, 1], sc5[:, 1].rearrange("p b n m -> p b m n"), AX, ALU.max))
            assert count[0] == io["D_M1"]
            dve.wait_ge(mt_done, 2)
            step(dve.tensor_reduce(mx, MT[:, 0:P], AX, ALU.max))
            step(dve.tensor_tensor(mx, mx, MC[:, 0:1], ALU.max))
            step(dve.tensor_scalar(diag[:, :], ident[:, :], mx, -1.0, ALU.mult, ALU.mult))
            assert count[0] == io["D_DIAG"]
            dve.wait_ge(nm_done, 1)
            step(dve.tensor_copy(negm[:, :], NM[:, 0:P]))
            for k in range(2):
                nb = negm[:, :].rearrange("p (k b n m) -> p k b n m", k=2, b=DB, n=1)[:, k].to_broadcast([P, DB, PAGES, MAPS])
                step(dve.tensor_tensor(sc5[:, k], sc5[:, k], nb, ALU.add))
            assert count[0] == io["D_SUB"]
            step(dve.tensor_tensor(npad[0:DB, :], npad[0:DB, :], negm[0:DB, :], ALU.add))
            step(dve.tensor_scalar(npad[0:DB, :], npad[0:DB, :], 0.0, None, ALU.min))
            assert count[0] == io["D_PN"]
            dve.wait_ge(e_done, 2)
            step(dve.tensor_tensor(npad[0:DB, :].rearrange("p (k b m) -> p k b m", k=2, b=DB)[:, 0], npad[0:DB, :].rearrange("p (k b m) -> p k b m", k=2, b=DB)[:, 0], diag8[:, 0], ALU.mult))
            step(dve.tensor_tensor(npad[0:DB, :].rearrange("p (k b m) -> p k b m", k=2, b=DB)[:, 1], npad[0:DB, :].rearrange("p (k b m) -> p k b m", k=2, b=DB)[:, 1], diag8[:, 1], ALU.mult))
            for k in range(2):
                step(dve.tensor_reduce(m1[:, :].rearrange("p (k b m) -> p k b m", k=2, b=DB)[:, k], sc5[:, k].rearrange("p b n m -> p b m n"), AX, ALU.add))
            assert count[0] == io["D_L"]
            dve.wait_ge(zeroed, 1)
            for b in range(DB):
                dve.tensor_copy(epad[:, 0, b * PAGES:(b + 1) * PAGES, b * MAPS:(b + 1) * MAPS], sc5[:, 0, b, :, :]).then_inc(padded, 1)
            dve.wait_ge(lc_done, 1)
            step(dve.reciprocal(l_r, LC[:, 0:1]))
            step(dve.tensor_scalar(coef, sgn[:, 1:2], small[:, 50:51], sgn[:, 0:1], ALU.mult, ALU.add))
            step(dve.tensor_tensor(coef, coef, l_r, ALU.mult))
            dve.wait_ge(v_used, DB * PAGES)
            step(dve.scalar_tensor_tensor(gated[:, :], DOUT, coef, hm, ALU.mult, ALU.mult))
            assert count[0] == io["D_GATED"]
            dve.wait_ge(sel_done, 1)
            step(dve.tensor_copy(osamp[0:DB, 0:GRP], OD[0:DB, :]))
            step(dve.tensor_copy(osamp[0:DB, GRP:], OF[0:DB, :]))

        @block.tensor
        def _(pe):
            pe.wait_ge(consts_in, 80)
            pe.wait_ge(v_step, io["D_PADS"])
            fb3 = FB.rearrange("p (b n) -> p b n", b=DB)
            pe.matmul(fb3, suffix, lf[:, :, :], start=True, stop=False, skip_group_check=True)
            for d in range(1, PAGES):
                n = (PAGES - d) * MAPS
                pe.matmul(fb3[:, :, 0:n], ones, lf[:, :, d * MAPS:], start=False, stop=False, skip_group_check=True)
            pe.matmul(FB.rearrange("p (b n m) -> p b n m", b=DB, m=MAPS), ones[0:DB, :],
                      lfpad[0:DB, :].rearrange("p (b n m) -> p b n m", b=DB, n=1).to_broadcast([DB, DB, PAGES, MAPS]),
                      start=False, stop=True, skip_group_check=True).then_inc(fb_done, 1)
            pe.wait_ge(v_step, io["D_M1"])
            pe.transpose(MT[:, 0:P], m1[:, :], ident[:, :]).then_inc(mt_done, 1)
            pe.matmul(MC[:, 0:1], npad[0:DB, :], ones[0:DB, 0:1], start=True, stop=True).then_inc(mt_done, 1)
            pe.wait_ge(v_step, io["D_DIAG"])
            pe.matmul(NM[:, 0:P], ones, diag[:, :], start=True, stop=True).then_inc(nm_done, 1)
            pe.wait_ge(v_step, io["D_L"])
            pe.matmul(LC[:, 0:1], m1[:, :], ones[:, 0:1], start=True, stop=False)
            pe.matmul(LC[:, 0:1], npad[0:DB, :], ones[0:DB, 0:1], start=False, stop=True).then_inc(lc_done, 1)
            pe.wait_ge(padded, 2 * DB)
            for k, g in enumerate((VA, VF)):
                pe.matmul(DOUT[k * HD:(k + 1) * HD, :], npad[0:DB, k * HD:(k + 1) * HD], zs[0:DB, g, :], start=True, stop=False,
                          skip_group_check=True)
            for g in range(DB * PAGES):
                pe.wait_ge(vp_in[g % VP], 32 * (g // VP + 1))
                for k in range(2):
                    ins = pe.matmul(DOUT[k * HD:(k + 1) * HD, :], epad[:, k, g, :], vpage[:, g % VP, k * GRP:(k + 1) * GRP],
                                    start=False, stop=(g == DB * PAGES - 1), skip_group_check=True)
                ins.then_inc(v_used, 1)
            pe.wait_ge(v_step, io["D_GATED"])
            for k, dst in ((0, OD), (1, OF)):
                ins = pe.matmul(dst[0:DB, :], selb[k * HD:(k + 1) * HD, :], gated[k * HD:(k + 1) * HD, :], start=True, stop=True)
            ins.then_inc(sel_done, 1)


def attend(nc, io, place):
    ident = place.at(R_ID, "ident", P)
    small = place.at(R_SMALL, "small", 64)
    neg_lam = small[:, 50:51]
    f_sb = place.at(R_F, "f_tmp", 3 * (NT + 1) * MAPS)
    o = 0
    ks = view(place.at(o, "k_split", 4 * SEQ, F32R), s=2, m=2, n=SEQ); o += 16 * SEQ
    qh = view(place.at(o, "q_hi", 4 * SEQ, F32R), s=2, m=2, n=SEQ); o += 16 * SEQ
    ql = view(place.at(o, "q_lo", 4 * SEQ, F32R), s=2, m=2, n=SEQ); o += 16 * SEQ
    vh = view(place.at(o, "v_hi", 2 * NT * P, F32R), s=2, t=NT, n=P); o += 8 * NT * P
    vl = view(place.at(o, "v_lo", 2 * NT * P, F32R), s=2, t=NT, n=P); o += 8 * NT * P
    assert o <= R_ID
    o = R_FREE
    o_all = view(place.at(o, "o_all", NT * D), t=NT, n=D); o += 4 * NT * D
    qd = view(place.at(o, "q_twice", 2 * 2 * NT * P), s=2, m=2, t=NT, n=P); o += 16 * NT * P
    kd = view(place.at(o, "k_twice", 2 * 2 * NT * P), s=2, m=2, t=NT, n=P); o += 16 * NT * P
    vr = view(place.at(o, "v_raw", 2 * NT * P), s=2, t=NT, n=P); o += 8 * NT * P
    probs = view(place.at(o, "probs", 4 * SEQ), s=4, n=SEQ); o += 16 * SEQ
    asum = view(place.at(o, "a_sum", 2 * SEQ), s=2, n=SEQ); o += 8 * SEQ
    ath = view(place.at(o, "a_hi", 4 * SEQ, F32R), s=2, k=NT, q=2 * P); o += 16 * SEQ
    atl = view(place.at(o, "a_lo", 4 * SEQ, F32R), s=2, k=NT, q=2 * P); o += 16 * SEQ
    ot = view(place.at(R_OT, "o_transposed", 2 * P), q=2, n=P)
    cb = place.at(o, "gate_sums", SEQ, F32R); o += 4 * SEQ
    selh = view(place.at(o, "sel_head", MAPS * P, F32R), h=MAPS, n=P); o += 4 * MAPS * P
    cmask = place.at(o, "mask_bf", P, BF16); o += 2 * P
    cid = place.at(o, "ident_bf", P, BF16); o += 2 * P
    stat = view(place.at(o, "stat", 8 * 8), s=8, c=8); o += 256
    assert o <= 212800
    craw = asum[:, 0, 0:2 * P]
    selraw = probs[:, 3, :]
    lft, csum, ones = probs[0:MAPS, 0, :], probs[0:MAPS, 1, :], probs[0:MAPS, 2, :]
    PS = io["PS"]
    sem = lambda n: io["ctx"].enter_context(nc.semaphore("b_" + n))
    load_in = [sem("load_in0"), sem("load_in1")]
    consts_in, consts_done, ones_done, lft_done, cb_step = map(sem, ["consts_in", "consts_done", "ones_done", "lft_done", "cb_step"])
    t_done, t_hi, t_lo, v_hi_done, v_ready = map(sem, ["t_done", "t_hi", "t_lo", "v_hi_done", "v_ready"])
    zero_done, pv_copy, ot_done = map(sem, ["zero_done", "pv_copy", "ot_done"])
    qk_done, max_step, max_done, exp_done, a_step, a_ready, pv_done, o_done = map(
        sem, ["qk_done", "max_step", "max_done", "exp_done", "a_step", "a_ready", "pv_done", "o_done"])

    UNITS = 8
    jobs = [(u, 2 * g + t, maps) for u in range(UNITS) for g in range(NT // 2)
            for maps in ([(0, 1)] if u < 4 else [(0,), (1,)]) for t in range(2)]
    NJ = len(jobs)
    first_job = [8 * u if u < 4 else 32 + 16 * (u - 4) for u in range(UNITS + 1)]
    maps_before = [0]
    for _, _, maps in jobs:
        maps_before.append(maps_before[-1] + len(maps))
    blocks_of = lambda t: [(c, min(4, t + 1 - c)) for c in range(0, t + 1, 4)]

    def prep_at(J):
        u = jobs[J][0]
        n = J - first_job[u]
        if u + 1 == UNITS or (u >= 4 and n % 2):
            return None
        return n if u < 4 else n // 2
    t_end, p_end, nb = [0] * NJ, [8] + [0] * (UNITS - 1), 8
    for J in range(NJ + 1):
        if J < NJ and prep_at(J) is not None:
            nb += 1
            p_end[jobs[J][0] + 1] = nb
        if J >= 1:
            nb += len(blocks_of(jobs[J - 1][1]))
            t_end[J - 1] = nb

    def sources(u):
        if u < 4:
            return io["q_dram"], u * P, io["o_dk"], io["o_dv"], u * P
        return io["q_dram"], u * P, io["o_fk"], io["o_fv"], (u - 4) * P

    def prep_batch(n):
        return n // 4, n // 2 % 2, n % 2

    with nc.Block() as block:

        @block.sync
        def _(sp):
            sp.dma_start(craw, io["consts"][:, C_ID:C_ID + 2 * P]).then_inc(consts_in, 16)
            sp.dma_start(selraw, io["consts"][:, C_SELH:C_SELH + MAPS * P]).then_inc(consts_in, 16)
            for u in range(UNITS):
                if u >= 2:
                    sp.wait_ge(t_done, p_end[u - 2])
                    sp.wait_ge(v_ready, u - 1)
                q, qc, k, v, kc = sources(u)
                for m in range(2):
                    for twice in range(2):
                        for dst, src, c in ((kd, k, kc), (qd, q, qc)):
                            sp.dma_start(dst[:, u % 2, m, :, twice * HD:(twice + 1) * HD],
                                         src[:, c + m * HD:c + (m + 1) * HD].rearrange("(t p) c -> p t c", p=P)).then_inc(load_in[u % 2], 16)
                sp.dma_start(vr[:, u % 2, :, :], v[:, kc:kc + P].rearrange("(t p) c -> p t c", p=P)).then_inc(load_in[u % 2], 16)

        @block.gpsimd
        def _(pool):
            pool.memset(cb[:, :].bitcast(F32), 0.0).then_inc(ones_done, 1)
            pool.memset(ones, 1.0).then_inc(ones_done, 1)
            for G in range(NJ // 2):
                u, t, _ = jobs[2 * G]
                if G >= 2:
                    pool.wait_ge(pv_done, G - 1)
                for x in (ath, atl):
                    pool.memset(x[:, G % 2, t + 1, 0:P].bitcast(F32), 0.0).then_inc(zero_done, 1)
                n = 2 * G - first_job[u]
                if G and n != (4 if u < 4 else 6):
                    continue
                u = u + 1 if G else 0
                if u == UNITS:
                    continue
                pool.wait_ge(v_hi_done, u + 1)
                pool.tensor_tensor(vl[:, u % 2, :, :], vr[:, u % 2, :, :], vh[:, u % 2, :, :].bitcast(F32), ALU.subtract).then_inc(v_ready, 1)

        def hi_dst(n, u):
            kind, m, half = prep_batch(n)
            return (ks, qh)[kind][:, u % 2, m, half * 512:(half + 1) * 512]

        @block.scalar
        def _(act):
            b = 0
            act.wait_ge(consts_in, 32)
            act.activation(cid[:, :], craw[:, 0:P], ACT.Copy).then_inc(consts_done, 1)
            act.activation(cmask[:, :], craw[:, P:2 * P], ACT.Copy).then_inc(consts_done, 1)
            act.activation(selh[:, :, :], selraw.rearrange("p (h n) -> p h n", n=P), ACT.Copy).then_inc(consts_done, 1)

            def prep_hi(n, u):
                nonlocal b
                act.wait_ge(t_done, b + 1)
                if n == 0 and u >= 2:
                    act.wait_ge(qk_done, maps_before[first_job[u - 1]])
                act.activation(hi_dst(n, u), PS[:, 4 + b % 3, :], ACT.Copy).then_inc(t_hi, 1)
                b += 1

            def v_hi(u):
                act.wait_ge(load_in[u % 2], 16 * 9 * (u // 2 + 1))
                if u >= 2:
                    act.wait_ge(pv_done, first_job[u - 1] // 2)
                act.activation(vh[:, u % 2, :, :], vr[:, u % 2, :, :], ACT.Copy).then_inc(v_hi_done, 1)

            def evac(G):
                w = P if jobs[2 * G][0] < 4 else HD
                act.wait_ge(pv_done, G + 1)
                if G:
                    act.wait_ge(ot_done, G)
                act.activation(ot[0:w, :, :].rearrange("p q n -> p (q n)"), PS[0:w, 7, 0:2 * P], ACT.Copy).then_inc(pv_copy, 1)

            for n in range(8):
                prep_hi(n, 0)
            v_hi(0)
            for J in range(NJ + 3):
                if J < NJ and prep_at(J) is not None:
                    prep_hi(prep_at(J), jobs[J][0] + 1)
                if 1 <= J <= NJ:
                    G, half = divmod(J - 1, 2)
                    for c, nblk in blocks_of(jobs[J - 1][1]):
                        act.wait_ge(t_done, b + 1)
                        if G >= 2:
                            act.wait_ge(pv_done, G - 1)
                        act.activation(ath[:, G % 2, c:c + nblk, half * P:(half + 1) * P],
                                       PS[:, 4 + b % 3, 0:nblk * P].rearrange("p (k q) -> p k q", q=P), ACT.Copy).then_inc(t_hi, 1)
                        b += 1
                if J < NJ:
                    u, t, maps = jobs[J]
                    for m in maps:
                        M = maps_before[J] + (m if u < 4 else 0)
                        n = (t + 1) * P
                        act.wait_ge(max_done, M + 1)
                        if J >= 2:
                            act.wait_ge(t_done, t_end[J - 2])
                            if jobs[J - 2][0] < 4:
                                act.wait_ge(a_ready, J - 1)
                        k = m if u < 4 else 0
                        act.activation(probs[:, 2 * (J % 2) + k, 0:n], PS[:, 2 * (M % 2):2 * (M % 2) + 2, :].rearrange("p b c -> p (b c)")[:, 0:n],
                                       ACT.Exp, bias=stat[:, J % 8, k:k + 1], scale=SCALE,
                                       accum_out=stat[:, J % 8, 2 + k:3 + k]).then_inc(exp_done, 1)
                    if J - first_job[u] == 4 and u + 1 < UNITS:
                        v_hi(u + 1)
                if J >= 3 and J % 2:
                    evac((J - 3) // 2)

        @block.vector
        def _(dve):
            b = 0
            steps = [0, 0, 0]

            def step(n, s, ins):
                ins.then_inc(s, 1)
                steps[n] += 1
                dve.wait_ge(s, steps[n])

            dve.wait_ge(lft_done, 1)
            step(0, cb_step, dve.tensor_copy(lft, PS[0:MAPS, 0:2, :].rearrange("p b c -> p (b c)")))
            dve.wait_ge(ones_done, 2)
            step(0, cb_step, dve.tensor_tensor_scan(csum, ones, lft, 0.0, ALU.mult, ALU.add))
            step(0, cb_step, dve.tensor_scalar(csum, csum, -1.0 / SCALE, None, ALU.mult))
            step(0, cb_step, dve.tensor_copy(cb[0:MAPS, :], csum))
            step(0, cb_step, dve.tensor_tensor(cb[LO_ROW:LO_ROW + MAPS, :], csum, cb[0:MAPS, :].bitcast(F32), ALU.subtract))

            def prep_lo(n, u):
                nonlocal b
                kind, m, half = prep_batch(n)
                dve.wait_ge(t_hi, b + 1)
                src, cols = PS[:, 4 + b % 3, :], slice(half * 512, (half + 1) * 512)
                if kind == 0:
                    dst = ks[HD:, u % 2, m, cols]
                    dve.tensor_tensor(dst, src[HD:, :], dst.bitcast(F32), ALU.subtract).then_inc(t_lo, 1)
                else:
                    dve.tensor_tensor(ql[:, u % 2, m, cols], src, qh[:, u % 2, m, cols].bitcast(F32), ALU.subtract).then_inc(t_lo, 1)
                b += 1

            for n in range(8):
                prep_lo(n, 0)
            def rows_out(G):
                u, t, maps = jobs[2 * G]
                w = P if u < 4 else HD
                c = u * P + (0 if u < 4 else maps[0] * HD)
                dve.wait_ge(ot_done, G + 1)
                for half in range(2):
                    dve.tensor_scalar(o_all[:, t + half, c:c + w], PS[:, 7, (2 + half) * P:(2 + half) * P + w],
                                      stat[:, (2 * G + half) % 8, 4:5], None, ALU.mult).then_inc(o_done, 1)

            for J in range(NJ + 4):
                if 1 <= J <= NJ and jobs[J - 1][0] < 4:
                    st = stat[:, (J - 1) % 8, :]
                    n = (jobs[J - 1][1] + 1) * P
                    dve.wait_ge(exp_done, maps_before[J])
                    step(1, a_step, dve.reciprocal(st[:, 4:6], st[:, 2:4]))
                    step(1, a_step, dve.scalar_tensor_tensor(st[:, 6:7], st[:, 2:3], neg_lam, st[:, 5:6], ALU.mult, ALU.mult))
                    if J >= 3:
                        dve.wait_ge(t_done, t_end[J - 3])
                    p0 = 2 * ((J - 1) % 2)
                    dve.scalar_tensor_tensor(asum[:, (J - 1) % 2, 0:n], probs[:, p0 + 1, 0:n], st[:, 6:7], probs[:, p0, 0:n],
                                             ALU.mult, ALU.add).then_inc(a_ready, 1)
                if J < NJ:
                    u, t, maps = jobs[J]
                    n = (t + 1) * P
                    for m in maps:
                        M = maps_before[J] + (m if u < 4 else 0)
                        k = m if u < 4 else 0
                        dve.wait_ge(qk_done, M + 1)
                        if J >= 4:
                            dve.wait_ge(exp_done, maps_before[J - 3])
                        step(2, max_step, dve.tensor_reduce(stat[:, J % 8, 6 + k:7 + k], PS[:, 2 * (M % 2):2 * (M % 2) + 2, :].rearrange("p b c -> p (b c)")[:, 0:n],
                                                            AX, ALU.max))
                        dve.tensor_scalar(stat[:, J % 8, k:k + 1], stat[:, J % 8, 6 + k:7 + k], -SCALE, None, ALU.mult).then_inc(max_done, 1)
                    n = prep_at(J)
                    if n is not None:
                        prep_lo(n, u + 1)
                if 1 <= J <= NJ:
                    for c, nblk in blocks_of(jobs[J - 1][1]):
                        dve.wait_ge(t_hi, b + 1)
                        G, half = divmod(J - 1, 2)
                        sl = (slice(None), G % 2, slice(c, c + nblk), slice(half * P, (half + 1) * P))
                        dve.tensor_tensor(atl[sl], PS[:, 4 + b % 3, 0:nblk * P].rearrange("p (k q) -> p k q", q=P), ath[sl].bitcast(F32),
                                          ALU.subtract).then_inc(t_lo, 1)
                        b += 1
                if 1 <= J <= NJ and jobs[J - 1][0] >= 4:
                    dve.wait_ge(exp_done, maps_before[J])
                    dve.reciprocal(stat[:, (J - 1) % 8, 4:5], stat[:, (J - 1) % 8, 2:3]).then_inc(a_ready, 1)
                if J >= 4 and J % 2 == 0:
                    rows_out((J - 4) // 2)

        @block.tensor
        def _(pe):
            b = 0
            for t in range(NT):
                ins = pe.transpose(PS[0:MAPS, t // 4, t % 4 * P:t % 4 * P + P], f_sb[:, t * MAPS:(t + 1) * MAPS], ident[:, :])
            ins.then_inc(lft_done, 1)
            pe.wait_ge(consts_done, 3)

            def bank():
                if b >= 3:
                    pe.wait_ge(t_lo, b - 2)
                return PS[:, 4 + b % 3, :]

            def prep(n, u):
                nonlocal b
                kind, m, half = prep_batch(n)
                if n == 0:
                    pe.wait_ge(load_in[u % 2], 16 * 9 * (u // 2 + 1))
                dst = bank()
                for c in range(4):
                    ins = pe.transpose(dst[:, c * P:(c + 1) * P], (kd, qd)[kind][:, u % 2, m, 4 * half + c, :], ident[:, :])
                ins.then_inc(t_done, 1)
                b += 1

            def qk(J):
                u, t, maps = jobs[J]
                s = u % 2
                if J == first_job[u]:
                    pe.wait_ge(t_lo, p_end[u])
                for m in maps:
                    M = maps_before[J] + (m if u < 4 else 0)
                    if M >= 2:
                        pe.wait_ge(exp_done, M - 1)
                    elif M == 0:
                        pe.wait_ge(cb_step, 5)
                    rows = slice(t * P, (t + 1) * P)
                    for half in range(t // 4 + 1):
                        n = min(512, (t + 1) * P - half * 512)
                        w = max(n, 2 * P)
                        keys = slice(half * 512, half * 512 + w)
                        dst = PS[:, 2 * (M % 2) + half, :]
                        pe.matmul(dst[:, 0:w], qh[:, s, m, rows], ks[:, s, m, keys], start=True, stop=False, skip_group_check=True)
                        if half == t // 4:
                            pe.matmul(dst[:, n - P:n], cid[:, :], cmask[:, :], start=False, stop=False, skip_group_check=True)
                        if u >= 4:
                            pe.matmul(dst[:, 0:w], selh[:, 2 * (u - 4) + m, :], cb[:, keys], start=False, stop=False, skip_group_check=True)
                        ins = pe.matmul(dst[:, 0:w], ql[:, s, m, rows], ks[:, s, m, keys], start=False, stop=True, skip_group_check=True)
                    ins.then_inc(qk_done, 1)

            def turn(J):
                nonlocal b
                u, t, maps = jobs[J]
                if u < 4:
                    pe.wait_ge(a_ready, J + 1)
                else:
                    pe.wait_ge(exp_done, maps_before[J + 1])
                src = asum[:, J % 2, :] if u < 4 else probs[:, 2 * (J % 2), :]
                for c, nblk in blocks_of(t):
                    dst = bank()
                    for k in range(nblk):
                        ins = pe.transpose(dst[:, k * P:(k + 1) * P], src[:, (c + k) * P:(c + k + 1) * P], ident[:, :])
                    ins.then_inc(t_done, 1)
                    b += 1

            def pv(G):
                u, t, maps = jobs[2 * G]
                pe.wait_ge(t_lo, t_end[2 * G + 1])
                pe.wait_ge(zero_done, 2 * G + 2)
                if 2 * G == first_job[u]:
                    pe.wait_ge(v_ready, u + 1)
                if G:
                    pe.wait_ge(o_done, 2 * G)
                w = P if u < 4 else HD
                c = 0 if u < 4 else maps[0] * HD
                for k in range(t + 2):
                    for n, (v, x) in enumerate(((vh, ath), (vh, atl), (vl, ath))):
                        ins = pe.matmul(PS[0:w, 7, 0:2 * P], v[:, u % 2, k, c:c + w], x[:, G % 2, k, :],
                                        start=(k == 0 and n == 0), stop=(k == t + 1 and n == 2))
                ins.then_inc(pv_done, 1)

            def turn_back(G):
                w = P if jobs[2 * G][0] < 4 else HD
                pe.wait_ge(pv_copy, G + 1)
                for half in range(2):
                    ins = pe.transpose(PS[:, 7, (2 + half) * P:(2 + half) * P + w], ot[0:w, half, :], ident[0:w, 0:w])
                ins.then_inc(ot_done, 1)

            for n in range(8):
                prep(n, 0)
            for J in range(NJ + 4):
                if J < NJ:
                    qk(J)
                    n = prep_at(J)
                    if n is not None:
                        prep(n, jobs[J][0] + 1)
                if 1 <= J <= NJ:
                    turn(J - 1)
                if J >= 4 and J % 2 == 0:
                    turn_back((J - 4) // 2)
                if J >= 3 and J % 2 and J - 3 < NJ:
                    pv((J - 3) // 2)


def merge(nc, io, place):
    ident = place.at(R_ID, "ident", P)
    ht_hi = view(place.at(R_HI, "ht_hi", KC * TOK, F32R), k=KC, t=TOK)
    ht_lo = view(place.at(R_LO, "ht_lo", KC * TOK, F32R), k=KC, t=TOK)
    osamp = place.at(R_OS, "o_sample", 2 * GRP)
    o = R_FREE
    o_all = view(place.at(o, "o_all", NT * D), t=NT, n=D); o += 4 * NT * D
    w_hi = view(place.at(o, "wo_hi", KC * D, F32R), k=KC, n=D); o += 4 * KC * D
    w_lo = view(place.at(o, "wo_lo", KC * D, F32R), k=KC, n=D); o += 4 * KC * D
    hsp = view(place.at(o, "o_sample_t", KC * P, F32R), k=KC, m=P)
    raw = view(place.at(o, "wo_raw", 2 * 512), s=2, n=512); o += 4 * KC * P
    sq = place.at(o, "squares", GRP); o += 4 * GRP
    xr = view(place.at(o, "x_residual", 2 * D), s=2, n=D); o += 8 * D
    yb = view(place.at(o, "y", 2 * D), s=2, n=D); o += 8 * D
    x2 = place.at(o, "x2", D); o += 4 * D
    h = place.at(o, "h", D); o += 4 * D
    g_post = place.at(o, "g_post", D); o += 4 * D
    g_pre = place.at(o, "g_pre", D); o += 4 * D
    g_sub = place.at(o, "g_sub", P); o += 4 * P
    st = view(place.at(o, "stat", 32 * 4), k=4, c=32); o += 512
    assert o <= 212800, o
    PS = io["PS"]
    sem = lambda n: io["ctx"].enter_context(nc.semaphore("c_" + n))
    consts_in, consts_done, zeroed, w_hi_done, w_lo_done = map(sem, ["consts_in", "consts_done", "zeroed", "w_hi_done", "w_lo_done"])
    raw_in, x_in = [[sem(f"{n}{s}") for s in range(2)] for n in ("raw_in", "x_in")]
    a_step, a_sum, a_rstd, a_norm = map(sem, ["a_step", "a_sum", "a_rstd", "a_norm"])
    pool_step, t_done, t_hi, t_lo, b_done = map(sem, ["pool_step", "t_done", "t_hi", "t_lo", "b_done"])
    y_copy, y_low, y_ready, y_sq, y_rstd, c_step, x2_done, x2_stored, x2_sq, x2_rstd, h_done = map(
        sem, ["y_copy", "y_low", "y_ready", "y_sq", "y_rstd", "c_step", "x2_done", "x2_stored", "x2_sq", "x2_rstd", "h_done"])
    NS = NT + 1
    rows = lambda t: P if t < NT else DB
    attn = lambda t: o_all[:, t, :] if t < NT else osamp[0:DB, :]
    a_batch = {0: 0}
    h_batch, nb = {}, 2
    for t in range(NS + 1):
        if t + 1 < NS:
            a_batch[t + 1] = nb
            nb += 2
        if t >= 1:
            h_batch[t - 1] = nb
            nb += 2
    wo_v = io["w_o"].rearrange("(k p) n -> p k n", p=P)
    NW = 2 * KC

    with nc.Block() as block:

        @block.sync
        def _(sp):
            sp.dma_start(g_sub[:, :], io["subln_g"].to_broadcast([P, P])).then_inc(consts_in, 16)
            sp.dma_start(g_post[:, :], io["attn_post_g"].to_broadcast([P, D])).then_inc(consts_in, 16)
            sp.dma_start(g_pre[:, :], io["ffn_pre_g"].to_broadcast([P, D])).then_inc(consts_in, 16)
            for q in range(NW):
                if q >= 2:
                    sp.wait_ge(w_lo_done, q - 1)
                sp.dma_start(raw[:, q % 2, :], wo_v[:, q // 2, q % 2 * 512:q % 2 * 512 + 512]).then_inc(raw_in[q % 2], 16)
            for t in range(NS + 1):
                if t < NS:
                    if t >= 2:
                        sp.wait_ge(x2_done, t - 1)
                    src = io["x"][t * P:(t + 1) * P, :] if t < NT else io["xs"]
                    sp.dma_start(xr[0:rows(t), t % 2, :], src).then_inc(x_in[t % 2], 16)
                if t >= 1:
                    u = t - 1
                    sp.wait_ge(x2_done, u + 1)
                    sp.dma_start(io["x2_dram"][u * P:u * P + rows(u), :], x2[0:rows(u), :]).then_inc(x2_stored, 16)
            sp.wait_ge(x2_stored, 16 * NS)

        @block.gpsimd
        def _(pool):
            n_step = 0

            def rstd(k, t, c, width, done):
                nonlocal n_step
                n = rows(t)
                cs = slice(c, c + (4 if k == 0 else 1))
                pool.tensor_scalar(st[0:n, 1, cs], st[0:n, 0, cs], 1.0 / width, EPS, ALU.mult, ALU.add).then_inc(pool_step, 1)
                n_step += 1
                pool.wait_ge(pool_step, n_step)
                pool.tensor_tensor(st[0:n, 2, cs], st[0:n, 1, cs], st[0:n, 3, cs], ALU.pow).then_inc(done, 1)

            pool.memset(st[:, 3, :], -0.5).then_inc(zeroed, 1)
            pool.wait_ge(w_lo_done, NW)
            pool.memset(hsp.bitcast(F32), 0.0).then_inc(zeroed, 1)
            pool.wait_ge(zeroed, 2)
            for t in range(-1, NS + 1):
                if t + 1 < NS:
                    pool.wait_ge(a_sum, t + 2)
                    rstd(0, t + 1, 4 * ((t + 1) % 2), P, a_rstd)
                if 1 <= t:
                    pool.wait_ge(y_sq, t)
                    rstd(1, t - 1, 8 + (t - 1) % 2, D, y_rstd)
                    pool.wait_ge(x2_sq, t)
                    rstd(1, t - 1, 10 + (t - 1) % 2, D, x2_rstd)

        @block.scalar
        def _(act):
            b = 0

            def hi(t, dst_of):
                nonlocal b
                n = rows(t)
                for half in range(2):
                    act.wait_ge(t_done, b + 1)
                    src = PS[:, 4 + b % 4, 0:4 * n].rearrange("p (k n) -> p k n", n=n)
                    act.activation(dst_of(half), src, ACT.Copy).then_inc(t_hi, 1)
                    b += 1

            for q in range(NW):
                act.wait_ge(raw_in[q % 2], 16 * (q // 2 + 1))
                act.activation(w_hi[:, q // 2, q % 2 * 512:q % 2 * 512 + 512], raw[:, q % 2, :], ACT.Copy).then_inc(w_hi_done, 1)
            for t in range(-1, NS + 1):
                u = t - 1
                if u >= 0:
                    n = rows(u)
                    act.wait_ge(b_done, u + 1)
                    if u >= 2:
                        act.wait_ge(x2_done, u - 1)
                    psum = PS[:, 2 * (u % 2):2 * (u % 2) + 2, :]
                    act.activation(yb[0:n, u % 2, :].rearrange("p (b c) -> p b c", b=2), psum[0:n], ACT.Copy).then_inc(y_copy, 1)
                    if u == NT:
                        act.activation(yb[0:n, 1 - u % 2, :].rearrange("p (b c) -> p b c", b=2), psum[LO_ROW:LO_ROW + DB], ACT.Copy).then_inc(y_low, 1)
                        act.wait_ge(y_ready, 1)
                    act.wait_ge(y_copy, u + 1)
                    if u:
                        act.wait_ge(x2_stored, 16 * u)
                        act.wait_ge(h_done, u)
                        act.wait_ge(x2_sq, u)
                    act.activation(x2[0:n, :], yb[0:n, u % 2, :], ACT.Square, accum_out=st[0:n, 0, 8 + u % 2:9 + u % 2]).then_inc(y_sq, 1)
                if t + 1 < NS:
                    v = t + 1
                    if v == NT:
                        act.wait_ge(zeroed, 2)
                    hi(v, (lambda half: ht_hi[:, 4 * half:4 * half + 4, v * P:(v + 1) * P]) if v < NT else
                       (lambda half: hsp[:, 4 * half:4 * half + 4, 0:DB]))
                if u >= 0:
                    act.wait_ge(x2_done, u + 1)
                    if u:
                        act.wait_ge(t_done, h_batch[u - 1] + 2)
                    act.activation(h[0:n, :], x2[0:n, :], ACT.Square, accum_out=st[0:n, 0, 10 + u % 2:11 + u % 2]).then_inc(x2_sq, 1)
                    hi(u, lambda half: ht_hi[:, 4 * half:4 * half + 4, u * P:u * P + n])

        @block.vector
        def _(dve):
            b = 0
            n_a, n_c = 0, 0

            def lo(t, hi_of, dst_of):
                nonlocal b
                n = rows(t)
                for half in range(2):
                    dve.wait_ge(t_hi, b + 1)
                    src = PS[:, 4 + b % 4, 0:4 * n].rearrange("p (k n) -> p k n", n=n)
                    dve.tensor_tensor(dst_of(half), src, hi_of(half).bitcast(F32), ALU.subtract).then_inc(t_lo, 1)
                    b += 1

            dve.wait_ge(consts_in, 48)
            dve.tensor_scalar(g_sub[:, :], g_sub[:, :], 1.0 - LAM_INIT, None, ALU.mult).then_inc(consts_done, 1)
            for q in range(NW):
                dve.wait_ge(w_hi_done, q + 1)
                sl = (slice(None), q // 2, slice(q % 2 * 512, q % 2 * 512 + 512))
                dve.tensor_tensor(w_lo[sl], raw[:, q % 2, :], w_hi[sl].bitcast(F32), ALU.subtract).then_inc(w_lo_done, 1)
            dve.wait_ge(consts_done, 1)
            for t in range(-1, NS + 1):
                u, v = t - 1, t + 1
                if v < NS:
                    n = rows(v)
                    src = attn(v)[:, 0:GRP]
                    c = 4 * (v % 2)
                    dve.tensor_tensor(sq[0:n, :], src, src, ALU.mult).then_inc(a_step, 1)
                    n_a += 1
                    dve.wait_ge(a_step, n_a)
                    dve.tensor_reduce(st[0:n, 0, c:c + 4], sq[0:n, :].rearrange("p (h c) -> p h c", h=4), AX, ALU.add).then_inc(a_sum, 1)
                if u >= 0:
                    m = rows(u)
                    if u == NT:
                        dve.wait_ge(y_copy, NS)
                        dve.wait_ge(y_low, 1)
                        dve.tensor_tensor(yb[0:m, u % 2, :], yb[0:m, u % 2, :], yb[0:m, 1 - u % 2, :], ALU.add).then_inc(y_ready, 1)
                    dve.wait_ge(y_rstd, u + 1)
                    dve.scalar_tensor_tensor(x2[0:m, :], yb[0:m, u % 2, :], st[0:m, 2, 8 + u % 2:9 + u % 2], g_post[0:m, :], ALU.mult, ALU.mult).then_inc(c_step, 1)
                    n_c += 1
                    dve.wait_ge(c_step, n_c)
                    dve.wait_ge(x_in[u % 2], 16 * (u // 2 + 1))
                    dve.tensor_tensor(x2[0:m, :], x2[0:m, :], xr[0:m, u % 2, :], ALU.add).then_inc(x2_done, 1)
                if v < NS:
                    dve.wait_ge(a_rstd, v + 1)
                    s3 = src.rearrange("p (h c) -> p h c", h=4)
                    dve.tensor_tensor(s3, s3, st[0:n, 2, c:c + 4].rearrange("p (h c) -> p h c", c=1).to_broadcast([n, 4, P]), ALU.mult).then_inc(a_step, 1)
                    n_a += 1
                    dve.wait_ge(a_step, n_a)
                    dve.tensor_tensor(s3, s3, g_sub[0:n, :].rearrange("p (h c) -> p h c", h=1).to_broadcast([n, 4, P]), ALU.mult).then_inc(a_norm, 1)
                    if v < NT:
                        cols = slice(v * P, (v + 1) * P)
                        lo(v, lambda half: ht_hi[:, 4 * half:4 * half + 4, cols], lambda half: ht_lo[:, 4 * half:4 * half + 4, cols])
                    else:
                        lo(v, lambda half: hsp[:, 4 * half:4 * half + 4, 0:DB], lambda half: hsp[:, 4 * half:4 * half + 4, LO_ROW:LO_ROW + DB])
                if u >= 0:
                    dve.wait_ge(x2_rstd, u + 1)
                    dve.scalar_tensor_tensor(h[0:m, :], x2[0:m, :], st[0:m, 2, 10 + u % 2:11 + u % 2], g_pre[0:m, :], ALU.mult, ALU.mult).then_inc(h_done, 1)
                    cu = slice(u * P, u * P + m)
                    lo(u, lambda half: ht_hi[:, 4 * half:4 * half + 4, cu], lambda half: ht_lo[:, 4 * half:4 * half + 4, cu])

        @block.tensor
        def _(pe):
            b = 0

            def turn(t, src):
                nonlocal b
                n = rows(t)
                for half in range(2):
                    if b >= 4:
                        pe.wait_ge(t_lo, b - 3)
                    for k in range(4):
                        c = (4 * half + k) * P
                        ins = pe.transpose(PS[:, 4 + b % 4, k * n:k * n + n], src[:, c:c + P], ident[0:n, 0:n])
                    ins.then_inc(t_done, 1)
                    b += 1

            for t in range(-1, NS + 1):
                if t + 1 < NS:
                    pe.wait_ge(a_norm, t + 2)
                    turn(t + 1, attn(t + 1))
                if 0 <= t < NS:
                    if t == 0:
                        pe.wait_ge(w_lo_done, NW)
                    pe.wait_ge(t_lo, a_batch[t] + 2)
                    if t >= 2:
                        pe.wait_ge(y_copy, t - 1)
                    parts = ([(ht_hi, w_hi), (ht_hi, w_lo), (ht_lo, w_hi)] if t < NT else [(hsp, w_hi), (hsp, w_lo)])
                    for half in range(2):
                        for k in range(KC):
                            for n, (a, w) in enumerate(parts):
                                at = a[:, k, t * P:(t + 1) * P] if t < NT else a[:, k, :]
                                ins = pe.matmul(PS[:, 2 * (t % 2) + half, :], at, w[:, k, half * 512:half * 512 + 512],
                                                start=(n == 0 and k == 0), stop=(n == len(parts) - 1 and k == KC - 1))
                    ins.then_inc(b_done, 1)
                if t >= 1:
                    pe.wait_ge(h_done, t)
                    turn(t - 1, h[0:rows(t - 1), :])


def ffn(nc, io, place):
    ident = place.at(R_ID, "ident", P)
    ht_hi = view(place.at(R_HI, "ht_hi", KC * TOK, F32R), k=KC, t=TOK)
    ht_lo = view(place.at(R_LO, "ht_lo", KC * TOK, F32R), k=KC, t=TOK)
    o = R_OS
    acc = view(place.at(o, "acc", KC * TOK), d=KC, t=TOK)
    rows_in = place.at(o, "rows_in", FF); o += 4 * KC * TOK
    a_hi = view(place.at(o, "act_hi", 4 * TOK, F32R), s=4, t=TOK); o += 16 * TOK
    a_lo = view(place.at(o, "act_lo", 4 * TOK, F32R), s=4, t=TOK); o += 16 * TOK
    WR = 3
    w_hi = view(place.at(o, "wgu_hi", WR * KC * P, F32R), s=WR, k=KC, n=P); o += 4 * WR * KC * P
    w_lo = view(place.at(o, "wgu_lo", WR * KC * P, F32R), s=WR, k=KC, n=P); o += 4 * WR * KC * P
    raw = view(place.at(o, "wgu_raw", 2 * KC * P), s=2, k=KC, n=P); o += 8 * KC * P
    wd_hi = view(place.at(o, "wd_hi", 2 * D, F32R), s=2, n=D); o += 8 * D
    wd_lo = view(place.at(o, "wd_lo", 2 * D, F32R), s=2, n=D); o += 8 * D
    wd_raw = view(place.at(o, "wd_raw", 2 * 512), s=2, n=512); o += 4 * 2 * 512
    GW = TOK + 8
    gb = view(place.at(o, "gate", 2 * GW), s=2, t=GW); o += 8 * GW
    cbuf = view(place.at(o, "conv", 2 * TOK), s=2, t=TOK); o += 8 * TOK
    NR = 2 * DB + 4
    cst = view(place.at(o, "conv_consts", FC * NR), f=FC, r=NR); o += 4 * FC * NR
    tails = view(place.at(o, "gate_tails", FC * (DB + 2)), f=FC, r=DB + 2); o += 896
    stat = view(place.at(o, "stat", 4 * 16), k=4, c=16); o += 256
    assert o <= 212800, o
    state = cst[:, :, 0:2 * DB].rearrange("p f (b j) -> p f b j", j=2)
    taps = [cst[:, :, 2 * DB + j] for j in range(3)]
    bias = cst[:, :, 2 * DB + 3]
    e = 0
    yb = view(place.at(e, "y_rows", 2 * D), s=2, n=D); e += 8 * D
    sq = place.at(e, "y_squares", D); e += 4 * D
    xr = view(place.at(e, "x2_rows", 2 * D), s=2, n=D); e += 8 * D
    out = view(place.at(e, "out_rows", 2 * D), s=2, n=D); e += 8 * D
    tail_rows = place.at(e, "tail_rows", FF); e += 4 * FF
    g_post = place.at(e, "ffn_post", D); e += 4 * D
    assert e <= R_ID
    PS = io["PS"]
    sem = lambda n: io["ctx"].enter_context(nc.semaphore("e_" + n))
    raw_in, wd_in, x2_in, stored = [[sem(f"{n}{s}") for s in range(2)] for n in ("raw_in", "wd_in", "x2_in", "stored")]
    rows_ready, cst_t, cst_done, zeroed, gu_hi, gu_lo, wdh, wdl = map(
        sem, ["rows_ready", "cst_t", "cst_done", "zeroed", "gu_hi", "gu_lo", "wdh", "wdl"])
    gate_done, up_done, g_evac, c_init, conv_step, conv_done, gelu_done, mul_done, a_hi_done, a_lo_done, tail_done = map(
        sem, ["gate_done", "up_done", "g_evac", "c_init", "conv_step", "conv_done", "gelu_done", "mul_done", "a_hi_done", "a_lo_done", "tail_done"])
    down_done, acc_done, g_in, state_stored, tt_done, tt_copy, tails_stored = map(
        sem, ["down_done", "acc_done", "g_in", "state_stored", "tt_done", "tt_copy", "tails_stored"])
    t_done, y_copy, y_sq, y_step, y_rstd, n_done, out_done = map(
        sem, ["t_done", "y_copy", "y_sq", "y_step", "y_rstd", "n_done", "out_done"])
    NG = FC // 2
    NS = NT + 1
    PER = 3 * KC
    rows = lambda t: P if t < NT else DB
    third_of = lambda t: (t * P + rows(t) - 1) // THIRD
    wg_v = io["w_gate"].rearrange("(k p) n -> p k n", p=P)
    wu_v = io["w_up"].rearrange("(k p) n -> p k n", p=P)

    def down_halves(f):
        return [] if f < 2 else [2 * (f - 2), 2 * (f - 2) + 1]

    with nc.Block() as block:

        @block.sync
        def _(sp):
            sp.dma_start(rows_in[0:2 * DB, :], io["state_ffn_conv"].rearrange("b j n -> (b j) n")).then_inc(rows_ready, 16)
            sp.dma_start(rows_in[2 * DB:2 * DB + 3, :], io["conv_w"]).then_inc(rows_ready, 16)
            sp.dma_start(rows_in[2 * DB + 3:NR, :], io["conv_b"]).then_inc(rows_ready, 16)
            sp.dma_start(io["o_sconv"][:, 0, :], io["state_ffn_conv"][:, 1, :]).then_inc(state_stored, 16)

            def load_unit(q):
                if q >= 2:
                    sp.wait_ge(gu_lo, q - 1)
                f = q // 2
                sp.dma_start(raw[:, q % 2, :, :], (wg_v, wu_v)[q % 2][:, :, f * P:(f + 1) * P]).then_inc(raw_in[q % 2], 16)

            def load_down(q):
                if q >= 2:
                    sp.wait_ge(wdl, q - 1)
                sp.dma_start(wd_raw[:, q % 2, :], io["w_down"][q // 2 * P:(q // 2 + 1) * P, q % 2 * 512:q % 2 * 512 + 512]).then_inc(wd_in[q % 2], 16)

            load_unit(0)
            load_unit(1)
            for f in range(FC + 2):
                for q in (2 * f + 2, 2 * f + 3):
                    if q < 2 * FC:
                        load_unit(q)
                for q in down_halves(f):
                    load_down(q)
            sp.wait_ge(up_done, FC)
            sp.dma_start(g_post[:, :], io["ffn_post_g"].to_broadcast([P, D])).then_inc(g_in, 16)
            for t in range(NS + 1):
                if t < NS:
                    if t >= 2:
                        sp.wait_ge(out_done, t - 1)
                    sp.dma_start(xr[0:rows(t), t % 2, :], io["x2_dram"][t * P:t * P + rows(t), :]).then_inc(x2_in[t % 2], 16)
                if t >= 1:
                    u = t - 1
                    sp.wait_ge(out_done, u + 1)
                    dst = io["y"][u * P:(u + 1) * P, :] if u < NT else io["ys"]
                    sp.dma_start(dst, out[0:rows(u), u % 2, :]).then_inc(stored[u % 2], 16)
            sp.wait_ge(tt_copy, 6)
            sp.dma_start(io["o_conv"], tail_rows[0:2, :]).then_inc(tails_stored, 16)
            sp.dma_start(io["o_sconv"][:, 1, :], tail_rows[2:2 + DB, :]).then_inc(tails_stored, 16)
            sp.wait_ge(tails_stored, 32)
            sp.wait_ge(state_stored, 16)
            for s in range(2):
                sp.wait_ge(stored[s], 16 * ((NS + 1 - s) // 2))

        @block.gpsimd
        def _(pool):
            pool.memset(stat[:, 3, :], -0.5).then_inc(zeroed, 1)
            for s in range(2):
                pool.memset(gb[:, s, 0:2], 0.0).then_inc(zeroed, 1)

            def lo_unit(q):
                pool.wait_ge(gu_hi, q + 1)
                pool.tensor_tensor(w_lo[:, q % WR, :, :], raw[:, q % 2, :, :], w_hi[:, q % WR, :, :].bitcast(F32), ALU.subtract).then_inc(gu_lo, 1)

            lo_unit(0)
            lo_unit(1)
            for f in range(FC + 2):
                for q in (2 * f + 2, 2 * f + 3):
                    if q < 2 * FC:
                        lo_unit(q)
                for q in down_halves(f):
                    pool.wait_ge(wdh, q + 1)
                    sl = (slice(None), q // 2 % 2, slice(q % 2 * 512, q % 2 * 512 + 512))
                    pool.tensor_tensor(wd_lo[sl], wd_raw[:, q % 2, :], wd_hi[sl].bitcast(F32), ALU.subtract).then_inc(wdl, 1)
                if f < FC:
                    pool.wait_ge(g_evac, 3 * f + 3)
                    pool.tensor_copy(tails[:, f, :], gb[:, f % 2, SEQ:SEQ + DB + 2]).then_inc(tail_done, 1)
                    pool.wait_ge(a_hi_done, f + 1)
                    pool.tensor_tensor(a_lo[:, f % 4, :], cbuf[:, f % 2, :], a_hi[:, f % 4, :].bitcast(F32), ALU.subtract).then_inc(a_lo_done, 1)
            for t in range(NS):
                n = rows(t)
                pool.wait_ge(y_sq, t + 1)
                pool.tensor_scalar(stat[0:n, 1, t:t + 1], stat[0:n, 0, t:t + 1], 1.0 / D, EPS, ALU.mult, ALU.add).then_inc(y_step, 1)
                pool.wait_ge(y_step, t + 1)
                pool.tensor_tensor(stat[0:n, 2, t:t + 1], stat[0:n, 1, t:t + 1], stat[0:n, 3, t:t + 1], ALU.pow).then_inc(y_rstd, 1)

        @block.scalar
        def _(act):
            def hi_unit(q):
                act.wait_ge(raw_in[q % 2], 16 * (q // 2 + 1))
                if q >= WR:
                    r = q - WR
                    act.wait_ge((gate_done, up_done)[r % 2], r // 2 + 1)
                act.activation(w_hi[:, q % WR, :, :], raw[:, q % 2, :, :], ACT.Copy).then_inc(gu_hi, 1)

            hi_unit(0)
            hi_unit(1)
            for f in range(FC + 2):
                if 2 * f + 2 < 2 * FC:
                    hi_unit(2 * f + 2)
                if f < FC:
                    act.wait_ge(gate_done, f + 1)
                    if f >= 2:
                        act.wait_ge(conv_done, 2 * f - 2)
                        act.wait_ge(tail_done, f - 1)
                    if f == 0:
                        act.wait_ge(zeroed, 3)
                        act.wait_ge(cst_done, 1)
                    for i in range(3):
                        act.activation(gb[:, f % 2, 2 + i * THIRD:2 + (i + 1) * THIRD], PS[:, i, 0:THIRD], ACT.Copy).then_inc(g_evac, 1)
                if 2 * f + 3 < 2 * FC:
                    hi_unit(2 * f + 3)
                for q in down_halves(f):
                    act.wait_ge(wd_in[q % 2], 16 * (q // 2 + 1))
                    if q >= 4:
                        act.wait_ge(down_done, PER * (q // 4))
                    act.activation(wd_hi[:, q // 2 % 2, q % 2 * 512:q % 2 * 512 + 512], wd_raw[:, q % 2, :], ACT.Copy).then_inc(wdh, 1)
                if f >= FC:
                    continue
                act.wait_ge(g_evac, 3 * f + 3)
                if f >= 2:
                    act.wait_ge(a_lo_done, f - 1)
                act.activation(cbuf[:, f % 2, :], gb[:, f % 2, 2:2 + TOK], ACT.Identity, bias=bias[:, f:f + 1], scale=taps[2][:, f:f + 1]).then_inc(c_init, 1)
                act.wait_ge(conv_done, 2 * f + 2)
                act.activation(cbuf[:, f % 2, :], cbuf[:, f % 2, :], ACT.Gelu_apprx_tanh).then_inc(gelu_done, 1)
                act.wait_ge(mul_done, 3 * f + 3)
                if f >= 4:
                    act.wait_ge(down_done, PER * (f // 2 - 1))
                act.activation(a_hi[:, f % 4, :], cbuf[:, f % 2, :], ACT.Copy).then_inc(a_hi_done, 1)
            for t in range(NS):
                n = rows(t)
                act.wait_ge(t_done, t + 1)
                if t >= 2:
                    act.wait_ge(n_done, t - 1)
                act.activation(yb[0:n, t % 2, :].rearrange("p (b c) -> p b c", b=2), PS[0:n, 2 * (t % 2):2 * (t % 2) + 2, :], ACT.Copy).then_inc(y_copy, 1)
                act.wait_ge(y_copy, t + 1)
                if t:
                    act.wait_ge(y_sq, t)
                act.activation(sq[0:n, :], yb[0:n, t % 2, :], ACT.Square, accum_out=stat[0:n, 0, t:t + 1]).then_inc(y_sq, 1)

        @block.vector
        def _(dve):
            def sums(g):
                for n in range(PER):
                    i, d = divmod(n, KC)
                    k = g * PER + n
                    dve.wait_ge(down_done, k + 1)
                    if g:
                        dve.wait_ge(acc_done, k - PER + 1)
                    dst, src = acc[:, d, i * THIRD:(i + 1) * THIRD], PS[:, 6 + k % 2, 0:THIRD]
                    if g == 0:
                        dve.tensor_copy(dst, src).then_inc(acc_done, 1)
                    else:
                        dve.tensor_tensor(dst, src, dst, ALU.add).then_inc(acc_done, 1)

            dve.wait_ge(cst_t, 1)
            dve.tensor_copy(cst[:, :, :], PS[:, 6, 0:FC * NR].rearrange("p (f r) -> p f r", r=NR)).then_inc(cst_done, 1)
            dve.wait_ge(cst_done, 1)
            for f in range(FC):
                c, g = cbuf[:, f % 2, :], gb[:, f % 2, :]
                dve.wait_ge(c_init, f + 1)
                for j, back in ((1, 1), (0, 2)):
                    s = conv_step if j else conv_done
                    dve.scalar_tensor_tensor(c[:, 0:SEQ], g[:, 2 - back:2 - back + SEQ], taps[j][:, f:f + 1], c[:, 0:SEQ],
                                             ALU.mult, ALU.add).then_inc(s, 1)
                    dve.scalar_tensor_tensor(c[:, SEQ:], state[:, f, :, j], taps[j][:, f:f + 1], c[:, SEQ:],
                                             ALU.mult, ALU.add).then_inc(s, 1)
                    if j:
                        dve.wait_ge(conv_step, 2 * f + 2)
                dve.wait_ge(gelu_done, f + 1)
                dve.wait_ge(up_done, f + 1)
                for i in range(3):
                    cols = slice(i * THIRD, (i + 1) * THIRD)
                    dve.tensor_tensor(c[:, cols], PS[:, 3 + i, 0:THIRD], c[:, cols], ALU.mult).then_inc(mul_done, 1)
                if f % 2 and f > 2:
                    sums(f // 2 - 1)
            sums(NG - 1)
            dve.wait_ge(g_in, 16)
            for t in range(NS):
                n = rows(t)
                dve.wait_ge(y_rstd, t + 1)
                if t >= 2:
                    dve.wait_ge(stored[t % 2], 16 * (t // 2))
                dve.scalar_tensor_tensor(out[0:n, t % 2, :], yb[0:n, t % 2, :], stat[0:n, 2, t:t + 1], g_post[0:n, :], ALU.mult, ALU.mult).then_inc(n_done, 1)
                dve.wait_ge(n_done, t + 1)
                dve.wait_ge(x2_in[t % 2], 16 * (t // 2 + 1))
                dve.tensor_tensor(out[0:n, t % 2, :], out[0:n, t % 2, :], xr[0:n, t % 2, :], ALU.add).then_inc(out_done, 1)
            for n in range(6):
                w = min(4, FC - 4 * n) * P
                dve.wait_ge(tt_done, n + 1)
                dve.tensor_copy(tail_rows[0:DB + 2, 4 * n * P:4 * n * P + w], PS[0:DB + 2, 4 + n % 2, 0:w]).then_inc(tt_copy, 1)

        @block.tensor
        def _(pe):
            pe.wait_ge(rows_ready, 48)
            for f in range(FC):
                ins = pe.transpose(PS[:, 6, f * NR:(f + 1) * NR], rows_in[0:NR, f * P:(f + 1) * P], ident[0:NR, 0:NR])
            ins.then_inc(cst_t, 1)

            def unit(q):
                f, up = divmod(q, 2)
                s = q % WR
                pe.wait_ge(gu_lo, q + 1)
                for i in range(3):
                    if f:
                        pe.wait_ge((g_evac, mul_done)[up], 3 * (f - 1) + i + 1)
                    cols = slice(i * THIRD, (i + 1) * THIRD)
                    for k in range(KC):
                        for n, (w, a) in enumerate(((w_hi, ht_hi), (w_hi, ht_lo), (w_lo, ht_hi))):
                            ins = pe.matmul(PS[:, 3 * up + i, 0:THIRD], w[:, s, k, :], a[:, k, cols],
                                            start=(k == 0 and n == 0), stop=(k == KC - 1 and n == 2))
                ins.then_inc((gate_done, up_done)[up], 1)

            def down(g):
                pe.wait_ge(a_lo_done, 2 * g + 2)
                pe.wait_ge(wdl, 4 * g + 4)
                for n in range(PER):
                    i, d = divmod(n, KC)
                    k = g * PER + n
                    if k >= 2:
                        pe.wait_ge(acc_done, k - 1)
                    else:
                        pe.wait_ge(cst_done, 1)
                    cols = slice(i * THIRD, (i + 1) * THIRD)
                    for c in range(2):
                        for m, (w, a) in enumerate(((wd_hi, a_hi), (wd_hi, a_lo), (wd_lo, a_hi))):
                            ins = pe.matmul(PS[:, 6 + k % 2, 0:THIRD], w[:, c, d * P:(d + 1) * P], a[:, (2 * g + c) % 4, cols],
                                            start=(c == 0 and m == 0), stop=(c == 1 and m == 2))
                    ins.then_inc(down_done, 1)

            for g in range(NG):
                for q in range(4 * g, 4 * g + 4):
                    unit(q)
                if g:
                    down(g - 1)
            down(NG - 1)
            pe.wait_ge(g_evac, 3 * FC)
            for t in range(NS):
                n = rows(t)
                pe.wait_ge(acc_done, PER * (NG - 1) + KC * (third_of(t) + 1))
                if t >= 2:
                    pe.wait_ge(y_copy, t - 1)
                elif t == 1:
                    pe.wait_ge(mul_done, 3 * FC)
                for d in range(KC):
                    ins = pe.transpose(PS[0:n, 2 * (t % 2) + d // 4, d % 4 * P:(d % 4 + 1) * P], acc[:, d, t * P:t * P + n], ident[:, :])
                ins.then_inc(t_done, 1)
            pe.wait_ge(tail_done, FC)
            pe.wait_ge(mul_done, 3 * FC)
            for n in range(6):
                if n >= 2:
                    pe.wait_ge(tt_copy, n - 1)
                for f in range(4 * n, min(4 * n + 4, FC)):
                    ins = pe.transpose(PS[0:DB + 2, 4 + n % 2, f % 4 * P:(f % 4 + 1) * P], tails[:, f, :], ident[:, :])
                ins.then_inc(tt_done, 1)


_SHAPES = {
    "x_prompt": (SEQ, D), "x_sample": (DB, D),
    "cache_diff_k": (NPOOL * P, GRP), "cache_diff_v": (NPOOL * P, GRP), "cache_fox_k": (NPOOL * P, GRP),
    "cache_fox_v": (NPOOL * P, GRP), "cache_fox_logf": (NPOOL * P, MAPS), "state_ffn_conv": (DB, 2, FF),
    "page_table": (1, DB * PAGES), "attn_pre_g": (1, D), "w_in": (D, F_COL + MAPS), "b_f": (1, MAPS),
    "lam_q1": (1, HD), "lam_k1": (1, HD), "lam_q2": (1, HD), "lam_k2": (1, HD), "subln_g": (1, P),
    "w_o": (D, D), "attn_post_g": (1, D), "ffn_pre_g": (1, D), "w_gate": (D, FF), "w_up": (D, FF),
    "conv_w": (3, FF), "conv_b": (1, FF), "w_down": (FF, D), "ffn_post_g": (1, D),
}
_OUTS = [("y", (1, SEQ, D)), ("ys", (DB, 1, D)), ("o_dk", (1, 1, SEQ, 4, P)), ("o_dv", (1, 1, SEQ, 4, P)),
         ("o_fk", (1, 1, SEQ, 8, HD)), ("o_fv", (1, 1, SEQ, 8, HD)), ("o_flf", (1, 1, SEQ, 8)),
         ("o_conv", (1, 1, 2, FF)), ("o_sdk", (1, DB, 1, 4, P)), ("o_sdv", (1, DB, 1, 4, P)),
         ("o_sfk", (1, DB, 1, 8, HD)), ("o_sfv", (1, DB, 1, 8, HD)), ("o_sflf", (1, DB, 1, 8)),
         ("o_sconv", (1, DB, 2, FF))]
_FLAT = {"y": (SEQ, D), "ys": (DB, D), "o_dk": (SEQ, GRP), "o_dv": (SEQ, GRP), "o_fk": (SEQ, GRP),
         "o_fv": (SEQ, GRP), "o_flf": (SEQ, MAPS), "o_conv": (2, FF), "o_sdk": (DB, GRP), "o_sdv": (DB, GRP),
         "o_sfk": (DB, GRP), "o_sfv": (DB, GRP), "o_sflf": (DB, MAPS), "o_sconv": (DB, 2, FF)}
_ALIAS = {"x": "x_prompt", "xs": "x_sample", "c_dk": "cache_diff_k", "c_dv": "cache_diff_v",
          "c_fk": "cache_fox_k", "c_fv": "cache_fox_v", "c_lf": "cache_fox_logf"}


def build(nc, io):
    with ExitStack() as ctx:
        io["ctx"] = ctx
        place = Place(nc, 16544)
        io["PS"] = ctx.enter_context(nc.psum_tensor("PS", [P, 8, 512], F32))
        io["pt_sb"] = nc.alloc_sbuf_tensor_at("pt_sb", [1, DB * PAGES], I32, offset=place.base + R_PT)
        io["q_dram"] = nc.dram_tensor("q_dram", (SEQ, 2 * GRP), F32).ap()
        io["qs_dram"] = nc.dram_tensor("qs_dram", (DB, 2 * GRP), F32).ap()
        io["x2_dram"] = nc.dram_tensor("x2_dram", (TOK, D), F32).ap()
        io.update(D_PADS=6, D_M1=12, D_DIAG=15, D_SUB=18, D_PN=20, D_L=24, D_GATED=28)
        for phase in PHASES:
            phase(nc, io, place)


PHASES = [project, decode, attend, merge, ffn]


def kernel(**inputs):
    import concourse.bacc as _bacc
    from concourse.bass_utils import run_bass_kernel_spmd as _run

    nc = _bacc.Bacc("TRN2", target_bir_lowering=False, num_devices=1)
    arrays, io = {}, {}
    for name, shape in _SHAPES.items():
        a = np.ascontiguousarray(inputs[name]).reshape(shape)
        arrays[f"in_{name}"] = a
        io[name] = nc.dram_tensor(f"in_{name}", a.shape, mybir.dt.from_np(a.dtype), kind="ExternalInput").ap()
    consts = shape_constants()
    arrays["in_consts"] = consts
    io["consts"] = nc.dram_tensor("in_consts", consts.shape, F32, kind="ExternalInput").ap()
    for short, name in _ALIAS.items():
        io[short] = io[name]
    for name, _ in _OUTS:
        io[name] = nc.dram_tensor(f"out_{name}", _FLAT[name], F32, kind="ExternalOutput").ap()
    build(nc, io)
    r = _run(nc, [arrays], core_ids=[0])
    return tuple(np.asarray(r.results[0][f"out_{name}"]).reshape(shape) for name, shape in _OUTS)
```

```python
import math
from contextlib import ExitStack

import numpy as np
import concourse.bass as bass
from concourse import mybir

F32 = mybir.dt.float32
F32R = mybir.dt.float32r
BF16 = mybir.dt.bfloat16
I32 = mybir.dt.int32
ALU = mybir.AluOpType
ACT = mybir.ActivationFunctionType
AX = mybir.AxisListType.X

P = 128
D = 1024
KC = D // P
SEQ = 1024
NT = SEQ // P
DB = 8
TOK = SEQ + DB
THIRD = TOK // 3
PAGES = 8
PAST = PAGES * P
NPOOL = DB * PAGES * 5 // 4
MAPS = 8
HD = 64
GRP = MAPS * HD
FF = 2816
FC = FF // P
EPS = 1e-6
LAM_INIT = 0.8 - 0.6 * math.exp(0.0)
SCALE = HD ** -0.5
NEG = -1e37
THETA = 10000.0
LO_ROW = 32

QA, KA, QF, KF, VA, VF = range(6)
BLOCK_COL = {QA: 0, KA: 512, VA: 1024, QF: 1536, KF: 2048, VF: 2560}
ORDER = [QA, QF, KA, KF, VA, VF]
F_COL = 3072

C_ID, C_MASK, C_SUFFIX, C_ONES, C_HM, C_SELB, C_SIGN, C_ROPE, C_SELH = (
    0, 128, 256, 384, 512, 1024, 1032, 1040, 1040 + 9 * P)
C_END = C_SELH + MAPS * P


def shape_constants():
    c = np.zeros((P, C_END), np.float32)
    i = np.arange(P)
    c[:, C_ID:C_ID + P] = np.eye(P)
    c[:, C_MASK:C_MASK + P] = np.where(i[None, :] <= i[:, None], 0.0, NEG)
    c[:, C_SUFFIX:C_SUFFIX + P] = i[:, None] > i[None, :]
    c[:, C_ONES:C_ONES + P] = 1.0
    col = np.arange(GRP)
    m = i % MAPS
    diff = i < HD
    c[:, C_HM:C_HM + GRP] = np.where(diff[:, None], (col[None, :] // P) == (m[:, None] // 2),
                                     (col[None, :] // HD) == m[:, None])
    c[:, C_SIGN] = ~diff | (m % 2 == 0)
    c[:, C_SIGN + 1] = diff & (m % 2 == 1)
    c[:, C_SELB:C_SELB + DB] = (i[:, None] % HD // MAPS) == np.arange(DB)[None, :]
    half = HD // 2
    inv = np.float32(THETA) ** (-np.arange(half, dtype=np.float32) / np.float32(half))
    for t in range(NT + 1):
        pos = (t * P + i if t < NT else np.full(P, PAST)).astype(np.float32)
        ang = (pos[:, None] * inv[None, :]).astype(np.float32).astype(np.float64)
        at = C_ROPE + t * P
        c[:, at:at + half] = c[:, at + half:at + HD] = np.cos(ang)
        c[:, at + HD:at + HD + half] = -np.sin(ang)
        c[:, at + HD + half:at + 2 * HD] = np.sin(ang)
    for h in range(MAPS):
        c[h, C_SELH + h * P:C_SELH + (h + 1) * P] = 1.0
        c[LO_ROW + h, C_SELH + h * P:C_SELH + (h + 1) * P] = 1.0
    return c


class Place:

    def __init__(self, nc, base):
        self.nc, self.base, self.n, self.made = nc, base, 0, {}

    def at(self, off, name, cols, dt=F32):
        assert off + (2 if dt == BF16 else 4) * cols <= 212800, (name, off + 4 * cols)
        key = (off, name, cols, dt)
        if key not in self.made:
            self.made[key] = self._make(off, name, cols, dt)
        return self.made[key]

    def _make(self, off, name, cols, dt):
        self.n += 1
        return self.nc.alloc_sbuf_tensor_at(f"{name}_{self.n}", [P, cols], dt, offset=self.base + off)


def view(tensor, **dims):
    names = list(dims)
    return tensor[:, :].rearrange("p (%s) -> p %s" % (" ".join(names), " ".join(names)),
                             **{n: dims[n] for n in names[:-1]})


HT_BYTES = 4 * KC * TOK
R_HI, R_LO = 0, HT_BYTES
R_ID = 2 * HT_BYTES + 512
R_SMALL = R_ID + 512
R_F = R_SMALL + 256
R_PT = R_F + 864
R_OS = R_SMALL + 1408
R_FREE = R_OS + 4 * D
R_LF = R_OS + 1024
R_OT = 4 * (12 * SEQ + 4 * SEQ)
R_WO = R_FREE + 4 * NT * D
R_ZS = R_FREE + 4 * (4 * KC * GRP + 6 * GRP + 6 * GRP + (NT + 1) * P + KC * P)
R_SCORES = R_ZS + 4 * (6 * GRP + 8 * GRP)
R_ROPE = R_ZS - 4 * (KC * P + (NT + 1) * P)
R_TMP = R_ROPE - 8 * GRP


def project(nc, io, place):
    ht_hi = view(place.at(R_HI, "ht_hi", KC * TOK, F32R), k=KC, t=TOK)
    ht_lo = view(place.at(R_LO, "ht_lo", KC * TOK, F32R), k=KC, t=TOK)
    ht_hi_f = ht_hi.bitcast(F32)
    ident = place.at(R_ID, "ident", P)
    o = R_FREE
    w_hi = view(place.at(o, "w_hi", 2 * KC * GRP, F32R), s=2, k=KC, n=GRP); o += 8 * KC * GRP
    w_lo = view(place.at(o, "w_lo", 2 * KC * GRP, F32R), s=2, k=KC, n=GRP); o += 8 * KC * GRP
    RAW = 3
    raw = view(place.at(o, "w_raw", RAW * 2 * GRP), s=RAW, k=2, n=GRP); o += 4 * RAW * 2 * GRP
    zst = view(place.at(o, "z_stage", 2 * GRP), s=2, n=GRP); o += 8 * GRP
    zraw = view(place.at(o, "z_raw", 2 * GRP), s=2, n=GRP); o += 8 * GRP
    tmp = view(place.at(o, "rope_tmp", 2 * GRP), s=2, n=GRP); o += 8 * GRP
    rope = view(place.at(o, "rope", (NT + 1) * P), t=NT + 1, n=P); o += 4 * (NT + 1) * P
    hsp = view(place.at(o, "h_sample", KC * P, F32R), k=KC, m=P); o += 4 * KC * P
    assert o == R_ZS
    zs = view(place.at(o, "z_sample", 6 * GRP), g=6, n=GRP); o += 4 * 6 * GRP
    KP = 4
    kpage = view(place.at(o, "k_page", KP * 2 * GRP), s=KP, n=2 * GRP)
    x_sb = [place.at(at, f"x{n}", D) for n, at in enumerate((o, o + 4 * D, R_TMP - 16 * GRP, R_TMP - 8 * GRP))]
    XS = len(x_sb)
    xn = view(place.at(o + 8 * D, "xn", 2 * D), s=2, n=D)
    g_bc = place.at(o + 24 * D, "g_bc", D); o += 4 * KP * 2 * GRP
    assert o == R_SCORES
    scores = place.at(o, "scores", DB * PAGES * 16); o += 4 * DB * PAGES * 16
    qbc = view(place.at(o, "q_bc", 2 * 2 * GRP), s=2, n=2 * GRP); o += 16 * GRP
    small = place.at(R_SMALL, "small", 64)
    ssq, ms, rstd, expo, b_f = (small[:, 9 * n:9 * n + 9] for n in range(5))
    b_f = b_f[:, 0:MAPS]
    f_sb = place.at(R_F, "f_tmp", 3 * (NT + 1) * MAPS)
    junk = scores
    ptab = io["pt_sb"]

    w_v = io["w_in"].rearrange("(k p) n -> p k n", p=P)

    sem = lambda n: io["ctx"].enter_context(nc.semaphore("a_" + n))
    consts_in, ssq_done, ms_done, rstd_done = map(sem, ["consts_in", "ssq_done", "ms_done", "rstd_done"])
    x_in = [sem(f"x_in{s}") for s in range(XS)]
    xn_done, tr_done, hi_done, lo_done = map(sem, ["xn_done", "tr_done", "hi_done", "lo_done"])
    raw_in = [sem(f"raw_in{s}") for s in range(RAW)]
    w_hi_done, w_lo_done, proj_done, evac, rope_step = map(sem, ["w_hi_done", "w_lo_done", "proj_done", "evac", "rope_step"])
    z_done, z_copy = map(sem, ["z_done", "z_copy"])
    stored = [sem("stored0"), sem("stored1")]
    zs_stored, qs_stored = map(sem, ["zs_stored", "qs_stored"])
    qbc_in = [sem("qbc_in0"), sem("qbc_in1")]
    kp_in = [sem(f"kp_in{s}") for s in range(KP)]
    mult_done, red_done, zeroed = map(sem, ["mult_done", "red_done", "zeroed"])
    lf_in = sem("lf_in")
    io["loads_through"] = [(s, 32 * (DB * PAGES // KP)) for s in kp_in] + [(s, 16 * (24 // RAW)) for s in raw_in]
    io["loads_through"] = [(x_in[n], 16 * len(range(n, NT + 1, XS))) for n in range(XS)] + io["loads_through"]
    lf = view(place.at(R_LF, "lf_pages", DB * PAGES * MAPS), g=DB * PAGES, h=MAPS)
    f_prod, ft_done = map(sem, ["f_prod", "ft_done"])
    f_in, wf_done, f_done, f_step, f_stored = map(sem, ["f_in", "wf_done", "f_done", "f_step", "f_stored"])
    PS = io["PS"]
    wf_hi = w_hi[:, 1, 0, 0:KC * MAPS].rearrange("p (k n) -> p k n", n=MAPS)
    wf_lo = w_lo[:, 1, 0, 0:KC * MAPS].rearrange("p (k n) -> p k n", n=MAPS)
    ft = qbc[0:MAPS, :, :].rearrange("p s n -> p (s n)")[:, 0:TOK]
    wf_raw = tmp[:, 0, 0:KC * MAPS].rearrange("p (k n) -> p k n", n=MAPS)

    NS = NT + 1
    steps = [(i, t) for i in range(6) for t in range(NS)]
    is_rope = lambda i, t: ORDER[i] in (QA, KA)
    uses_zraw = lambda i, t: is_rope(i, t) or t == NT
    zr_count = [0]
    for i, t in steps:
        zr_count.append(zr_count[-1] + uses_zraw(i, t))
    out_of = {KA: io["o_dk"], VA: io["o_dv"], KF: io["o_fk"], VF: io["o_fv"]}
    outs_of = {KA: io["o_sdk"], VA: io["o_sdv"], KF: io["o_sfk"], VF: io["o_sfv"]}
    PG0 = 2
    pages_at = {}
    per = -(-DB * PAGES // ((6 - PG0) * NS))
    for n in range(DB * PAGES):
        pages_at.setdefault((PG0 + n // per // NS, n // per % NS), []).append(n)

    with nc.Block() as block:

        @block.sync
        def _(sp):
            def load_x(t):
                if t >= XS:
                    sp.wait_ge(xn_done, t - XS + 1)
                n = P if t < NT else DB
                src = io["x"][t * P:t * P + P, :] if t < NT else io["xs"]
                sp.dma_start(x_sb[t % XS][0:n, :], src).then_inc(x_in[t % XS], 16)
            load_x(0)
            sp.dma_start(g_bc[:, :], io["attn_pre_g"].to_broadcast([P, D])).then_inc(consts_in, 16)
            sp.dma_start(ident[:, :], io["consts"][:, C_ID:C_ID + P]).then_inc(consts_in, 16)
            load_x(1)
            load_x(2)
            load_x(3)
            sp.dma_start(wf_raw, w_v[:, :, F_COL:F_COL + MAPS]).then_inc(f_in, 16)
            sp.dma_start(b_f, io["b_f"].to_broadcast([P, MAPS])).then_inc(f_in, 16)
            sp.dma_start(ptab[0:1, :], io["page_table"]).then_inc(consts_in, 16)

            sp.dma_start(rope[:, :, :], io["consts"][:, C_ROPE:C_SELH].rearrange("p (t n) -> p t n", n=P)).then_inc(consts_in, 16)

            def load_w(q):
                i, pair = divmod(q, 4)
                if q >= RAW:
                    sp.wait_ge(w_lo_done, q - RAW + 1)
                c = BLOCK_COL[ORDER[i]]
                sp.dma_start(raw[:, q % RAW, :, :], w_v[:, 2 * pair:2 * pair + 2, c:c + GRP]).then_inc(raw_in[q % RAW], 16)

            for t in range(XS, NS):
                load_x(t)
                if t >= NS - RAW:
                    load_w(t - (NS - RAW))
            for q in range(RAW, 16):
                load_w(q)
            sp.wait_ge(z_done, zr_count[PG0 * NS])
            for n, g in enumerate((QA, QF)):
                sp.dma_start(io["qs_dram"][:, n * GRP:n * GRP + GRP], zs[0:DB, g, :]).then_inc(qs_stored, 16)
            sp.wait_ge(qs_stored, 32)
            def load_page(g):
                b, n = divmod(g, PAGES)
                if n == 0:
                    if b >= 2:
                        sp.wait_ge(mult_done, (b - 1) * PAGES)
                    sp.dma_start(qbc[:, b % 2, :], io["qs_dram"][b:b + 1, :].to_broadcast([P, 2 * GRP])).then_inc(qbc_in[b % 2], 16)
                if g >= KP:
                    sp.wait_ge(red_done, g - KP + 1)
                page = sp.value_load(ptab[0:1, g:g + 1], min_val=0, max_val=NPOOL - 1)
                for kind, cache in enumerate((io["c_dk"], io["c_fk"])):
                    sp.dma_start(kpage[:, g % KP, kind * GRP:(kind + 1) * GRP],
                                 cache[bass.ds(page * P, P), :]).then_inc(kp_in[g % KP], 16)

            sp.wait_ge(consts_in, 64)
            q = 16
            for i, t in steps[PG0 * NS:]:
                while q < 24 and ((q - RAW) // 4 - 1, (q - RAW) % 4) < (i, t):
                    load_w(q)
                    q += 1
                for g in pages_at.get((i, t), []):
                    load_page(g)
            sp.wait_ge(z_done, zr_count[3 * NS])
            decode_constants(io, place)[-1](sp)
            sp.wait_ge(proj_done, 5 * NS)
            sp.wait_ge(w_lo_done, 24)
            load_value_page = value_pages(io, place)[-1]
            for g in range(VP_EARLY):
                load_value_page(sp, g)
            sp.wait_ge(lf_in, 16 * DB * PAGES)
            sp.wait_ge(f_stored, 32)
            sp.wait_ge(zs_stored, 16 * 4)

        @block.gpsimd
        def _(pool):
            pool.memset(expo, -0.5).then_inc(zeroed, 1)
            pool.memset(hsp.bitcast(F32), 0.0).then_inc(zeroed, 1)
            pool.memset(f_sb[:, 208:216], 0.0).then_inc(zeroed, 1)
            pool.wait_ge(zeroed, 1)
            for t in range(NS):
                n = P if t < NT else DB
                pool.wait_ge(ssq_done, t + 1)
                pool.tensor_scalar(ms[0:n, t:t + 1], ssq[0:n, t:t + 1], 1.0 / D, EPS, ALU.mult, ALU.add).then_inc(ms_done, 1)
                pool.wait_ge(ms_done, t + 1)
                pool.tensor_tensor(rstd[0:n, t:t + 1], ms[0:n, t:t + 1], expo[0:n, t:t + 1], ALU.pow).then_inc(rstd_done, 1)
            pool.wait_ge(consts_in, 64)
            with pool.Fori(0, DB * PAGES) as g:
                page = pool.value_load(ptab[0:1, bass.ds(g, 1)], min_val=0, max_val=NPOOL - 1)
                pool.dma_start(lf[:, bass.ds(g, 1), :], io["c_lf"][bass.ds(page * P, P), :].rearrange("p (a h) -> p a h", a=1)).then_inc(lf_in, 16)
            for g in range(DB * PAGES):
                b = g // PAGES
                if g % PAGES == 0:
                    pool.wait_ge(qbc_in[b % 2], 16 * (b // 2 + 1))
                pool.wait_ge(kp_in[g % KP], 32 * (g // KP + 1))
                pool.tensor_tensor(kpage[:, g % KP, :], kpage[:, g % KP, :], qbc[:, b % 2, :], ALU.mult).then_inc(mult_done, 1)

        @block.scalar
        def _(act):
            def square(t):
                n = P if t < NT else DB
                act.wait_ge(x_in[t % XS], 16 * (t // XS + 1))
                if t:
                    act.wait_ge(ssq_done, t)
                act.activation(junk[0:n, :], x_sb[t % XS][0:n, :], ACT.Square, accum_out=ssq[0:n, t:t + 1]).then_inc(ssq_done, 1)

            def hi_part(t):
                n = P if t < NT else DB
                for half in range(2):
                    act.wait_ge(tr_done, 2 * t + half + 1)
                    src = PS[:, 4 + 2 * (t % 2) + half, 0:4 * n].rearrange("p (k n) -> p k n", n=n)
                    dst = (ht_hi[:, 4 * half:4 * half + 4, t * P:t * P + n] if t < NT else
                           hsp[:, 4 * half:4 * half + 4, 0:n])
                    if t == NT:
                        act.wait_ge(zeroed, 2)
                        act.activation(ht_hi[:, 4 * half:4 * half + 4, SEQ:], src, ACT.Copy).then_inc(hi_done, 1)
                    act.activation(dst, src, ACT.Copy).then_inc(hi_done, 1)

            def w_split(q):
                i, pair = divmod(q, 4)
                act.wait_ge(raw_in[q % RAW], 16 * (q // RAW + 1))
                if i >= 2:
                    act.wait_ge(proj_done, NS * (i - 1))
                if i == 1:
                    act.wait_ge(f_prod, 1)
                act.activation(w_hi[:, i % 2, 2 * pair:2 * pair + 2, :], raw[:, q % RAW, :, :], ACT.Copy).then_inc(w_hi_done, 1)

            square(0)
            square(1)
            act.wait_ge(f_in, 32)
            act.activation(wf_hi, wf_raw, ACT.Copy).then_inc(wf_done, 1)
            for t in range(2, NS):
                square(t)
                hi_part(t - 2)
                if 4 <= t < 4 + RAW:
                    w_split(t - 4)
            hi_part(NT - 1)
            hi_part(NT)
            w_split(3)
            act.wait_ge(f_prod, 1)
            act.activation(ft.rearrange("p (i n) -> p i n", n=THIRD), PS[0:MAPS, 4:7, 0:THIRD], ACT.Copy).then_inc(ft_done, 1)

            pending = None
            for j, (i, t) in enumerate(steps):
                blk = ORDER[i]
                act.wait_ge(proj_done, j + 1)
                bank = PS[:, j % 4, :]
                slot = (i * NT + t) % 2
                if uses_zraw(i, t) and zr_count[j - 1] and j >= 2:
                    act.wait_ge(z_done, zr_count[j - 1])
                if t == NT:
                    act.activation(zraw[0:DB, j % 2, :], bank[LO_ROW:LO_ROW + DB, :], ACT.Copy).then_inc(evac, 1)
                elif is_rope(i, t):
                    act.activation(zraw[:, j % 2, :], bank, ACT.Copy).then_inc(evac, 1)
                else:
                    act.wait_ge(stored[slot], 16 * ((i * NT + t) // 2))
                    act.activation(zst[:, slot, :], bank, ACT.Copy).then_inc(evac, 1)
                if pending is not None:
                    pending()
                    pending = None
                if t < NT:
                    def pending(i=i, t=t, j=j, slot=slot, blk=blk):
                        if is_rope(i, t):
                            act.wait_ge(z_done, zr_count[j + 1])
                        else:
                            act.wait_ge(evac, j + 1)
                        dst = (io["q_dram"][t * P:(t + 1) * P, (blk == QF) * GRP:(blk == QF) * GRP + GRP]
                               if blk in (QA, QF) else out_of[blk][t * P:(t + 1) * P, :])
                        act.dma_start(dst, zst[:, slot, :]).then_inc(stored[slot], 16)
                elif blk in outs_of:
                    def pending(i=i, blk=blk):
                        act.wait_ge(z_done, zr_count[(i + 1) * NS])
                        act.dma_start(outs_of[blk], zs[0:DB, blk, :]).then_inc(zs_stored, 16)
                if i < 5 and t < 4:
                    w_split(4 * (i + 1) + t)
                if (i, t) == (5, 1):
                    act.wait_ge(f_step, 3)
                    act.activation(f_sb[:, 72:144], f_sb[:, 72:144], ACT.Exp).then_inc(f_step, 1)
                    act.wait_ge(f_step, 4)
                    act.activation(f_sb[:, 144:216], f_sb[:, 72:144], ACT.Ln, bias=1.0).then_inc(f_step, 1)
                if (i, t) == (5, 3):
                    act.wait_ge(f_step, 6)
                    act.dma_start(io["o_flf"].rearrange("(t p) h -> p t h", p=P),
                                  f_sb[:, 0:64].rearrange("p (t h) -> p t h", h=MAPS)).then_inc(f_stored, 16)
                    act.dma_start(io["o_sflf"], f_sb[0:DB, 64:72]).then_inc(f_stored, 16)
            pending()
            for s in range(2):
                act.wait_ge(stored[s], 16 * 6 * NT // 2)

        @block.vector
        def _(dve):
            dve.wait_ge(consts_in, 64)
            def lo_part(t):
                n = P if t < NT else DB
                for half in range(2):
                    dve.wait_ge(hi_done, 2 * t + half + 1 if t < NT else 2 * (t + half + 1))
                    src = PS[:, 4 + 2 * (t % 2) + half, 0:4 * n].rearrange("p (k n) -> p k n", n=n)
                    sl = slice(4 * half, 4 * half + 4)
                    if t < NT:
                        hi, dst = ht_hi_f[:, sl, t * P:t * P + n], ht_lo[:, sl, t * P:t * P + n]
                    else:
                        hi, dst = hsp[:, sl, 0:n].bitcast(F32), hsp[:, sl, LO_ROW:LO_ROW + n]
                    if t == NT:
                        dve.tensor_tensor(ht_lo[:, sl, SEQ:], src, ht_hi_f[:, sl, SEQ:], ALU.subtract)
                    dve.tensor_tensor(dst, src, hi, ALU.subtract).then_inc(lo_done, 1)

            def norm(t):
                n = P if t < NT else DB
                dve.wait_ge(rstd_done, t + 1)
                if t >= 2:
                    dve.wait_ge(tr_done, 2 * t - 2)
                dve.scalar_tensor_tensor(xn[0:n, t % 2, :], x_sb[t % XS][0:n, :], rstd[0:n, t:t + 1], g_bc[0:n, :],
                                         ALU.mult, ALU.mult).then_inc(xn_done, 1)

            norm(0)
            norm(1)
            for t in range(2, NS):
                norm(t)
                lo_part(t - 2)
            lo_part(NT - 1)
            lo_part(NT)
            dve.wait_ge(wf_done, 1)
            dve.tensor_tensor(wf_lo, wf_raw, wf_hi.bitcast(F32), ALU.subtract).then_inc(wf_done, 1)

            def w_split(q):
                i, pair = divmod(q, 4)
                dve.wait_ge(w_hi_done, q + 1)
                sl = (slice(None), i % 2, slice(2 * pair, 2 * pair + 2), slice(None))
                dve.tensor_tensor(w_lo[sl], raw[:, q % RAW, :, :], w_hi[sl].bitcast(F32), ALU.subtract).then_inc(w_lo_done, 1)

            for q in range(4):
                w_split(q)

            rs = 0
            fs = 0
            for j, (i, t) in enumerate(steps):
                blk = ORDER[i]
                n = P if t < NT else DB
                if i < 5 and t < 4:
                    w_split(4 * (i + 1) + t)
                if uses_zraw(i, t):
                    dve.wait_ge(evac, j + 1)
                    if zr_count[j]:
                        dve.wait_ge(z_done, zr_count[j])
                    src = zraw[0:n, j % 2, :]
                    if t == NT:
                        ins = dve.tensor_tensor(zs[0:DB, blk, :], PS[0:DB, j % 4, :], src, ALU.add)
                        if is_rope(i, t):
                            ins.then_inc(rope_step, 1)
                            rs += 1
                            dve.wait_ge(rope_step, rs)
                            src = zs[0:DB, blk, :]
                        else:
                            ins.then_inc(z_done, 1)
                    if is_rope(i, t):
                        xv = src.rearrange("p (m h c) -> p m h c", m=MAPS, h=2)
                        cos = rope[0:n, t:t + 1, 0:HD].to_broadcast([n, MAPS, HD])
                        sin = rope[0:n, t:t + 1, HD:2 * HD].to_broadcast([n, MAPS, HD])
                        t1 = tmp[0:n, 0, :].rearrange("p (m c) -> p m c", c=HD)
                        t2 = tmp[0:n, 1, :].rearrange("p (m h c) -> p m h c", m=MAPS, h=2)
                        dve.tensor_tensor(t1, src.rearrange("p (m c) -> p m c", c=HD), cos, ALU.mult).then_inc(rope_step, 1)
                        dve.tensor_tensor(t2[:, :, 0, :], xv[:, :, 1, :], sin[:, :, 0:HD // 2], ALU.mult).then_inc(rope_step, 1)
                        dve.tensor_tensor(t2[:, :, 1, :], xv[:, :, 0, :], sin[:, :, HD // 2:HD], ALU.mult).then_inc(rope_step, 1)
                        rs += 3
                        dve.wait_ge(rope_step, rs)
                        if t < NT:
                            slot = (i * NT + t) % 2
                            if i * NT + t >= 2:
                                dve.wait_ge(stored[slot], 16 * ((i * NT + t) // 2))
                            dst = zst[:, slot, :]
                        else:
                            dst = src
                        last = dve.tensor_tensor(dst, tmp[0:n, 0, :], tmp[0:n, 1, :], ALU.add)
                        last.then_inc(z_done, 1)
                if (i, t) == (0, NT):
                    dve.wait_ge(f_done, 1)
                    dve.wait_ge(zeroed, 3)
                    dve.tensor_copy(f_sb[:, 144:208], PS[:, 7, 0:64])
                    dve.tensor_copy(f_sb[0:DB, 208:216], PS[0:DB, 7, 64:72]).then_inc(f_step, 1)
                    dve.wait_ge(f_step, 1)
                    dve.tensor_tensor(f_sb[:, 0:72].rearrange("p (t h) -> p t h", h=MAPS),
                                      f_sb[:, 144:216].rearrange("p (t h) -> p t h", h=MAPS),
                                      b_f.rearrange("p (a h) -> p a h", a=1).to_broadcast([P, NS, MAPS]),
                                      ALU.add).then_inc(f_step, 1)
                    dve.wait_ge(f_step, 2)
                    dve.scalar_tensor_tensor(f_sb[:, 72:144], f_sb[:, 0:72], -1.0, f_sb[:, 0:72], ALU.mult, ALU.min).then_inc(f_step, 1)
                if (i, t) == (5, 2):
                    dve.wait_ge(f_step, 5)
                    dve.scalar_tensor_tensor(f_sb[:, 0:72], f_sb[:, 0:72], 0.0, f_sb[:, 144:216], ALU.min, ALU.subtract).then_inc(f_step, 1)
                for g in pages_at.get(steps[j - 1] if j else None, []):
                    dve.wait_ge(mult_done, g + 1)
                    dve.tensor_reduce(scores[:, :].rearrange("p (k g m) -> p k g m", k=2, m=MAPS)[:, :, g, :], kpage[:, g % KP, :].rearrange("p (k m c) -> p k m c", k=2, c=HD),
                                      AX, ALU.add).then_inc(red_done, 1)

        @block.tensor
        def _(pe):
            pe.wait_ge(consts_in, 64)
            for t in range(NS):
                n = P if t < NT else DB
                pe.wait_ge(xn_done, t + 1)
                for half in range(2):
                    if t >= 2:
                        pe.wait_ge(lo_done, 2 * (t - 2) + half + 1)
                    for k in range(4):
                        c = (4 * half + k) * P
                        ins = pe.transpose(PS[:, 4 + 2 * (t % 2) + half, k * n:k * n + n], xn[0:n, t % 2, c:c + P], ident[0:n, 0:n])
                    ins.then_inc(tr_done, 1)
            pe.wait_ge(lo_done, 2 * NS)
            pe.wait_ge(wf_done, 2)
            for i in range(3):
                for k in range(KC):
                    for n, (w, a) in enumerate(((wf_hi, ht_hi), (wf_lo, ht_hi), (wf_hi, ht_lo))):
                        ins = pe.matmul(PS[0:MAPS, 4 + i, 0:THIRD], w[:, k, :], a[:, k, i * THIRD:(i + 1) * THIRD],
                                        start=(k == 0 and n == 0), stop=(k == KC - 1 and n == 2))
            ins.then_inc(f_prod, 1)
            for j, (i, t) in enumerate(steps):
                if t == 0:
                    pe.wait_ge(w_lo_done, 4 * (i + 1))
                if j >= 4:
                    pe.wait_ge(evac, j - 3)
                    if zr_count[j - 3]:
                        pe.wait_ge(z_done, zr_count[j - 3])
                parts = ([(ht_hi, w_hi), (ht_hi, w_lo), (ht_lo, w_hi)] if t < NT else [(hsp, w_hi), (hsp, w_lo)])
                for k in range(KC):
                    for n, (a, w) in enumerate(parts):
                        at = a[:, k, t * P:(t + 1) * P] if t < NT else a[:, k, :]
                        ins = pe.matmul(PS[:, j % 4, :], at, w[:, i % 2, k, :], start=(n == 0 and k == 0),
                                        stop=(n == len(parts) - 1 and k == KC - 1))
                ins.then_inc(proj_done, 1)
                if j == 1:
                    pe.wait_ge(ft_done, 1)
                    for u in range(NS):
                        n = P if u < NT else DB
                        ins = pe.transpose(PS[0:n, 7, u * MAPS:(u + 1) * MAPS], ft[:, u * P:u * P + n], ident[0:MAPS, 0:MAPS])
                    ins.then_inc(f_done, 1)


VP_PLACES = ([R_FREE + 8 * GRP * s for s in range(4)]
             + [R_FREE + 4 * (4 * KC * GRP) + 8 * GRP * s for s in range(3)]
             + [8 * GRP * s for s in range(4)] + [R_WO + 4 * (4 + s) * D for s in range(4)])
VP, VP_EARLY = len(VP_PLACES), 7


def value_pages(io, place):
    slots = [place.at(at, f"v_page{s}", 2 * GRP) for s, at in enumerate(VP_PLACES)]
    if "vp_in" not in io:
        io["vp_in"] = [(io["ctx"].enter_context(io["nc"].semaphore(f"d_vp_in{s}")), 0) for s in range(VP - len(io["loads_through"]))] + io["loads_through"]
    vp_in = io["vp_in"]

    def slot(g):
        return slots[g % VP][:, :]

    def load(sp, g):
        page = sp.value_load(io["pt_sb"][0:1, g:g + 1], min_val=0, max_val=NPOOL - 1)
        for kind, cache in enumerate((io["c_dv"], io["c_fv"])):
            sp.dma_start(slot(g)[:, kind * GRP:(kind + 1) * GRP], cache[bass.ds(page * P, P), :]).then_inc(vp_in[g % VP][0], 16)

    return slot, vp_in, load


def decode_constants(io, place):
    consts = place.at(R_ROPE, "consts", C_ROPE - C_SUFFIX)
    lamv = view(place.at(R_TMP, "lam_vectors", 6 * HD), v=6, n=HD)
    if "d_consts_in" not in io:
        io["d_consts_in"] = io["ctx"].enter_context(io["nc"].semaphore("d_consts_in"))

    def load(sp):
        sp.dma_start(consts[:, :], io["consts"][:, C_SUFFIX:C_ROPE]).then_inc(io["d_consts_in"], 16)
        for n, name in enumerate(("lam_q1", "lam_k1", "lam_q2", "lam_k2")):
            sp.dma_start(lamv[:, n, :], io[name].to_broadcast([P, HD])).then_inc(io["d_consts_in"], 16)

    return consts, lamv, io["d_consts_in"], load


def attention_inputs(io, place):
    o = R_WO
    qk = view(place.at(o, "qk_rows", 2 * 2 * NT * P), s=2, a=2, t=NT, n=P); o += 16 * NT * P
    o += 16 * NT * P
    vr = view(place.at(o, "v_raw", 2 * NT * P), s=2, t=NT, n=P); o += 8 * NT * P
    probs = view(place.at(o, "probs", 4 * SEQ), s=4, n=SEQ); o += 16 * SEQ
    asum = view(place.at(o, "a_sum", 2 * SEQ), s=2, n=SEQ); o += 8 * SEQ
    assert o <= R_ZS
    craw, selraw = asum[:, 0, 0:2 * P], probs[:, 3, :]
    if "b_load_in" not in io:
        io["b_load_in"] = [io["ctx"].enter_context(io["nc"].semaphore(f"b_{n}")) for n in ("load_in0", "load_in1", "consts_in")]
    *load_in, consts_in = io["b_load_in"]

    def load_constants(sp):
        sp.dma_start(craw, io["consts"][:, C_ID:C_ID + 2 * P]).then_inc(consts_in, 16)
        sp.dma_start(selraw, io["consts"][:, C_SELH:C_SELH + MAPS * P]).then_inc(consts_in, 16)

    def load_unit(sp, u, parts=(0, 1, 2)):
        q, c, kc = io["q_dram"], u * P, u % 4 * P
        k, v = (io["o_dk"], io["o_dv"]) if u < 4 else (io["o_fk"], io["o_fv"])
        k_q_v = ((qk[:, u % 2, 0, :, :], k, kc), (qk[:, u % 2, 1, :, :], q, c), (vr[:, u % 2, :, :], v, kc))
        for dst, src, at in [k_q_v[n] for n in parts]:
            sp.dma_start(dst, src[:, at:at + P].rearrange("(t p) c -> p t c", p=P)).then_inc(load_in[u % 2], 16)

    return qk, vr, probs, asum, craw, selraw, load_in, consts_in, load_constants, load_unit


def decode(nc, io, place):
    ident = place.at(R_ID, "ident", P)
    zs = view(place.at(R_ZS, "z_sample", 6 * GRP), g=6, n=GRP)
    scores = place.at(R_SCORES, "scores", 2 * DB * PAGES * MAPS)
    sc5 = scores[:, :].rearrange("p (k b n m) -> p k b n m", k=2, b=DB, m=MAPS)
    sck = scores[:, :].rearrange("p (k c) -> p k c", k=2)
    f_sb = place.at(R_F, "f_tmp", 3 * (NT + 1) * MAPS)
    lf = view(place.at(R_LF, "lf_pages", DB * PAGES * MAPS), b=DB, n=PAGES * MAPS)
    small = place.at(R_SMALL, "small", 64)
    vpage, vp_in, load_value_page = value_pages(io, place)
    o = 4 * 4 * 2 * GRP
    epad = view(place.at(o, "e_pad", 2 * DB * PAGES * HD), k=2, g=DB * PAGES, c=HD); o += 8 * DB * PAGES * HD
    consts, lamv, consts_in, _ = decode_constants(io, place)
    suffix, ones = consts[:, 0:P], consts[:, P:2 * P]
    hm = consts[:, C_HM - C_SUFFIX:C_HM - C_SUFFIX + GRP]
    selb = consts[:, C_SELB - C_SUFFIX:C_SELB - C_SUFFIX + DB]
    sgn = consts[:, C_SIGN - C_SUFFIX:C_SIGN - C_SUFFIX + 2]
    prod = place.at(o, "prod", 2 * GRP); o += 8 * GRP
    snew = place.at(o, "s_new", 2 * MAPS); o += 8 * MAPS
    npad = place.at(o, "new_pad", P); o += 4 * P
    lfpad = place.at(o, "lf_pad", DB * MAPS); o += 4 * DB * MAPS
    m1 = place.at(o, "m1", P); o += 4 * P
    diag = place.at(o, "diag", P); o += 4 * P
    negm = place.at(o, "neg_max", P); o += 4 * P
    cols = place.at(o, "cols", 16); o += 64
    gated = place.at(o, "gated", GRP); o += 4 * GRP
    osamp = place.at(R_OS, "o_sample", 2 * GRP)
    assert o <= R_ID
    PS = io["PS"]
    DOUT, FB, MT, MC, NM, LC, OD, OF = (PS[:, n, :] for n in (0, 1, 2, 3, 4, 5, 6, 7))
    mx, mxc, l_r, coef, lam = (cols[:, n:n + 1] for n in range(5))
    lsum = cols[:, 6:8]
    sem = lambda n: io["ctx"].enter_context(nc.semaphore("d_" + n))
    zeroed, v_step, fb_done, mt_done, nm_done, e_done, lc_done = map(
        sem, ["zeroed", "v_step", "fb_done", "mt_done", "nm_done", "e_done", "lc_done"])
    pads_ready, padded, sel_done, lam_step = map(sem, ["pads_ready", "padded", "sel_done", "lam_step"])
    v_used = sem("v_used")
    diag8 = ident[0:DB, 0:DB].rearrange("p (k b m) -> p k b m", k=1, m=1).to_broadcast([DB, 2, DB, MAPS])

    with nc.Block() as block:

        @block.sync
        def _(sp):
            for g in range(VP_EARLY, DB * PAGES):
                if g >= VP:
                    sp.wait_ge(v_used, g - VP + 1)
                load_value_page(sp, g)
            load_constants, load_unit = attention_inputs(io, place)[-2:]
            load_constants(sp)
            for u in range(2):
                load_unit(sp, u, (0, 1))
            sp.wait_ge(v_used, DB * PAGES)
            for u in range(2):
                load_unit(sp, u, (2,))

        @block.gpsimd
        def _(pool):
            pool.memset(epad[:, :, :, :], 0.0).then_inc(zeroed, 1)

        @block.scalar
        def _(act):
            act.wait_ge(lam_step, 3)
            act.activation(lsum, lsum, ACT.Exp).then_inc(lam_step, 1)
            act.wait_ge(v_step, io["D_SUB"])
            act.activation(scores[:, :], scores[:, :], ACT.Exp).then_inc(e_done, 1)
            act.wait_ge(v_step, io["D_PN"])
            act.activation(npad[0:DB, :], npad[0:DB, :], ACT.Exp).then_inc(e_done, 1)
            act.wait_ge(zeroed, 1)
            act.wait_ge(e_done, 2)
            for b in range(DB):
                act.activation(epad[:, 1, b * PAGES:(b + 1) * PAGES, b * MAPS:(b + 1) * MAPS], sc5[:, 1, b, :, :], ACT.Copy).then_inc(padded, 1)

        @block.vector
        def _(dve):
            count = [0]

            def step(ins):
                ins.then_inc(v_step, 1)
                count[0] += 1
                dve.wait_ge(v_step, count[0])

            dve.wait_ge(consts_in, 80)
            step(dve.tensor_tensor(lfpad[0:DB, :].rearrange("p (b m) -> p b m", b=DB),
                                   f_sb[0:DB, 64:72].rearrange("p (b m) -> p b m", b=1).to_broadcast([DB, DB, MAPS]),
                                   diag8[:, 0], ALU.mult))
            step(dve.tensor_tensor(prod[0:DB, 0:GRP], zs[0:DB, QA, :], zs[0:DB, KA, :], ALU.mult))
            step(dve.tensor_tensor(prod[0:DB, GRP:], zs[0:DB, QF, :], zs[0:DB, KF, :], ALU.mult))
            step(dve.tensor_reduce(snew[0:DB, :], prod[0:DB, :].rearrange("p (m c) -> p m c", c=HD), AX, ALU.add))
            step(dve.scalar_tensor_tensor(npad[0:DB, :].rearrange("p (k b m) -> p k b m", k=2, b=DB)[:, 0],
                                          snew[0:DB, 0:MAPS].rearrange("p (b m) -> p b m", b=1).to_broadcast([DB, DB, MAPS]), SCALE,
                                          diag8[:, 0], ALU.mult, ALU.mult))
            step(dve.scalar_tensor_tensor(npad[0:DB, :].rearrange("p (k b m) -> p k b m", k=2, b=DB)[:, 1],
                                          snew[0:DB, MAPS:].rearrange("p (b m) -> p b m", b=1).to_broadcast([DB, DB, MAPS]), SCALE,
                                          diag8[:, 1], ALU.mult, ALU.mult))
            assert count[0] == io["D_PADS"]
            for n in range(2):
                dve.tensor_tensor(lamv[:, 4 + n, :], lamv[:, 2 * n, :], lamv[:, 2 * n + 1, :], ALU.mult).then_inc(lam_step, 1)
            dve.wait_ge(lam_step, 2)
            dve.tensor_reduce(lsum, lamv[:, 4:6, :], AX, ALU.add).then_inc(lam_step, 1)
            dve.wait_ge(lam_step, 4)
            step(dve.tensor_scalar(lam, lsum[:, 0:1], lsum[:, 1:2], LAM_INIT, ALU.subtract, ALU.add))
            step(dve.tensor_scalar(small[:, 50:51], lam, -1.0, None, ALU.mult))
            step(dve.tensor_scalar(sck[:, 0, :], sck[:, 0, :], SCALE, None, ALU.mult))
            dve.wait_ge(fb_done, 1)
            step(dve.scalar_tensor_tensor(sck[:, 1, :], sck[:, 1, :], SCALE, FB, ALU.mult, ALU.add))
            step(dve.tensor_reduce(m1[:, :].rearrange("p (k b m) -> p k b m", k=2, b=DB)[:, 0], sc5[:, 0].rearrange("p b n m -> p b m n"), AX, ALU.max))
            step(dve.tensor_reduce(m1[:, :].rearrange("p (k b m) -> p k b m", k=2, b=DB)[:, 1], sc5[:, 1].rearrange("p b n m -> p b m n"), AX, ALU.max))
            assert count[0] == io["D_M1"]
            dve.wait_ge(mt_done, 2)
            step(dve.tensor_reduce(mx, MT[:, 0:P], AX, ALU.max))
            step(dve.tensor_tensor(mx, mx, MC[:, 0:1], ALU.max))
            step(dve.tensor_scalar(diag[:, :], ident[:, :], mx, -1.0, ALU.mult, ALU.mult))
            assert count[0] == io["D_DIAG"]
            dve.wait_ge(nm_done, 1)
            step(dve.tensor_copy(negm[:, :], NM[:, 0:P]))
            for k in range(2):
                nb = negm[:, :].rearrange("p (k b n m) -> p k b n m", k=2, b=DB, n=1)[:, k].to_broadcast([P, DB, PAGES, MAPS])
                step(dve.tensor_tensor(sc5[:, k], sc5[:, k], nb, ALU.add))
            assert count[0] == io["D_SUB"]
            step(dve.tensor_tensor(npad[0:DB, :], npad[0:DB, :], negm[0:DB, :], ALU.add))
            step(dve.tensor_scalar(npad[0:DB, :], npad[0:DB, :], 0.0, None, ALU.min))
            assert count[0] == io["D_PN"]
            dve.wait_ge(e_done, 2)
            step(dve.tensor_tensor(npad[0:DB, :].rearrange("p (k b m) -> p k b m", k=2, b=DB)[:, 0], npad[0:DB, :].rearrange("p (k b m) -> p k b m", k=2, b=DB)[:, 0], diag8[:, 0], ALU.mult))
            step(dve.tensor_tensor(npad[0:DB, :].rearrange("p (k b m) -> p k b m", k=2, b=DB)[:, 1], npad[0:DB, :].rearrange("p (k b m) -> p k b m", k=2, b=DB)[:, 1], diag8[:, 1], ALU.mult))
            for k in range(2):
                step(dve.tensor_reduce(m1[:, :].rearrange("p (k b m) -> p k b m", k=2, b=DB)[:, k], sc5[:, k].rearrange("p b n m -> p b m n"), AX, ALU.add))
            assert count[0] == io["D_L"]
            dve.wait_ge(zeroed, 1)
            for b in range(DB):
                dve.tensor_copy(epad[:, 0, b * PAGES:(b + 1) * PAGES, b * MAPS:(b + 1) * MAPS], sc5[:, 0, b, :, :]).then_inc(padded, 1)
            dve.wait_ge(lc_done, 1)
            step(dve.reciprocal(l_r, LC[:, 0:1]))
            step(dve.tensor_scalar(coef, sgn[:, 1:2], small[:, 50:51], sgn[:, 0:1], ALU.mult, ALU.add))
            step(dve.tensor_tensor(coef, coef, l_r, ALU.mult))
            dve.wait_ge(v_used, DB * PAGES)
            step(dve.scalar_tensor_tensor(gated[:, :], DOUT, coef, hm, ALU.mult, ALU.mult))
            assert count[0] == io["D_GATED"]
            dve.wait_ge(sel_done, 1)
            step(dve.tensor_copy(osamp[0:DB, 0:GRP], OD[0:DB, :]))
            step(dve.tensor_copy(osamp[0:DB, GRP:], OF[0:DB, :]))

        @block.tensor
        def _(pe):
            pe.wait_ge(consts_in, 80)
            pe.wait_ge(v_step, 1)
            fb3 = FB.rearrange("p (b n) -> p b n", b=DB)
            pe.matmul(fb3, suffix, lf[:, :, :], start=True, stop=False, skip_group_check=True)
            for d in range(1, PAGES):
                n = (PAGES - d) * MAPS
                pe.matmul(fb3[:, :, 0:n], ones, lf[:, :, d * MAPS:], start=False, stop=False, skip_group_check=True)
            pe.matmul(FB.rearrange("p (b n m) -> p b n m", b=DB, m=MAPS), ones[0:DB, :],
                      lfpad[0:DB, :].rearrange("p (b n m) -> p b n m", b=DB, n=1).to_broadcast([DB, DB, PAGES, MAPS]),
                      start=False, stop=True, skip_group_check=True).then_inc(fb_done, 1)
            pe.wait_ge(v_step, io["D_M1"])
            pe.transpose(MT[:, 0:P], m1[:, :], ident[:, :]).then_inc(mt_done, 1)
            pe.matmul(MC[:, 0:1], npad[0:DB, :], ones[0:DB, 0:1], start=True, stop=True).then_inc(mt_done, 1)
            pe.wait_ge(v_step, io["D_DIAG"])
            pe.matmul(NM[:, 0:P], ones, diag[:, :], start=True, stop=True).then_inc(nm_done, 1)
            pe.wait_ge(v_step, io["D_L"])
            pe.matmul(LC[:, 0:1], m1[:, :], ones[:, 0:1], start=True, stop=False)
            pe.matmul(LC[:, 0:1], npad[0:DB, :], ones[0:DB, 0:1], start=False, stop=True).then_inc(lc_done, 1)
            pe.wait_ge(padded, 2 * DB)
            for k, g in enumerate((VA, VF)):
                pe.matmul(DOUT[k * HD:(k + 1) * HD, :], npad[0:DB, k * HD:(k + 1) * HD], zs[0:DB, g, :], start=True, stop=False,
                          skip_group_check=True)
            for g in range(DB * PAGES):
                loaded, before = vp_in[g % VP]
                pe.wait_ge(loaded, before + 32 * (g // VP + 1))
                for k in range(2):
                    ins = pe.matmul(DOUT[k * HD:(k + 1) * HD, :], epad[:, k, g, :], vpage(g)[:, k * GRP:(k + 1) * GRP],
                                    start=False, stop=(g == DB * PAGES - 1), skip_group_check=True)
                ins.then_inc(v_used, 1)
            pe.wait_ge(v_step, io["D_GATED"])
            for k, dst in ((0, OD), (1, OF)):
                ins = pe.matmul(dst[0:DB, :], selb[k * HD:(k + 1) * HD, :], gated[k * HD:(k + 1) * HD, :], start=True, stop=True)
            ins.then_inc(sel_done, 1)


def output_weights(place):
    parts = (("wo_raw", R_WO, F32), ("wo_hi", R_WO + 4 * KC * D, F32R), ("wo_lo", R_WO, F32R))
    return [view(place.at(at, name, KC * D, dt), k=KC, n=D) for name, at, dt in parts]


def attend(nc, io, place):
    ident = place.at(R_ID, "ident", P)
    small = place.at(R_SMALL, "small", 64)
    neg_lam = small[:, 50:51]
    f_sb = place.at(R_F, "f_tmp", 3 * (NT + 1) * MAPS)
    o = 0
    ks = view(place.at(o, "k_split", 4 * SEQ, F32R), s=2, m=2, n=SEQ); o += 16 * SEQ
    qh = view(place.at(o, "q_hi", 4 * SEQ, F32R), s=2, m=2, n=SEQ); o += 16 * SEQ
    ql = view(place.at(o, "q_lo", 4 * SEQ, F32R), s=2, m=2, n=SEQ); o += 16 * SEQ
    vh = view(place.at(o, "v_hi", 2 * NT * P, F32R), s=2, t=NT, n=P); o += 8 * NT * P
    vl = view(place.at(o, "v_lo", 2 * NT * P, F32R), s=2, t=NT, n=P); o += 8 * NT * P
    assert o <= R_ID
    o = R_FREE
    o_all = view(place.at(o, "o_all", NT * D), t=NT, n=D); o += 4 * NT * D
    assert o == R_WO
    qk_rows, vr, probs, asum, craw, selraw, load_in, consts_in, _, load_unit = attention_inputs(io, place)
    o += 40 * NT * P + 24 * SEQ
    wo_raw = output_weights(place)[0]
    ath = view(place.at(o, "a_hi", 4 * SEQ, F32R), s=2, k=NT, q=2 * P); o += 16 * SEQ
    atl = view(place.at(o, "a_lo", 4 * SEQ, F32R), s=2, k=NT, q=2 * P); o += 16 * SEQ
    ot = view(place.at(R_OT, "o_transposed", 2 * P), q=2, n=P)
    cb = place.at(o, "gate_sums", SEQ, F32R); o += 4 * SEQ
    selh = view(place.at(o, "sel_head", MAPS * P, F32R), h=MAPS, n=P); o += 4 * MAPS * P
    cmask = place.at(o, "mask_bf", P, BF16); o += 2 * P
    cid = place.at(o, "ident_bf", P, BF16); o += 2 * P
    stat = view(place.at(o, "stat", 8 * 8), s=8, c=8); o += 256
    assert o <= 212800
    lft, csum, ones = probs[0:MAPS, 0, :], probs[0:MAPS, 1, :], probs[0:MAPS, 2, :]
    PS = io["PS"]
    sem = lambda n: io["ctx"].enter_context(nc.semaphore("b_" + n))
    consts_done, ones_done, lft_done, cb_step = map(sem, ["consts_done", "ones_done", "lft_done", "cb_step"])
    t_done, t_hi, t_lo, v_hi_done, v_ready = map(sem, ["t_done", "t_hi", "t_lo", "v_hi_done", "v_ready"])
    zero_done, pv_copy, ot_done = map(sem, ["zero_done", "pv_copy", "ot_done"])
    wo_in = sem("wo_in")
    NPREP = 4
    qk_done, max_step, max_done, exp_done, a_step, a_ready, pv_done, o_done = map(
        sem, ["qk_done", "max_step", "max_done", "exp_done", "a_step", "a_ready", "pv_done", "o_done"])

    UNITS = 8
    jobs = [(u, 2 * g + t, maps) for u in range(UNITS) for g in range(NT // 2)
            for maps in ([(0, 1)] if u < 4 else [(0,), (1,)]) for t in range(2)]
    NJ = len(jobs)
    first_job = [8 * u if u < 4 else 32 + 16 * (u - 4) for u in range(UNITS + 1)]
    maps_before = [0]
    for _, _, maps in jobs:
        maps_before.append(maps_before[-1] + len(maps))
    probs_slot = lambda J, k: 2 * (J % 2) + k if jobs[J][0] < 4 else J % 4
    blocks_of = lambda t: [(c, min(4, t + 1 - c)) for c in range(0, t + 1, 4)]

    def prep_at(J):
        u = jobs[J][0]
        n = J - first_job[u]
        every = (first_job[u + 1] - first_job[u]) // NPREP
        return None if u + 1 == UNITS or n % every else n // every
    t_end, p_end, nb = [0] * NJ, [NPREP] + [0] * (UNITS - 1), NPREP
    for J in range(NJ + 2):
        if J < NJ and prep_at(J) is not None:
            nb += 1
            p_end[jobs[J][0] + 1] = nb
        if J >= 2:
            nb += len(blocks_of(jobs[J - 2][1]))
            t_end[J - 2] = nb
    s_bank, s_free = [], []
    at, last_in = 0, [0] * 4
    for J, (_, t, maps) in enumerate(jobs):
        for _ in maps:
            w = t // 4 + 1
            s_bank.append(at)
            s_free.append(max(last_in[at:at + w]))
            last_in[at:at + w] = [len(s_bank)] * w
            at = (at + w) % 4

    def s_psum(M, n):
        return PS[:, s_bank[M]:s_bank[M] + -(-n // 512), :].rearrange("p b c -> p (b c)")[:, 0:n]

    with nc.Block() as block:

        @block.sync
        def _(sp):
            for u in range(2, UNITS):
                sp.wait_ge(t_done, p_end[u - 2])
                sp.wait_ge(v_ready, u - 1)
                load_unit(sp, u)
            for s in (1, 0):
                if s == 0:
                    sp.wait_ge(t_done, p_end[UNITS - 1])
                sp.dma_start(wo_raw[:, 4 * s:4 * s + 4, :], io["w_o"].rearrange("(k p) n -> p k n", p=P)[:, 4 * s:4 * s + 4, :]).then_inc(wo_in, 16)
            sp.wait_ge(wo_in, 32)

        @block.gpsimd
        def _(pool):
            pool.memset(cb[:, :].bitcast(F32), 0.0).then_inc(ones_done, 1)
            pool.memset(ones, 1.0).then_inc(ones_done, 1)
            for G in range(NJ // 2):
                u, t, _ = jobs[2 * G]
                if G >= 2:
                    pool.wait_ge(pv_done, G - 1)
                for x in (ath, atl):
                    pool.memset(x[:, G % 2, t + 1, 0:P].bitcast(F32), 0.0).then_inc(zero_done, 1)
                n = 2 * G - first_job[u]
                if G and n != (4 if u < 4 else 6):
                    continue
                u = u + 1 if G else 0
                if u == UNITS:
                    continue
                pool.wait_ge(v_hi_done, u + 1)
                pool.tensor_tensor(vl[:, u % 2, :, :], vr[:, u % 2, :, :], vh[:, u % 2, :, :].bitcast(F32), ALU.subtract).then_inc(v_ready, 1)

        @block.scalar
        def _(act):
            b = 0
            act.wait_ge(consts_in, 32)
            act.activation(cid[:, :], craw[:, 0:P], ACT.Copy).then_inc(consts_done, 1)
            act.activation(cmask[:, :], craw[:, P:2 * P], ACT.Copy).then_inc(consts_done, 1)
            act.activation(selh[:, :, :], selraw.rearrange("p (h n) -> p h n", n=P), ACT.Copy).then_inc(consts_done, 1)

            def prep_hi(n, u):
                nonlocal b
                act.wait_ge(t_done, b + 1)
                if n == 0 and u >= 2:
                    act.wait_ge(qk_done, maps_before[first_job[u - 1]])
                kind, half = divmod(n, 2)
                cols = slice(half * 512, (half + 1) * 512)
                for m in range(2):
                    src = PS[m * HD:(m + 1) * HD, 4 + b % 3, :]
                    if kind == 0:
                        ins = act.activation(ks[0:HD, u % 2, m, cols], src, ACT.Copy)
                    else:
                        act.activation(qh[0:HD, u % 2, m, cols], src, ACT.Copy)
                        ins = act.activation(qh[HD:, u % 2, m, cols], src, ACT.Copy)
                ins.then_inc(t_hi, 1)
                b += 1

            def v_hi(u):
                act.wait_ge(load_in[u % 2], 16 * 3 * (u // 2 + 1))
                if u >= 2:
                    act.wait_ge(pv_done, first_job[u - 1] // 2)
                act.activation(vh[:, u % 2, :, :], vr[:, u % 2, :, :], ACT.Copy).then_inc(v_hi_done, 1)

            def evac(G):
                w = P if jobs[2 * G][0] < 4 else HD
                act.wait_ge(pv_done, G + 1)
                if G:
                    act.wait_ge(ot_done, G)
                act.activation(ot[0:w, :, :].rearrange("p q n -> p (q n)"), PS[0:w, 7, 0:2 * P], ACT.Copy).then_inc(pv_copy, 1)

            for n in range(NPREP):
                prep_hi(n, 0)
            v_hi(0)
            for J in range(NJ + 3):
                if J < NJ and prep_at(J) is not None:
                    prep_hi(prep_at(J), jobs[J][0] + 1)
                if 2 <= J < NJ + 2:
                    G, half = divmod(J - 2, 2)
                    for c, nblk in blocks_of(jobs[J - 2][1]):
                        act.wait_ge(t_done, b + 1)
                        if G >= 2:
                            act.wait_ge(pv_done, G - 1)
                        act.activation(ath[:, G % 2, c:c + nblk, half * P:(half + 1) * P],
                                       PS[:, 4 + b % 3, 0:nblk * P].rearrange("p (k q) -> p k q", q=P), ACT.Copy).then_inc(t_hi, 1)
                        b += 1
                if J < NJ:
                    u, t, maps = jobs[J]
                    for m in maps:
                        M = maps_before[J] + (m if u < 4 else 0)
                        n = (t + 1) * P
                        act.wait_ge(max_done, M + 1)
                        if u < 4 and J >= 2:
                            act.wait_ge(a_ready, J - 1)
                        elif u >= 4:
                            act.wait_ge(a_ready, first_job[4])
                            if J >= first_job[4] + 4:
                                act.wait_ge(t_done, t_end[J - 4])
                        k = m if u < 4 else 0
                        act.activation(probs[:, probs_slot(J, k), 0:n], s_psum(M, n),
                                       ACT.Exp, bias=stat[:, J % 8, k:k + 1], scale=SCALE,
                                       accum_out=stat[:, J % 8, 2 + k:3 + k]).then_inc(exp_done, 1)
                    if J - first_job[u] == 4 and u + 1 < UNITS:
                        v_hi(u + 1)
                if J >= 4 and J % 2 == 0:
                    evac((J - 4) // 2)

        @block.vector
        def _(dve):
            b = 0
            steps = [0, 0, 0]

            def step(n, s, ins):
                ins.then_inc(s, 1)
                steps[n] += 1
                dve.wait_ge(s, steps[n])

            dve.wait_ge(lft_done, 1)
            step(0, cb_step, dve.tensor_copy(lft, PS[0:MAPS, 0:2, :].rearrange("p b c -> p (b c)")))
            dve.wait_ge(ones_done, 2)
            step(0, cb_step, dve.tensor_tensor_scan(csum, ones, lft, 0.0, ALU.mult, ALU.add))
            step(0, cb_step, dve.tensor_scalar(csum, csum, -1.0 / SCALE, None, ALU.mult))
            step(0, cb_step, dve.tensor_copy(cb[0:MAPS, :], csum))
            step(0, cb_step, dve.tensor_tensor(cb[LO_ROW:LO_ROW + MAPS, :], csum, cb[0:MAPS, :].bitcast(F32), ALU.subtract))

            def prep_lo(n, u):
                nonlocal b
                kind, half = divmod(n, 2)
                dve.wait_ge(t_hi, b + 1)
                cols = slice(half * 512, (half + 1) * 512)
                for m in range(2):
                    src = PS[m * HD:(m + 1) * HD, 4 + b % 3, :]
                    dst, high = ((ks[HD:, u % 2, m, cols], ks[0:HD, u % 2, m, cols]), (ql[0:HD, u % 2, m, cols], qh[0:HD, u % 2, m, cols]))[kind]
                    ins = dve.tensor_tensor(dst, src, high.bitcast(F32), ALU.subtract)
                ins.then_inc(t_lo, 1)
                b += 1

            for n in range(NPREP):
                prep_lo(n, 0)
            def rows_out(G):
                u, t, maps = jobs[2 * G]
                w = P if u < 4 else HD
                c = u * P + (0 if u < 4 else maps[0] * HD)
                dve.wait_ge(ot_done, G + 1)
                for half in range(2):
                    dve.tensor_scalar(o_all[:, t + half, c:c + w], PS[:, 7, (2 + half) * P:(2 + half) * P + w],
                                      stat[:, (2 * G + half) % 8, 4:5], None, ALU.mult).then_inc(o_done, 1)

            for J in range(NJ + 4):
                if J < NJ:
                    u, t, maps = jobs[J]
                    n = (t + 1) * P
                    for m in maps:
                        M = maps_before[J] + (m if u < 4 else 0)
                        k = m if u < 4 else 0
                        dve.wait_ge(qk_done, M + 1)
                        if J >= 4:
                            dve.wait_ge(exp_done, maps_before[J - 3])
                        step(2, max_step, dve.tensor_reduce(stat[:, J % 8, 6 + k:7 + k], s_psum(M, n), AX, ALU.max))
                        dve.tensor_scalar(stat[:, J % 8, k:k + 1], stat[:, J % 8, 6 + k:7 + k], -SCALE, None, ALU.mult).then_inc(max_done, 1)
                if J >= 5 and J % 2:
                    rows_out((J - 5) // 2)
                if 1 <= J <= NJ and jobs[J - 1][0] < 4:
                    st = stat[:, (J - 1) % 8, :]
                    n = (jobs[J - 1][1] + 1) * P
                    dve.wait_ge(exp_done, maps_before[J])
                    step(1, a_step, dve.reciprocal(st[:, 4:6], st[:, 2:4]))
                    step(1, a_step, dve.scalar_tensor_tensor(st[:, 6:7], st[:, 2:3], neg_lam, st[:, 5:6], ALU.mult, ALU.mult))
                    if J >= 3:
                        dve.wait_ge(t_done, t_end[J - 3])
                    p0 = 2 * ((J - 1) % 2)
                    dve.scalar_tensor_tensor(asum[:, (J - 1) % 2, 0:n], probs[:, p0 + 1, 0:n], st[:, 6:7], probs[:, p0, 0:n],
                                             ALU.mult, ALU.add).then_inc(a_ready, 1)
                if J < NJ:
                    n = prep_at(J)
                    if n is not None:
                        prep_lo(n, u + 1)
                if 2 <= J < NJ + 2:
                    for c, nblk in blocks_of(jobs[J - 2][1]):
                        dve.wait_ge(t_hi, b + 1)
                        G, half = divmod(J - 2, 2)
                        sl = (slice(None), G % 2, slice(c, c + nblk), slice(half * P, (half + 1) * P))
                        dve.tensor_tensor(atl[sl], PS[:, 4 + b % 3, 0:nblk * P].rearrange("p (k q) -> p k q", q=P), ath[sl].bitcast(F32),
                                          ALU.subtract).then_inc(t_lo, 1)
                        b += 1
                if 1 <= J <= NJ and jobs[J - 1][0] >= 4:
                    dve.wait_ge(exp_done, maps_before[J])
                    dve.reciprocal(stat[:, (J - 1) % 8, 4:5], stat[:, (J - 1) % 8, 2:3]).then_inc(a_ready, 1)

        @block.tensor
        def _(pe):
            b = 0
            for t in range(NT):
                ins = pe.transpose(PS[0:MAPS, t // 4, t % 4 * P:t % 4 * P + P], f_sb[:, t * MAPS:(t + 1) * MAPS], ident[:, :])
            ins.then_inc(lft_done, 1)
            pe.wait_ge(consts_done, 3)

            def bank():
                if b >= 3:
                    pe.wait_ge(t_lo, b - 2)
                return PS[:, 4 + b % 3, :]

            def prep(n, u):
                nonlocal b
                kind, half = divmod(n, 2)
                if n == 0:
                    pe.wait_ge(load_in[u % 2], 16 * 3 * (u // 2 + 1))
                dst = bank()
                for c in range(4):
                    ins = pe.transpose(dst[:, c * P:(c + 1) * P], qk_rows[:, u % 2, kind, 4 * half + c, :], ident[:, :])
                ins.then_inc(t_done, 1)
                b += 1

            def qk(J):
                u, t, maps = jobs[J]
                s = u % 2
                if J == first_job[u]:
                    pe.wait_ge(t_lo, p_end[u])
                for m in maps:
                    M = maps_before[J] + (m if u < 4 else 0)
                    if s_free[M]:
                        pe.wait_ge(exp_done, s_free[M])
                    elif M == 0:
                        pe.wait_ge(cb_step, 5)
                    rows = slice(t * P, (t + 1) * P)
                    for half in range(t // 4 + 1):
                        n = min(512, (t + 1) * P - half * 512)
                        w = max(n, 2 * P)
                        keys = slice(half * 512, half * 512 + w)
                        dst = PS[:, s_bank[M] + half, :]
                        pe.matmul(dst[:, 0:w], qh[:, s, m, rows], ks[:, s, m, keys], start=True, stop=False, skip_group_check=True)
                        if half == t // 4:
                            pe.matmul(dst[:, n - P:n], cid[:, :], cmask[:, :], start=False, stop=False, skip_group_check=True)
                        if u >= 4:
                            pe.matmul(dst[:, 0:w], selh[:, 2 * (u - 4) + m, :], cb[:, keys], start=False, stop=False, skip_group_check=True)
                        ins = pe.matmul(dst[:, 0:w], ql[0:HD, s, m, rows], ks[0:HD, s, m, keys], start=False, stop=True, skip_group_check=True)
                    ins.then_inc(qk_done, 1)

            def turn(J):
                nonlocal b
                u, t, maps = jobs[J]
                if u < 4:
                    pe.wait_ge(a_ready, J + 1)
                else:
                    pe.wait_ge(exp_done, maps_before[J + 1])
                src = asum[:, J % 2, :] if u < 4 else probs[:, probs_slot(J, 0), :]
                for c, nblk in blocks_of(t):
                    dst = bank()
                    for k in range(nblk):
                        ins = pe.transpose(dst[:, k * P:(k + 1) * P], src[:, (c + k) * P:(c + k + 1) * P], ident[:, :])
                    ins.then_inc(t_done, 1)
                    b += 1

            def pv(G):
                u, t, maps = jobs[2 * G]
                pe.wait_ge(t_lo, t_end[2 * G + 1])
                pe.wait_ge(zero_done, 2 * G + 2)
                if 2 * G == first_job[u]:
                    pe.wait_ge(v_ready, u + 1)
                if G:
                    pe.wait_ge(o_done, 2 * G)
                w = P if u < 4 else HD
                c = 0 if u < 4 else maps[0] * HD
                for k in range(t + 2):
                    for n, (v, x) in enumerate(((vh, ath), (vh, atl), (vl, ath))):
                        ins = pe.matmul(PS[0:w, 7, 0:2 * P], v[:, u % 2, k, c:c + w], x[:, G % 2, k, :],
                                        start=(k == 0 and n == 0), stop=(k == t + 1 and n == 2))
                ins.then_inc(pv_done, 1)

            def turn_back(G):
                w = P if jobs[2 * G][0] < 4 else HD
                pe.wait_ge(pv_copy, G + 1)
                for half in range(2):
                    ins = pe.transpose(PS[:, 7, (2 + half) * P:(2 + half) * P + w], ot[0:w, half, :], ident[0:w, 0:w])
                ins.then_inc(ot_done, 1)

            for n in range(NPREP):
                prep(n, 0)
            for J in range(NJ + 4):
                if J < NJ:
                    qk(J)
                    n = prep_at(J)
                    if n is not None:
                        prep(n, jobs[J][0] + 1)
                if 2 <= J < NJ + 2:
                    turn(J - 2)
                if J >= 5 and J % 2:
                    turn_back((J - 5) // 2)
                if J >= 4 and J % 2 == 0 and J - 4 < NJ:
                    pv((J - 4) // 2)


WR = 3


GATE_BANKS, UP_BANKS = (2, 3, 4), (0, 1, 5)


def ffn_product(pe, PS, bank, w_hi, w_lo, ht_hi, ht_lo, slot, i):
    for k in range(KC):
        for n, (w, a) in enumerate(((w_hi, ht_hi), (w_hi, ht_lo), (w_lo, ht_hi))):
            ins = pe.matmul(PS[:, bank, 0:THIRD], w[:, slot, k, :], a[:, k, i * THIRD:(i + 1) * THIRD],
                            start=(k == 0 and n == 0), stop=(k == KC - 1 and n == 2))
    return ins


def ffn_weights(io, place):
    o = R_FREE
    raw = view(place.at(o, "wgu_raw", 2 * KC * P), s=2, k=KC, n=P); o += 8 * KC * P
    w_hi = view(place.at(o, "wgu_hi", WR * KC * P, F32R), s=WR, k=KC, n=P); o += 4 * WR * KC * P
    w_lo = view(place.at(o, "wgu_lo", WR * KC * P, F32R), s=WR, k=KC, n=P); o += 4 * WR * KC * P
    assert o <= R_WO
    if "gu" not in io:
        io["gu"] = [io["ctx"].enter_context(io["nc"].semaphore("e_" + n)) for n in ("raw_in0", "raw_in1", "gu_hi", "gu_lo")]
    *raw_in, gu_hi, gu_lo = io["gu"]

    def load(sp, q):
        w = io[("w_gate", "w_up")[q % 2]].rearrange("(k p) n -> p k n", p=P)
        sp.dma_start(raw[:, q % 2, :, :], w[:, :, q // 2 * P:(q // 2 + 1) * P]).then_inc(raw_in[q % 2], 16)

    def split_hi(act, q):
        act.wait_ge(raw_in[q % 2], 16 * (q // 2 + 1))
        act.activation(w_hi[:, q % WR, :, :], raw[:, q % 2, :, :], ACT.Copy).then_inc(gu_hi, 1)

    def split_lo(pool, q):
        pool.wait_ge(gu_hi, q + 1)
        pool.tensor_tensor(w_lo[:, q % WR, :, :], raw[:, q % 2, :, :], w_hi[:, q % WR, :, :].bitcast(F32), ALU.subtract).then_inc(gu_lo, 1)

    return w_hi, w_lo, gu_lo, load, split_hi, split_lo


def merge(nc, io, place):
    ident = place.at(R_ID, "ident", P)
    ht_hi = view(place.at(R_HI, "ht_hi", KC * TOK, F32R), k=KC, t=TOK)
    ht_lo = view(place.at(R_LO, "ht_lo", KC * TOK, F32R), k=KC, t=TOK)
    osamp = place.at(R_OS, "o_sample", 2 * GRP)
    w_raw, w_hi, w_lo = output_weights(place)
    o = R_FREE
    o_all = view(place.at(o, "o_all", NT * D), t=NT, n=D); o += 4 * NT * D
    o += 8 * KC * D
    xr = view(place.at(o, "x_residual", 2 * D), s=2, n=D); o += 8 * D
    x2 = view(place.at(o, "x2", 2 * D), s=2, n=D); o += 8 * D
    h = place.at(o, "h", D); o += 4 * D
    junk = view(place.at(o, "squares", 2 * D), s=2, n=D); o += 8 * D
    g_post = place.at(o, "g_post", D); o += 4 * D
    g_pre = place.at(o, "g_pre", D); o += 4 * D
    g_sub = place.at(o, "g_sub", P); o += 4 * P
    st = view(place.at(o, "stat", 32 * 4), k=4, c=32); o += 512
    assert o <= 212800, o
    PS = io["PS"]
    sem = lambda n: io["ctx"].enter_context(nc.semaphore("c_" + n))
    sub_in, consts_in, consts_done, zeroed, w_hi_done, w_lo_done = map(sem, ["sub_in", "consts_in", "consts_done", "zeroed", "w_hi_done", "w_lo_done"])
    x_in = [sem("x_in0"), sem("x_in1")]
    x2_stored = [sem("x2_stored0"), sem("x2_stored1")]
    a_sq, a_rstd, a_norm, pool_step, t_done, t_hi, t_lo, b_done = map(
        sem, ["a_sq", "a_rstd", "a_norm", "pool_step", "t_done", "t_hi", "t_lo", "b_done"])
    y_sq, y_rstd, y_scaled, x2_done, x2_sq, x2_rstd, h_done = map(
        sem, ["y_sq", "y_rstd", "y_scaled", "x2_done", "x2_sq", "x2_rstd", "h_done"])
    NS = NT + 1
    rows = lambda t: P if t < NT else DB
    attn = lambda t: o_all[:, t, :] if t < NT else osamp[0:DB, :]
    y_of = lambda t: PS[0:rows(t), 2 * (t % 2):2 * (t % 2) + 2, :].rearrange("p b c -> p (b c)")
    a_batch, h_batch, nb = {}, {}, 0
    for t in range(-1, NS + 2):
        if t + 1 < NS:
            a_batch[t + 1] = nb
            nb += 2
        if t >= 2:
            h_batch[t - 2] = nb
            nb += 2
    w_ffn_hi, w_ffn_lo, gu_lo, load_ffn, split_ffn_hi, split_ffn_lo = ffn_weights(io, place)
    A, Y, X = 0, 16, 20

    with nc.Block() as block:

        @block.sync
        def _(sp):
            sp.dma_start(g_sub[:, :], io["subln_g"].to_broadcast([P, P])).then_inc(sub_in, 16)
            sp.dma_start(g_post[:, :], io["attn_post_g"].to_broadcast([P, D])).then_inc(consts_in, 16)
            sp.dma_start(g_pre[:, :], io["ffn_pre_g"].to_broadcast([P, D])).then_inc(consts_in, 16)
            for t in range(NS + 1):
                if t == NT:
                    sp.wait_ge(t_done, a_batch[NT - 1] + 2)
                    for q in range(2):
                        load_ffn(sp, q)
                if t < NS:
                    if t >= 2:
                        sp.wait_ge(x2_done, t - 1)
                    src = io["x"][t * P:(t + 1) * P, :] if t < NT else io["xs"]
                    sp.dma_start(xr[0:rows(t), t % 2, :], src).then_inc(x_in[t % 2], 16)
                if t >= 1:
                    u = t - 1
                    sp.wait_ge(x2_done, u + 1)
                    sp.dma_start(io["x2_dram"][u * P:u * P + rows(u), :], x2[0:rows(u), u % 2, :]).then_inc(x2_stored[u % 2], 16)
            for s in range(2):
                sp.wait_ge(x2_stored[s], 16 * ((NS + 1 - s) // 2))

        @block.gpsimd
        def _(pool):
            n_step = 0

            def rstd(t, cs, width, done):
                nonlocal n_step
                n = rows(t)
                pool.tensor_scalar(st[0:n, 1, cs], st[0:n, 0, cs], 1.0 / width, EPS, ALU.mult, ALU.add).then_inc(pool_step, 1)
                n_step += 1
                pool.wait_ge(pool_step, n_step)
                pool.tensor_tensor(st[0:n, 2, cs], st[0:n, 1, cs], st[0:n, 3, cs], ALU.pow).then_inc(done, 1)

            pool.memset(st[:, 3, :], -0.5).then_inc(zeroed, 1)
            pool.wait_ge(zeroed, 1)

            def a_stat(v):
                pool.wait_ge(a_sq, 4 * v + 4)
                rstd(v, slice(A + 4 * (v % 4), A + 4 * (v % 4) + 4), P, a_rstd)

            for v in range(3):
                a_stat(v)
            for u in range(NS):
                pool.wait_ge(y_sq, u + 1)
                rstd(u, slice(Y + u % 2, Y + u % 2 + 1), D, y_rstd)
                if u + 3 < NS:
                    a_stat(u + 3)
                pool.wait_ge(x2_sq, u + 1)
                rstd(u, slice(X + u % 2, X + u % 2 + 1), D, x2_rstd)
                if NT - 2 <= u < NT:
                    split_ffn_lo(pool, u - (NT - 2))

        @block.scalar
        def _(act):
            b = 0

            def hi(t):
                nonlocal b
                n = rows(t)
                for half in range(2):
                    act.wait_ge(t_done, b + 1)
                    src = PS[:, 4 + b % 4, 0:4 * n].rearrange("p (k n) -> p k n", n=n)
                    act.activation(ht_hi[:, 4 * half:4 * half + 4, t * P:t * P + n], src, ACT.Copy).then_inc(t_hi, 1)
                    b += 1

            def a_squares(v):
                n = rows(v)
                for k in range(4):
                    c = A + 4 * (v % 4) + k
                    if v >= 4 and k == 0:
                        act.wait_ge(a_norm, 4 * (v - 3))
                    if v or k:
                        act.wait_ge(a_sq, 4 * v + k)
                    act.activation(junk[0:n, 1, 0:P], attn(v)[:, k * P:(k + 1) * P], ACT.Square, accum_out=st[0:n, 0, c:c + 1]).then_inc(a_sq, 1)

            for v in range(2):
                a_squares(v)
            for k in range(KC):
                act.activation(w_hi[:, k, :], w_raw[:, k, :], ACT.Copy).then_inc(w_hi_done, 1)
                if k == 1:
                    hi(0)
            a_squares(2)
            for t in range(NS + 2):
                u = t - 1
                if 0 <= u < NS:
                    n = rows(u)
                    act.wait_ge(b_done, u + 1)
                    if u:
                        act.wait_ge(x2_sq, u)
                    if u >= 2:
                        act.wait_ge(y_scaled, u - 1)
                    act.activation(junk[0:n, 0, :], y_of(u), ACT.Square, accum_out=st[0:n, 0, Y + u % 2:Y + u % 2 + 1]).then_inc(y_sq, 1)
                if t + 1 < NS:
                    hi(t + 1)
                if t >= 2:
                    hi(t - 2)
                if 0 <= u < NS:
                    if u + 3 < NS:
                        a_squares(u + 3)
                    act.wait_ge(x2_done, u + 1)
                    act.wait_ge(y_sq, u + 1)
                    if u >= 2:
                        act.wait_ge(h_done, u - 1)
                    act.activation(junk[0:n, 0, :], x2[0:n, u % 2, :], ACT.Square, accum_out=st[0:n, 0, X + u % 2:X + u % 2 + 1]).then_inc(x2_sq, 1)
                    if NT - 2 <= u < NT:
                        split_ffn_hi(act, u - (NT - 2))

        @block.vector
        def _(dve):
            b = 0

            def lo(t):
                nonlocal b
                n = rows(t)
                for half in range(2):
                    dve.wait_ge(t_hi, b + 1)
                    src = PS[:, 4 + b % 4, 0:4 * n].rearrange("p (k n) -> p k n", n=n)
                    sl = (slice(None), slice(4 * half, 4 * half + 4), slice(t * P, t * P + n))
                    dve.tensor_tensor(ht_lo[sl], src, ht_hi[sl].bitcast(F32), ALU.subtract).then_inc(t_lo, 1)
                    b += 1

            def norm_attn(v):
                n = rows(v)
                dve.wait_ge(a_rstd, v + 1)
                for k in range(4):
                    c = A + 4 * (v % 4) + k
                    head = attn(v)[:, k * P:(k + 1) * P]
                    dve.scalar_tensor_tensor(head, head, st[0:n, 2, c:c + 1], g_sub[0:n, :], ALU.mult, ALU.mult).then_inc(a_norm, 1)

            dve.wait_ge(sub_in, 16)
            dve.tensor_scalar(g_sub[:, :], g_sub[:, :], 1.0 - LAM_INIT, None, ALU.mult).then_inc(consts_done, 1)
            dve.wait_ge(consts_done, 1)
            norm_attn(0)
            norm_attn(1)
            for k in range(KC):
                dve.wait_ge(w_hi_done, k + 1)
                dve.tensor_tensor(w_lo[:, k, :], w_raw[:, k, :], w_hi[:, k, :].bitcast(F32), ALU.subtract).then_inc(w_lo_done, 1)
                if k == 1:
                    lo(0)
            dve.wait_ge(consts_in, 32)
            for t in range(NS + 2):
                u = t - 1
                if t + 2 < NS:
                    norm_attn(t + 2)
                if t + 1 < NS:
                    lo(t + 1)
                if u == NS:
                    lo(NS - 1)
                elif u >= 0:
                    m = rows(u)
                    row = x2[0:m, u % 2, :]
                    dve.wait_ge(y_rstd, u + 1)
                    if u >= 2:
                        dve.wait_ge(x2_stored[u % 2], 16 * (u // 2))
                        dve.wait_ge(h_done, u - 1)
                    dve.scalar_tensor_tensor(row, y_of(u), st[0:m, 2, Y + u % 2:Y + u % 2 + 1], g_post[0:m, :], ALU.mult, ALU.mult).then_inc(y_scaled, 1)
                    dve.wait_ge(y_scaled, u + 1)
                    dve.wait_ge(x_in[u % 2], 16 * (u // 2 + 1))
                    dve.tensor_tensor(row, row, xr[0:m, u % 2, :], ALU.add).then_inc(x2_done, 1)
                    if u:
                        lo(u - 1)
                    dve.wait_ge(x2_done, u + 1)
                    dve.wait_ge(x2_rstd, u + 1)
                    if u:
                        dve.wait_ge(t_done, h_batch[u - 1] + 2)
                    dve.scalar_tensor_tensor(h[0:m, :], row, st[0:m, 2, X + u % 2:X + u % 2 + 1], g_pre[0:m, :], ALU.mult, ALU.mult).then_inc(h_done, 1)

        @block.tensor
        def _(pe):
            b = 0

            def turn(t, src):
                nonlocal b
                n = rows(t)
                for half in range(2):
                    if b >= 4:
                        pe.wait_ge(t_lo, b - 3)
                    for k in range(4):
                        c = (4 * half + k) * P
                        ins = pe.transpose(PS[:, 4 + b % 4, k * n:k * n + n], src[:, c:c + P], ident[0:n, 0:n])
                    ins.then_inc(t_done, 1)
                    b += 1

            def turn_h(t):
                pe.wait_ge(h_done, t + 1)
                turn(t, h[0:rows(t), :])

            for t in range(-1, NS + 2):
                if t + 1 < NS:
                    pe.wait_ge(a_norm, 4 * (t + 2))
                    turn(t + 1, attn(t + 1))
                if 0 <= t < NS:
                    pe.wait_ge(t_lo, a_batch[t] + 2)
                    if t >= 2:
                        pe.wait_ge(y_scaled, t - 1)
                    for half in range(2):
                        if half and t >= 2:
                            turn_h(t - 2)
                        for k in range(KC):
                            if t == 0 and half == 0:
                                pe.wait_ge(w_lo_done, k + 1)
                            for n, (a, w) in enumerate(((ht_hi, w_hi), (ht_hi, w_lo), (ht_lo, w_hi))):
                                ins = pe.matmul(PS[0:rows(t), 2 * (t % 2) + half, :], a[:, k, t * P:t * P + rows(t)],
                                                w[:, k, half * 512:half * 512 + 512],
                                                start=(n == 0 and k == 0), stop=(n == 2 and k == KC - 1))
                    ins.then_inc(b_done, 1)
                if t >= NS:
                    turn_h(t - 2)
                if t == NS:
                    pe.wait_ge(t_lo, h_batch[2 * THIRD // P] + 2)
                    pe.wait_ge(y_scaled, NS - 1)
                    pe.wait_ge(gu_lo, 1)
                    for i in range(2):
                        ffn_product(pe, PS, GATE_BANKS[i], w_ffn_hi, w_ffn_lo, ht_hi, ht_lo, 0, i)


def ffn(nc, io, place):
    ident = place.at(R_ID, "ident", P)
    ht_hi = view(place.at(R_HI, "ht_hi", KC * TOK, F32R), k=KC, t=TOK)
    ht_lo = view(place.at(R_LO, "ht_lo", KC * TOK, F32R), k=KC, t=TOK)
    w_hi, w_lo, gu_lo, load_weights, split_hi, split_lo = ffn_weights(io, place)
    o = R_WO
    acc = view(place.at(o, "acc", KC * TOK), d=KC, t=TOK)
    rows_in = place.at(o, "rows_in", FF); o += 4 * KC * TOK
    a_hi = view(place.at(o, "act_hi", 4 * TOK, F32R), s=4, t=TOK); o += 16 * TOK
    a_lo = view(place.at(o, "act_lo", 4 * TOK, F32R), s=4, t=TOK); o += 16 * TOK
    wd_hi = view(place.at(o, "wd_hi", 2 * D, F32R), s=2, n=D); o += 8 * D
    wd_lo = view(place.at(o, "wd_lo", 2 * D, F32R), s=2, n=D); o += 8 * D
    wd_raw = view(place.at(o, "wd_raw", 2 * 512), s=2, n=512); o += 4 * 2 * 512
    GW = TOK + 8
    gb = view(place.at(o, "gate", 2 * GW), s=2, t=GW); o += 8 * GW
    cbuf = view(place.at(o, "conv", 2 * TOK), s=2, t=TOK); o += 8 * TOK
    NR = 2 * DB + 4
    cst = view(place.at(o, "conv_consts", FC * NR), f=FC, r=NR); o += 4 * FC * NR
    tails = view(place.at(o, "gate_tails", FC * (DB + 2)), f=FC, r=DB + 2); o += 896
    stat = view(place.at(o, "stat", 4 * 16), k=4, c=16); o += 256
    assert o <= 212800, o
    state = cst[:, :, 0:2 * DB].rearrange("p f (b j) -> p f b j", j=2)
    taps = [cst[:, :, 2 * DB + j] for j in range(3)]
    bias = cst[:, :, 2 * DB + 3]
    e = 0
    sq = place.at(e, "y_squares", D); e += 4 * D
    OS = 4
    xr = view(place.at(e, "x2_rows", OS * D), s=OS, n=D); e += 4 * OS * D
    out = view(place.at(e, "out_rows", OS * D), s=OS, n=D); e += 4 * OS * D
    tail_rows = place.at(e, "tail_rows", FF); e += 4 * FF
    g_post = place.at(e, "ffn_post", D); e += 4 * D
    assert e <= R_ID
    PS = io["PS"]
    sem = lambda n: io["ctx"].enter_context(nc.semaphore("e_" + n))
    wd_in = [sem("wd_in0"), sem("wd_in1")]
    x2_in, stored = [[sem(f"{n}{s}") for s in range(OS)] for n in ("x2_in", "stored")]
    wd_last_hi = view(place.at(R_FREE + 8 * KC * P, "wd_last_hi", 2 * D, F32R), s=2, n=D)
    wd_last_lo = view(place.at(R_FREE + 8 * KC * P + 8 * D, "wd_last_lo", 2 * D, F32R), s=2, n=D)

    def wd_parts(g):
        return (wd_hi, wd_lo) if g < NG - 1 else (wd_last_hi, wd_last_lo)
    rows_ready, cst_t, cst_done, zeroed, wdh, wdl = map(sem, ["rows_ready", "cst_t", "cst_done", "zeroed", "wdh", "wdl"])
    gate_done, up_done, g_evac, c_init, conv_step, conv_done, gelu_done, mul_done, a_hi_done, a_lo_done, tail_done = map(
        sem, ["gate_done", "up_done", "g_evac", "c_init", "conv_step", "conv_done", "gelu_done", "mul_done", "a_hi_done", "a_lo_done", "tail_done"])
    down_done, acc_done, g_in, state_stored, tt_done, tt_copy, tails_stored = map(
        sem, ["down_done", "acc_done", "g_in", "state_stored", "tt_done", "tt_copy", "tails_stored"])
    t_done, y_sq, y_step, y_rstd, n_done, out_early, out_late = map(
        sem, ["t_done", "y_sq", "y_step", "y_rstd", "n_done", "out_early", "out_late"])
    NG = FC // 2
    NS = NT + 1
    PER = 3 * KC
    rows = lambda t: P if t < NT else DB
    third_of = lambda t: (t * P + rows(t) - 1) // THIRD
    y_of = lambda t: PS[0:rows(t), 2 * (t % OS):2 * (t % OS) + 2, :].rearrange("p b c -> p (b c)")
    EARLY = sum(third_of(t) < 2 for t in range(NS))
    FIRST = sum(third_of(t) < 1 for t in range(NS))

    def out_ready(engine, t):
        if t < EARLY:
            engine.wait_ge(out_early, t + 1)
        else:
            engine.wait_ge(out_late, t - EARLY + 1)

    def down_halves(f):
        return [] if f < 2 else [2 * (f - 2), 2 * (f - 2) + 1]

    with nc.Block() as block:

        @block.sync
        def _(sp):
            sp.dma_start(rows_in[0:2 * DB, :], io["state_ffn_conv"].rearrange("b j n -> (b j) n")).then_inc(rows_ready, 16)
            sp.dma_start(rows_in[2 * DB:2 * DB + 3, :], io["conv_w"]).then_inc(rows_ready, 16)
            sp.dma_start(rows_in[2 * DB + 3:NR, :], io["conv_b"]).then_inc(rows_ready, 16)
            sp.dma_start(io["o_sconv"][:, 0, :], io["state_ffn_conv"][:, 1, :]).then_inc(state_stored, 16)

            def load_unit(q):
                sp.wait_ge(gu_lo, q - 1)
                load_weights(sp, q)

            def load_down(q):
                if q >= 2:
                    sp.wait_ge(wdl, q - 1)
                sp.dma_start(wd_raw[:, q % 2, :], io["w_down"][q // 2 * P:(q // 2 + 1) * P, q % 2 * 512:q % 2 * 512 + 512]).then_inc(wd_in[q % 2], 16)

            for f in range(FC + 2):
                for q in (2 * f + 2, 2 * f + 3):
                    if q < 2 * FC:
                        load_unit(q)
                for q in down_halves(f):
                    load_down(q)
            sp.wait_ge(up_done, FC)
            sp.dma_start(g_post[:, :], io["ffn_post_g"].to_broadcast([P, D])).then_inc(g_in, 16)
            sp.wait_ge(tt_copy, 6)
            sp.dma_start(io["o_conv"], tail_rows[0:2, :]).then_inc(tails_stored, 16)
            sp.dma_start(io["o_sconv"][:, 1, :], tail_rows[2:2 + DB, :]).then_inc(tails_stored, 16)
            for t in range(NS + OS - 1):
                if t < NS:
                    if t >= OS:
                        out_ready(sp, t - OS)
                    sp.dma_start(xr[0:rows(t), t % OS, :], io["x2_dram"][t * P:t * P + rows(t), :]).then_inc(x2_in[t % OS], 16)
                if t >= OS - 1:
                    u = t - (OS - 1)
                    out_ready(sp, u)
                    dst = io["y"][u * P:(u + 1) * P, :] if u < NT else io["ys"]
                    sp.dma_start(dst, out[0:rows(u), u % OS, :]).then_inc(stored[u % OS], 16)
            sp.wait_ge(tails_stored, 32)
            sp.wait_ge(state_stored, 16)
            for s in range(OS):
                sp.wait_ge(stored[s], 16 * ((NS + OS - 1 - s) // OS))

        @block.gpsimd
        def _(pool):
            pool.memset(stat[:, 3, :], -0.5).then_inc(zeroed, 1)
            for s in range(2):
                pool.memset(gb[:, s, 0:2], 0.0).then_inc(zeroed, 1)

            for f in range(FC + 2):
                for q in (2 * f + 2, 2 * f + 3):
                    if q < 2 * FC:
                        split_lo(pool, q)
                for q in down_halves(f):
                    pool.wait_ge(wdh, q + 1)
                    sl = (slice(None), q // 2 % 2, slice(q % 2 * 512, q % 2 * 512 + 512))
                    high, low = wd_parts(q // 4)
                    pool.tensor_tensor(low[sl], wd_raw[:, q % 2, :], high[sl].bitcast(F32), ALU.subtract).then_inc(wdl, 1)
                if f < FC:
                    pool.wait_ge(g_evac, 3 * f + 3)
                    pool.tensor_copy(tails[:, f, :], gb[:, f % 2, SEQ:SEQ + DB + 2]).then_inc(tail_done, 1)
                    pool.wait_ge(a_hi_done, f + 1)
                    pool.tensor_tensor(a_lo[:, f % 4, :], cbuf[:, f % 2, :], a_hi[:, f % 4, :].bitcast(F32), ALU.subtract).then_inc(a_lo_done, 1)
            for t in range(NS):
                n = rows(t)
                pool.wait_ge(y_sq, t + 1)
                pool.tensor_scalar(stat[0:n, 1, t:t + 1], stat[0:n, 0, t:t + 1], 1.0 / D, EPS, ALU.mult, ALU.add).then_inc(y_step, 1)
                pool.wait_ge(y_step, t + 1)
                pool.tensor_tensor(stat[0:n, 2, t:t + 1], stat[0:n, 1, t:t + 1], stat[0:n, 3, t:t + 1], ALU.pow).then_inc(y_rstd, 1)
                if 1 <= t <= EARLY:
                    u = t - 1
                    pool.wait_ge(n_done, u + 1)
                    pool.wait_ge(x2_in[u % OS], 16 * (u // OS + 1))
                    pool.tensor_tensor(out[:, u % OS, :], out[:, u % OS, :], xr[:, u % OS, :], ALU.add).then_inc(out_early, 1)

        @block.scalar
        def _(act):
            def hi_unit(q):
                if q >= WR:
                    r = q - WR
                    act.wait_ge((gate_done, up_done)[r % 2], r // 2 + 1)
                split_hi(act, q)

            for f in range(FC + 2):
                if 2 * f + 2 < 2 * FC:
                    hi_unit(2 * f + 2)
                if f < FC:
                    act.wait_ge(gate_done, f + 1)
                    if f >= 2:
                        act.wait_ge(conv_done, 2 * f - 2)
                        act.wait_ge(tail_done, f - 1)
                    if f == 0:
                        act.wait_ge(zeroed, 3)
                    for i in range(3):
                        act.activation(gb[:, f % 2, 2 + i * THIRD:2 + (i + 1) * THIRD], PS[:, GATE_BANKS[i], 0:THIRD], ACT.Copy).then_inc(g_evac, 1)
                if 2 * f + 3 < 2 * FC:
                    hi_unit(2 * f + 3)
                for q in down_halves(f):
                    act.wait_ge(wd_in[q % 2], 16 * (q // 2 + 1))
                    if q // 4 == NG - 1:
                        act.wait_ge(up_done, FC)
                    elif q >= 4:
                        act.wait_ge(down_done, PER * (q // 4))
                    act.activation(wd_parts(q // 4)[0][:, q // 2 % 2, q % 2 * 512:q % 2 * 512 + 512], wd_raw[:, q % 2, :], ACT.Copy).then_inc(wdh, 1)
                if f >= FC:
                    continue
                act.wait_ge(g_evac, 3 * f + 3)
                act.wait_ge(cst_done, 1)
                if f >= 2:
                    act.wait_ge(a_lo_done, f - 1)
                act.activation(cbuf[:, f % 2, :], gb[:, f % 2, 2:2 + TOK], ACT.Identity, bias=bias[:, f:f + 1], scale=taps[2][:, f:f + 1]).then_inc(c_init, 1)
                act.wait_ge(conv_done, 2 * f + 2)
                act.activation(cbuf[:, f % 2, :], cbuf[:, f % 2, :], ACT.Gelu_apprx_tanh).then_inc(gelu_done, 1)
                act.wait_ge(mul_done, 3 * f + 3)
                if f >= 4:
                    act.wait_ge(down_done, PER * (f // 2 - 1))
                act.activation(a_hi[:, f % 4, :], cbuf[:, f % 2, :], ACT.Copy).then_inc(a_hi_done, 1)
            for n in range(6):
                w = min(4, FC - 4 * n) * P
                act.wait_ge(tt_done, n + 1)
                act.activation(tail_rows[0:DB + 2, 4 * n * P:4 * n * P + w], PS[0:DB + 2, 4 + n % 2, 0:w], ACT.Copy).then_inc(tt_copy, 1)
            for t in range(NS):
                n = rows(t)
                act.wait_ge(t_done, t + 1)
                if t:
                    act.wait_ge(y_sq, t)
                act.activation(sq[0:n, :], y_of(t), ACT.Square, accum_out=stat[0:n, 0, t:t + 1]).then_inc(y_sq, 1)

        @block.vector
        def _(dve):
            def norm(t):
                n = rows(t)
                dve.wait_ge(y_rstd, t + 1)
                if t >= OS:
                    dve.wait_ge(stored[t % OS], 16 * (t // OS))
                dve.scalar_tensor_tensor(out[0:n, t % OS, :], y_of(t), stat[0:n, 2, t:t + 1], g_post[0:n, :], ALU.mult, ALU.mult).then_inc(n_done, 1)
                if t >= EARLY:
                    dve.wait_ge(n_done, t + 1)
                    dve.wait_ge(x2_in[t % OS], 16 * (t // OS + 1))
                    dve.tensor_tensor(out[0:n, t % OS, :], out[0:n, t % OS, :], xr[0:n, t % OS, :], ALU.add).then_inc(out_late, 1)

            def sums(g):
                for n in range(PER):
                    if g == NG - 1 and n >= 2 * KC + 4 and (n - 2 * KC) % 3 == 1 and (n - 2 * KC) // 3 <= FIRST:
                        if n == 2 * KC + 4:
                            dve.wait_ge(g_in, 16)
                        norm((n - 2 * KC) // 3 - 1)
                    i, d = divmod(n, KC)
                    k = g * PER + n
                    dve.wait_ge(down_done, k + 1)
                    if g:
                        dve.wait_ge(acc_done, k - PER + 1)
                    dst, src = acc[:, d, i * THIRD:(i + 1) * THIRD], PS[:, 6 + k % 2, 0:THIRD]
                    if g == 0:
                        dve.tensor_copy(dst, src).then_inc(acc_done, 1)
                    else:
                        dve.tensor_tensor(dst, src, dst, ALU.add).then_inc(acc_done, 1)

            dve.wait_ge(cst_t, 1)
            dve.tensor_copy(cst[:, :, :], PS[:, 6, 0:FC * NR].rearrange("p (f r) -> p f r", r=NR)).then_inc(cst_done, 1)
            dve.wait_ge(cst_done, 1)
            for f in range(FC):
                c, g = cbuf[:, f % 2, :], gb[:, f % 2, :]
                dve.wait_ge(c_init, f + 1)
                for j, back in ((1, 1), (0, 2)):
                    s = conv_step if j else conv_done
                    dve.scalar_tensor_tensor(c[:, 0:SEQ], g[:, 2 - back:2 - back + SEQ], taps[j][:, f:f + 1], c[:, 0:SEQ],
                                             ALU.mult, ALU.add).then_inc(s, 1)
                    dve.scalar_tensor_tensor(c[:, SEQ:], state[:, f, :, j], taps[j][:, f:f + 1], c[:, SEQ:],
                                             ALU.mult, ALU.add).then_inc(s, 1)
                    if j:
                        dve.wait_ge(conv_step, 2 * f + 2)
                dve.wait_ge(gelu_done, f + 1)
                dve.wait_ge(up_done, f + 1)
                for i in range(3):
                    cols = slice(i * THIRD, (i + 1) * THIRD)
                    dve.tensor_tensor(c[:, cols], PS[:, UP_BANKS[i], 0:THIRD], c[:, cols], ALU.mult).then_inc(mul_done, 1)
                if f % 2 and f > 2:
                    sums(f // 2 - 1)
            sums(NG - 1)
            for t in range(FIRST, NS):
                norm(t)

        @block.tensor
        def _(pe):
            def unit(q):
                f, up = divmod(q, 2)
                s = q % WR
                pe.wait_ge(gu_lo, q + 1)
                for i in range(3):
                    if f:
                        pe.wait_ge((g_evac, mul_done)[up], 3 * (f - 1) + i + 1)
                    if q == 0 and i < 2:
                        continue
                    ins = ffn_product(pe, PS, (GATE_BANKS, UP_BANKS)[up][i], w_hi, w_lo, ht_hi, ht_lo, s, i)
                ins.then_inc((gate_done, up_done)[up], 1)

            def turn(t):
                pe.wait_ge(acc_done, PER * (NG - 1) + KC * (third_of(t) + 1))
                if t == 0:
                    pe.wait_ge(g_evac, 3 * FC)
                    pe.wait_ge(mul_done, 3 * FC)
                elif t == 2:
                    pe.wait_ge(tt_copy, 6)
                elif t == 3:
                    pe.wait_ge(acc_done, PER * NG)
                if t >= OS:
                    pe.wait_ge(n_done, t - OS + 1)
                for d in range(KC):
                    ins = pe.transpose(PS[0:rows(t), 2 * (t % OS) + d // 4, d % 4 * P:(d % 4 + 1) * P], acc[:, d, t * P:t * P + rows(t)], ident[:, :])
                ins.then_inc(t_done, 1)

            def down(g):
                pe.wait_ge(a_lo_done, 2 * g + 2)
                pe.wait_ge(wdl, 4 * g + 4)
                wd_high, wd_low = wd_parts(g)
                for n in range(PER):
                    if g == NG - 1 and n == 2 * KC:
                        for t in range(FIRST):
                            turn(t)
                    i, d = divmod(n, KC)
                    k = g * PER + n
                    if k >= 2:
                        pe.wait_ge(acc_done, k - 1)
                    else:
                        pe.wait_ge(cst_done, 1)
                    cols = slice(i * THIRD, (i + 1) * THIRD)
                    for c in range(2):
                        for m, (w, a) in enumerate(((wd_high, a_hi), (wd_high, a_lo), (wd_low, a_hi))):
                            ins = pe.matmul(PS[:, 6 + k % 2, 0:THIRD], w[:, c, d * P:(d + 1) * P], a[:, (2 * g + c) % 4, cols],
                                            start=(c == 0 and m == 0), stop=(c == 1 and m == 2))
                    ins.then_inc(down_done, 1)

            for g in range(NG):
                for q in range(4 * g, 4 * g + 4):
                    unit(q)
                    if q == 0:
                        pe.wait_ge(rows_ready, 48)
                        for f in range(FC):
                            ins = pe.transpose(PS[:, 6, f * NR:(f + 1) * NR], rows_in[0:NR, f * P:(f + 1) * P], ident[0:NR, 0:NR])
                        ins.then_inc(cst_t, 1)
                if g:
                    down(g - 1)
            pe.wait_ge(g_evac, 3 * FC)
            pe.wait_ge(mul_done, 3 * FC)
            pe.wait_ge(tail_done, FC)
            for n in range(6):
                if n >= 2:
                    pe.wait_ge(tt_copy, n - 1)
                for f in range(4 * n, min(4 * n + 4, FC)):
                    ins = pe.transpose(PS[0:DB + 2, 4 + n % 2, f % 4 * P:(f % 4 + 1) * P], tails[:, f, :], ident[:, :])
                ins.then_inc(tt_done, 1)
            down(NG - 1)
            for t in range(FIRST, NS):
                turn(t)


_SHAPES = {
    "x_prompt": (SEQ, D), "x_sample": (DB, D),
    "cache_diff_k": (NPOOL * P, GRP), "cache_diff_v": (NPOOL * P, GRP), "cache_fox_k": (NPOOL * P, GRP),
    "cache_fox_v": (NPOOL * P, GRP), "cache_fox_logf": (NPOOL * P, MAPS), "state_ffn_conv": (DB, 2, FF),
    "page_table": (1, DB * PAGES), "attn_pre_g": (1, D), "w_in": (D, F_COL + MAPS), "b_f": (1, MAPS),
    "lam_q1": (1, HD), "lam_k1": (1, HD), "lam_q2": (1, HD), "lam_k2": (1, HD), "subln_g": (1, P),
    "w_o": (D, D), "attn_post_g": (1, D), "ffn_pre_g": (1, D), "w_gate": (D, FF), "w_up": (D, FF),
    "conv_w": (3, FF), "conv_b": (1, FF), "w_down": (FF, D), "ffn_post_g": (1, D),
}
_OUTS = [("y", (1, SEQ, D)), ("ys", (DB, 1, D)), ("o_dk", (1, 1, SEQ, 4, P)), ("o_dv", (1, 1, SEQ, 4, P)),
         ("o_fk", (1, 1, SEQ, 8, HD)), ("o_fv", (1, 1, SEQ, 8, HD)), ("o_flf", (1, 1, SEQ, 8)),
         ("o_conv", (1, 1, 2, FF)), ("o_sdk", (1, DB, 1, 4, P)), ("o_sdv", (1, DB, 1, 4, P)),
         ("o_sfk", (1, DB, 1, 8, HD)), ("o_sfv", (1, DB, 1, 8, HD)), ("o_sflf", (1, DB, 1, 8)),
         ("o_sconv", (1, DB, 2, FF))]
_FLAT = {"y": (SEQ, D), "ys": (DB, D), "o_dk": (SEQ, GRP), "o_dv": (SEQ, GRP), "o_fk": (SEQ, GRP),
         "o_fv": (SEQ, GRP), "o_flf": (SEQ, MAPS), "o_conv": (2, FF), "o_sdk": (DB, GRP), "o_sdv": (DB, GRP),
         "o_sfk": (DB, GRP), "o_sfv": (DB, GRP), "o_sflf": (DB, MAPS), "o_sconv": (DB, 2, FF)}
_ALIAS = {"x": "x_prompt", "xs": "x_sample", "c_dk": "cache_diff_k", "c_dv": "cache_diff_v",
          "c_fk": "cache_fox_k", "c_fv": "cache_fox_v", "c_lf": "cache_fox_logf"}


def build(nc, io):
    with ExitStack() as ctx:
        io["ctx"], io["nc"] = ctx, nc
        place = Place(nc, 16544)
        io["PS"] = ctx.enter_context(nc.psum_tensor("PS", [P, 8, 512], F32))
        io["pt_sb"] = nc.alloc_sbuf_tensor_at("pt_sb", [1, DB * PAGES], I32, offset=place.base + R_PT)
        io["q_dram"] = nc.dram_tensor("q_dram", (SEQ, 2 * GRP), F32).ap()
        io["qs_dram"] = nc.dram_tensor("qs_dram", (DB, 2 * GRP), F32).ap()
        io["x2_dram"] = nc.dram_tensor("x2_dram", (TOK, D), F32).ap()
        io.update(D_PADS=6, D_M1=12, D_DIAG=15, D_SUB=18, D_PN=20, D_L=24, D_GATED=28)
        for phase in PHASES:
            phase(nc, io, place)


PHASES = [project, decode, attend, merge, ffn]


def kernel(**inputs):
    import concourse.bacc as _bacc
    from concourse.bass_utils import run_bass_kernel_spmd as _run

    nc = _bacc.Bacc("TRN2", target_bir_lowering=False, num_devices=1)
    arrays, io = {}, {}
    for name, shape in _SHAPES.items():
        a = np.ascontiguousarray(inputs[name]).reshape(shape)
        arrays[f"in_{name}"] = a
        io[name] = nc.dram_tensor(f"in_{name}", a.shape, mybir.dt.from_np(a.dtype), kind="ExternalInput").ap()
    consts = shape_constants()
    arrays["in_consts"] = consts
    io["consts"] = nc.dram_tensor("in_consts", consts.shape, F32, kind="ExternalInput").ap()
    for short, name in _ALIAS.items():
        io[short] = io[name]
    for name, _ in _OUTS:
        io[name] = nc.dram_tensor(f"out_{name}", _FLAT[name], F32, kind="ExternalOutput").ap()
    build(nc, io)
    r = _run(nc, [arrays], core_ids=[0])
    return tuple(np.asarray(r.results[0][f"out_{name}"]).reshape(shape) for name, shape in _OUTS)
```
